# Optimizing a Trainium2 kernel written in Bass

```python
import math
import jax, jax.numpy as jnp
from jax import lax
import numpy as np

D_MODEL = 1024
BATCH = 1
SEQ = 512
DEPTH = 1

MLA_HEADS = 4
MLA_Q_RANK = 256
MLA_KV_RANK = 128
MLA_NOPE = 128
MLA_ROPE = 64
MLA_VDIM = 128
ROPE_THETA = 10000.0
Q_BLOCK = 128
GDN_HEADS = 4
GDN_DK = 128
GDN_DV = 128
CONV_K = 5
CHUNK = 64
MLA_WIDTH = MLA_HEADS * MLA_VDIM
GDN_WIDTH = GDN_HEADS * GDN_DV
MIX_WIDTH = MLA_WIDTH + GDN_WIDTH
MLA_IN = MLA_Q_RANK + MLA_KV_RANK + MLA_ROPE
GDN_QKV = GDN_HEADS * (2 * GDN_DK + GDN_DV)
GDN_IN = GDN_QKV + GDN_WIDTH + 4 * GDN_HEADS
IN_WIDTH = MLA_IN + GDN_IN
PEER_HEADS = 8
PEER_NKEYS = 128
PEER_EXPERTS = PEER_NKEYS * PEER_NKEYS
PEER_TOPK = 16
PEER_QDIM = 256
PEER_HALF = PEER_QDIM // 2
TOKEN_BLOCK = 128
EPS = 1e-6

kernel_name = "hybrid_mla_gdn_peer_encoder"

F32 = jnp.float32

def rmsnorm(t, w):
    tf = t.astype(F32)
    y = tf * lax.rsqrt(jnp.mean(tf * tf, axis=-1, keepdims=True) + EPS)
    return (y * w.astype(F32)).astype(t.dtype)

def l2norm(t):
    tf = t.astype(F32)
    return (tf * lax.rsqrt(jnp.sum(tf * tf, axis=-1, keepdims=True) + EPS)).astype(t.dtype)

def rope_tables(positions):
    inv = ROPE_THETA ** (-jnp.arange(0, MLA_ROPE, 2, dtype=F32) / MLA_ROPE)
    ang = positions.astype(F32)[..., None] * inv
    return jnp.cos(ang)[:, :, None, :], jnp.sin(ang)[:, :, None, :]

def apply_rope(t, cos, sin):
    half = t.shape[-1] // 2
    t1, t2 = t[..., :half], t[..., half:]
    return jnp.concatenate([t1 * cos - t2 * sin, t2 * cos + t1 * sin], axis=-1).astype(t.dtype)

def block_dense_attention(q, k, v):
    B, S, H, D = q.shape
    scale = D ** -0.5
    kf = k.astype(F32)
    vf = v.astype(F32)
    qb = jnp.moveaxis(q.reshape(B, S // Q_BLOCK, Q_BLOCK, H, D), 1, 0)

    def attend(q_blk):
        s = jnp.einsum('bqhd,bkhd->bhqk', q_blk.astype(F32), kf) * scale
        p = jax.nn.softmax(s, axis=-1)
        return jnp.einsum('bhqk,bkhd->bqhd', p, vf)

    o = lax.map(attend, qb)
    return jnp.moveaxis(o, 0, 1).reshape(B, S, H, v.shape[-1]).astype(q.dtype)

def mla_group(mla_in, cos, sin, q_a_norm_w, w_q_up, kv_a_norm_w, w_kv_up):
    B, S, _ = mla_in.shape
    c_q = rmsnorm(mla_in[..., :MLA_Q_RANK], q_a_norm_w)
    c_kv = rmsnorm(mla_in[..., MLA_Q_RANK:MLA_Q_RANK + MLA_KV_RANK], kv_a_norm_w)
    k_pe = mla_in[..., MLA_Q_RANK + MLA_KV_RANK:]
    q = (c_q @ w_q_up).reshape(B, S, MLA_HEADS, MLA_NOPE + MLA_ROPE)
    q = jnp.concatenate([q[..., :MLA_NOPE], apply_rope(q[..., MLA_NOPE:], cos, sin)], axis=-1)
    kv = (c_kv @ w_kv_up).reshape(B, S, MLA_HEADS, MLA_NOPE + MLA_VDIM)
    k_pe = apply_rope(k_pe[:, :, None, :], cos, sin)
    k = jnp.concatenate([kv[..., :MLA_NOPE], jnp.broadcast_to(k_pe, (B, S, MLA_HEADS, MLA_ROPE))], axis=-1)
    v = kv[..., MLA_NOPE:]
    o = block_dense_attention(q, k, v)
    return o.reshape(B, S, MLA_WIDTH)

def centred_depthwise_conv(t, w):
    C = t.shape[-1]
    pad = CONV_K // 2
    return lax.conv_general_dilated(
        t, w.astype(t.dtype)[:, None, :], window_strides=(1,), padding=[(pad, pad)],
        dimension_numbers=('NWC', 'WIO', 'NWC'), feature_group_count=C)

def gated_delta_chunked(q, k, v, g, beta):
    dtype = v.dtype
    q, k, v, g, beta = (t.astype(F32) for t in (q, k, v, g, beta))
    B, H, S, DK = k.shape
    DV = v.shape[-1]
    NC = S // CHUNK
    q = q * (DK ** -0.5)

    def chunks(t):
        return t.reshape(B, H, NC, CHUNK, *t.shape[3:])

    q, k, v, g, beta = (chunks(t) for t in (q, k, v, g, beta))
    g = jnp.cumsum(g, axis=-1)
    idx = jnp.arange(CHUNK)
    incl = idx[:, None] >= idx[None, :]
    strict = idx[:, None] > idx[None, :]
    diff = g[..., :, None] - g[..., None, :]
    decay = jnp.where(incl, jnp.exp(jnp.where(incl, diff, 0.0)), 0.0)
    k_beta = k * beta[..., None]
    v_beta = v * beta[..., None]
    lower = jnp.where(strict, jnp.einsum('bhnid,bhnjd->bhnij', k_beta, k) * decay, 0.0)
    a_mat = lower + jnp.eye(CHUNK, dtype=F32)
    rhs = jnp.concatenate([v_beta, k_beta * jnp.exp(g)[..., None]], axis=-1)
    sol = lax.linalg.triangular_solve(a_mat, rhs, left_side=True, lower=True, unit_diagonal=True)
    u, w = sol[..., :DV], sol[..., DV:]
    attn = jnp.where(incl, jnp.einsum('bhnid,bhnjd->bhnij', q, k) * decay, 0.0)
    g_last = g[..., -1]
    q_dec = q * jnp.exp(g)[..., None]
    k_dec = k * jnp.exp(g_last[..., None] - g)[..., None]
    xs = tuple(jnp.moveaxis(t, 2, 0) for t in (q_dec, k_dec, u, w, attn, g_last))

    def step(state, inp):
        qd, kd, uc, wc, ac, gl = inp
        v_new = uc - jnp.einsum('bhck,bhkv->bhcv', wc, state)
        o = jnp.einsum('bhck,bhkv->bhcv', qd, state) + jnp.einsum('bhij,bhjv->bhiv', ac, v_new)
        state = state * jnp.exp(gl)[..., None, None] + jnp.einsum('bhck,bhcv->bhkv', kd, v_new)
        return state, o

    state0 = jnp.zeros((B, H, DK, DV), F32)
    _, o = lax.scan(step, state0, xs)
    o = jnp.moveaxis(o, 0, 2).reshape(B, H, S, DV)
    return o.astype(dtype)

def gdn_group(gdn_in, conv_w, a_log_f, dt_bias_f, a_log_b, dt_bias_b, norm_w):
    B, S, _ = gdn_in.shape
    qkv = gdn_in[..., :GDN_QKV]
    z = gdn_in[..., GDN_QKV:GDN_QKV + GDN_WIDTH].reshape(B, S, GDN_HEADS, GDN_DV)
    gates = gdn_in[..., GDN_QKV + GDN_WIDTH:].reshape(B, S, 4, GDN_HEADS)
    a_f, b_f, a_b, b_b = gates[:, :, 0], gates[:, :, 1], gates[:, :, 2], gates[:, :, 3]
    qkv = jax.nn.silu(centred_depthwise_conv(qkv, conv_w))
    nq = GDN_HEADS * GDN_DK
    q = l2norm(qkv[..., :nq].reshape(B, S, GDN_HEADS, GDN_DK))
    k = l2norm(qkv[..., nq:2 * nq].reshape(B, S, GDN_HEADS, GDN_DK))
    v = qkv[..., 2 * nq:].reshape(B, S, GDN_HEADS, GDN_DV)
    af = a_f.astype(F32)
    ab = a_b.astype(F32)
    g_f = -jnp.exp(a_log_f.astype(F32)) * jax.nn.softplus(af + dt_bias_f.astype(F32))
    g_b = -jnp.exp(a_log_b.astype(F32)) * jax.nn.softplus(ab + dt_bias_b.astype(F32))
    beta_f = jax.nn.sigmoid(b_f.astype(F32))
    beta_b = jax.nn.sigmoid(b_b.astype(F32))
    qt, kt, vt = (jnp.moveaxis(t, 2, 1) for t in (q, k, v))
    g_ft, g_bt, be_ft, be_bt = (jnp.moveaxis(t, 2, 1) for t in (g_f, g_b, beta_f, beta_b))
    o_f = gated_delta_chunked(qt, kt, vt, g_ft, be_ft)
    flip = lambda t: jnp.flip(t, axis=2)
    o_b = flip(gated_delta_chunked(flip(qt), flip(kt), flip(vt), flip(g_bt), flip(be_bt)))
    o = jnp.moveaxis(o_f + o_b, 1, 2)
    o = rmsnorm(o, norm_w) * jax.nn.silu(z)
    return o.reshape(B, S, GDN_WIDTH)

def peer_ffn(xn, w_q, sub_keys, u_tab, v_tab):
    B, S, D = xn.shape
    T = B * S
    xt = xn.reshape(T, D)
    q = (xt @ w_q).reshape(T, PEER_HEADS, 2, PEER_HALF)
    scores = jnp.einsum('thpd,hpnd->thpn', q, sub_keys).astype(F32)
    s_top, i_top = lax.top_k(scores, PEER_TOPK)
    cand = s_top[:, :, 0, :, None] + s_top[:, :, 1, None, :]
    cand_idx = i_top[:, :, 0, :, None] * PEER_NKEYS + i_top[:, :, 1, None, :]
    f_s, f_i = lax.top_k(cand.reshape(T, PEER_HEADS, PEER_TOPK * PEER_TOPK), PEER_TOPK)
    experts = jnp.take_along_axis(cand_idx.reshape(T, PEER_HEADS, PEER_TOPK * PEER_TOPK), f_i, axis=-1)
    gates = jax.nn.softmax(f_s, axis=-1)
    nb = T // TOKEN_BLOCK
    xb = xt.reshape(nb, TOKEN_BLOCK, D)
    eb = experts.reshape(nb, TOKEN_BLOCK, PEER_HEADS * PEER_TOPK)
    gb = gates.reshape(nb, TOKEN_BLOCK, PEER_HEADS * PEER_TOPK)

    def blk(args):
        xc, ec, gc = args
        uc = u_tab[ec]
        hid = jax.nn.gelu(jnp.einsum('td,ted->te', xc, uc).astype(F32), approximate=False)
        vc = v_tab[ec]
        return jnp.einsum('te,ted->td', (gc * hid).astype(vc.dtype), vc)

    out = lax.map(blk, (xb, eb, gb))
    return out.reshape(B, S, D).astype(xn.dtype)

def setup_inputs(seed: int = 0) -> dict:
    key = jax.random.key(seed)
    ks = jax.random.split(key, 24)
    L = DEPTH

    def nrm(k, shape, scale):
        return jax.random.normal(k, shape, F32) * scale

    def gain(k, shape):
        return 1.0 + 0.01 * jax.random.normal(k, shape, F32)

    def dt_bias(k):
        dt = jnp.exp(jax.random.uniform(k, (L, GDN_HEADS), F32, math.log(1e-3), math.log(1e-1)))
        return dt + jnp.log(-jnp.expm1(-dt))

    x = nrm(ks[0], (BATCH, SEQ, D_MODEL), 1.0)
    positions = jnp.arange(SEQ, dtype=jnp.int32)[None, :] + jax.random.randint(ks[1], (BATCH, 1), 0, 1024, dtype=jnp.int32)
    return {
        'x': x,
        'positions': positions,
        'ln1_w': gain(ks[2], (L, D_MODEL)),
        'w_in': nrm(ks[3], (L, D_MODEL, IN_WIDTH), D_MODEL ** -0.5),
        'q_a_norm_w': gain(ks[4], (L, MLA_Q_RANK)),
        'w_q_up': nrm(ks[5], (L, MLA_Q_RANK, MLA_HEADS * (MLA_NOPE + MLA_ROPE)), MLA_Q_RANK ** -0.5),
        'kv_a_norm_w': gain(ks[6], (L, MLA_KV_RANK)),
        'w_kv_up': nrm(ks[7], (L, MLA_KV_RANK, MLA_HEADS * (MLA_NOPE + MLA_VDIM)), MLA_KV_RANK ** -0.5),
        'conv_w': nrm(ks[8], (L, CONV_K, GDN_QKV), CONV_K ** -0.5),
        'a_log_f': jnp.log(jax.random.uniform(ks[9], (L, GDN_HEADS), F32, 1.0, 16.0)),
        'dt_bias_f': dt_bias(ks[10]),
        'a_log_b': jnp.log(jax.random.uniform(ks[11], (L, GDN_HEADS), F32, 1.0, 16.0)),
        'dt_bias_b': dt_bias(ks[12]),
        'gdn_norm_w': gain(ks[13], (L, GDN_DV)),
        'w_out': nrm(ks[14], (L, MIX_WIDTH, D_MODEL), MIX_WIDTH ** -0.5),
        'ln2_w': gain(ks[15], (L, D_MODEL)),
        'peer_wq': nrm(ks[16], (L, D_MODEL, PEER_HEADS * PEER_QDIM), D_MODEL ** -0.5),
        'peer_sub_keys': nrm(ks[17], (L, PEER_HEADS, 2, PEER_NKEYS, PEER_HALF), PEER_HALF ** -0.5),
        'peer_u': nrm(ks[18], (L, PEER_EXPERTS, D_MODEL), D_MODEL ** -0.5),
        'peer_v': nrm(ks[19], (L, PEER_EXPERTS, D_MODEL), PEER_HEADS ** -0.5),
        'final_norm_w': gain(ks[20], (D_MODEL,)),
    }

def reference(x, positions, ln1_w, w_in, q_a_norm_w, w_q_up, kv_a_norm_w, w_kv_up, conv_w,
              a_log_f, dt_bias_f, a_log_b, dt_bias_b, gdn_norm_w, w_out, ln2_w,
              peer_wq, peer_sub_keys, peer_u, peer_v, final_norm_w):
    cos, sin = rope_tables(positions)
    h = x
    for i in range(DEPTH):
        n1 = rmsnorm(h, ln1_w[i])
        proj = n1 @ w_in[i]
        o_mla = mla_group(proj[..., :MLA_IN], cos, sin, q_a_norm_w[i], w_q_up[i], kv_a_norm_w[i], w_kv_up[i])
        o_gdn = gdn_group(proj[..., MLA_IN:], conv_w[i], a_log_f[i], dt_bias_f[i], a_log_b[i], dt_bias_b[i], gdn_norm_w[i])
        h = h + jnp.concatenate([o_mla, o_gdn], axis=-1) @ w_out[i]
        n2 = rmsnorm(h, ln2_w[i])
        h = h + peer_ffn(n2, peer_wq[i], peer_sub_keys[i], peer_u[i], peer_v[i])
    return rmsnorm(h, final_norm_w)


_drawn_inputs = setup_inputs


def setup_inputs(seed=0):
    import zlib

    import numpy as np

    out = dict(_drawn_inputs(seed))
    spreads = {}
    factors = {'ln1_w': 3.882,
     'q_a_norm_w': 30.705,
     'kv_a_norm_w': 25.624,
     'gdn_norm_w': 29.014,
     'ln2_w': 77.217,
     'final_norm_w': 200.0}
    for name, (base, spread) in spreads.items():
        noise = np.random.default_rng([zlib.crc32(name.encode()), seed]).standard_normal(out[name].shape)
        drawn = base * np.exp(spread * noise) if base else spread * noise
        out[name] = __import__('jax').numpy.asarray(drawn.astype(out[name].dtype))
    for name, factor in factors.items():
        out[name] = (out[name] * factor).astype(out[name].dtype)
    return out
```

```python
import math
import numpy as np
import concourse.bass as bass
from concourse import mybir
from contextlib import ExitStack

F32 = mybir.dt.float32
I32 = mybir.dt.int32
U32 = mybir.dt.uint32
ALU = mybir.AluOpType
ACT = mybir.ActivationFunctionType
AX = mybir.AxisListType.X

P = 128
D = 1024
S = 512
T = S // P
KD = D // P
NH = 4
NOPE, ROPE, VD = 128, 64, 128
HR = ROPE // 2
QR, KVR = 256, 128
MLA_IN = QR + KVR + ROPE
QKV0 = MLA_IN
CT_N = 12
Z0 = QKV0 + CT_N * P
G0 = Z0 + NH * P
IN_W = G0 + 4 * NH
TAPS = 5
LEVELS = 7
PH = 8
NK = 128
TOPK = 16
EPS = 1e-6
SCALE = (NOPE + ROPE) ** -0.5
BIG = 1e30
TWO_PI = 2 * math.pi
PI_HI = 6.28125
PI_LO = TWO_PI - PI_HI
PI_F = 3.1415925
MAGIC = 12582912.0
LOWEST = -3.0e38
UN, VN, DN = 8, 4, 8

CONSTS = ["ident", "tri_f", "tri_b", "strict_f", "strict_b", "incl_f", "incl_b"]
CONSTS += [f"off_{d}{l}" for d in "fb" for l in range(LEVELS)]
NCONST = len(CONSTS) * P
CONST_W = NCONST + HR + TOPK


def shape_constants():
    i, j = np.arange(P)[:, None], np.arange(P)[None, :]
    m = {"ident": i == j, "tri_f": i <= j, "tri_b": i >= j}
    m["strict_f"], m["strict_b"] = np.where(j < i, 0, BIG), np.where(j > i, 0, BIG)
    m["incl_f"], m["incl_b"] = np.where(j >= i, 0, BIG), np.where(j <= i, 0, BIG)
    for l in range(LEVELS):
        b = 1 << l
        off = (i // (2 * b) == j // (2 * b)) & ((i // b) % 2 == 1) & ((j // b) % 2 == 0)
        m[f"off_f{l}"], m[f"off_b{l}"] = off, off.T
    out = np.zeros((P, CONST_W), np.float32)
    for n, name in enumerate(CONSTS):
        out[:, n * P:(n + 1) * P] = m[name]
    inv = np.float32(10000.0) ** (-np.arange(0, ROPE, 2, dtype=np.float32) / np.float32(ROPE))
    out[:, NCONST:NCONST + HR] = inv
    out[:, NCONST + HR:] = np.arange(TOPK)
    return out


def opens(h):
    return isinstance(h, int) and h == 0


def over_rows(ap, n):
    return ap.unsqueeze(1).broadcast_to([ap.shape[0], n, ap.shape[1]])


def over_cols(ap, m):
    return ap.unsqueeze(len(ap.shape)).broadcast_to(list(ap.shape) + [m])


class Names:

    def __init__(self, nc, ctx):
        self._nc, self._ctx, self._made = nc, ctx, {}

    def __call__(self, name):
        if name not in self._made:
            self._made[name] = self._ctx.enter_context(self._nc.semaphore(name))
        return self._made[name]


def encoder_block(nc, x, positions, w_in, w_q_up, w_kv_up, a_log_f, dt_bias_f, a_log_b, dt_bias_b, w_out,
                  ln2_w, peer_wq, sub_keys, peer_u, peer_v, final_norm_w, columns, consts, out):
    ctx = ExitStack()
    with ctx:
        sem = Names(nc, ctx)

        def sb(name, shape, dt=F32):
            return ctx.enter_context(nc.sbuf_tensor(name, shape, dt))

        CONST = sb("CONST", [P, CONST_W])
        H = sb("H", [P, T, D])
        R1A = sb("R1A", [P, 16384])
        R1B = sb("R1B", [P, 8192])
        R2 = sb("R2", [P, 16384])
        MIXT = sb("MIXT", [P, KD, S])
        SMALL = sb("SMALL", [P, 1100])
        PS = ctx.enter_context(nc.psum_tensor("PS", [P, 8, 512], F32))

        cmat = {n: CONST[:, k * P:(k + 1) * P] for k, n in enumerate(CONSTS)}
        ident = cmat["ident"]
        inv_freq = CONST[:, NCONST:NCONST + HR]
        n1T = MIXT

        KA = 6
        WA = R1A[:, 0:KA * IN_W].rearrange("p (k n) -> p k n", n=IN_W)
        WB = R1B[:, 0:(KD - KA) * IN_W].rearrange("p (k n) -> p k n", n=IN_W)

        def w_in_at(k, c0, c1):
            return WA[:, k, c0:c1] if k < KA else WB[:, k - KA, c0:c1]

        off = (KD - KA) * IN_W
        WQU = R1B[:, off:off + 2 * 768].rearrange("p (k n) -> p k n", k=2)
        WKU = R1B[:, off + 1536:off + 1536 + 1024]
        XS = R2[:, 0:T * D].rearrange("p (t n) -> p t n", t=T)
        TOK = R2[:, 0:T * CT_N * P].rearrange("p (t c n) -> p t c n", t=T, c=CT_N)
        KQT = R2[:, 6144:10240].rearrange("p (h w s) -> p h w s", h=NH, w=2)
        Z = R2[:, 10240:12288].rearrange("p (t n) -> p t n", t=T)
        MISC = R2[:, 12288:16384]
        MG = MISC[:, 0:T * 464].rearrange("p (t n) -> p t n", t=T)
        RAW = [MISC[:, 1856 + 516 * i:1856 + 516 * (i + 1)] for i in range(2)]
        CV = [MISC[:, 2888 + 512 * i:2888 + 512 * (i + 1)] for i in range(2)]

        at = [0]

        def small(n):
            at[0] += n
            assert at[0] <= 1100, at
            return SMALL[:, at[0] - n:at[0]]

        ONES = small(P)
        COLS = small(72)
        ssq, rstd = small(T), small(T)
        ss2, r2 = small(8 * T), small(8 * T)
        ssm, rm = small(2 * T), small(2 * T)
        BIAS, ALOG = small(8), small(8)
        cos, sin = small(T * HR), small(T * HR)
        mx, nb, rs, rr = small(16), small(16), small(16), small(16)
        gc_ = small(32)
        eg_ = small(32)
        beta = small(32)
        gg = small(32)
        beg = small(32)
        skd = [small(4), small(4)]
        egl = [small(4), small(4)]
        osq, orr = small(16), small(16)
        POS_I, POS_F = small(T).bitcast(I32), small(T)
        G_A, G_NA, G_E, G_B = small(32), small(32), small(32), small(32)
        ANG, ANG_S, ANG_C, TURN = (R1B[:, 7584 + 128 * i:7712 + 128 * i] for i in range(4))
        SQ3 = PS[:, 7, :].rearrange("p (t n) -> p t n", t=T)
        SQA = CV[0]

        conv_col = lambda tap, c: COLS[:, tap * CT_N + c:tap * CT_N + c + 1]
        ln1_col = lambda k: COLS[:, 60 + k:61 + k]
        qa_col = lambda k: COLS[:, 68 + k:69 + k]
        kva_col, gdn_col = COLS[:, 70:71], COLS[:, 71:72]

        wsat = [0]

        def ws(n):
            wsat[0] += n
            assert wsat[0] <= 16384, wsat
            return R1A[:, wsat[0] - n:wsat[0]]

        CQ = ws(T * 384).rearrange("p (t n) -> p t n", t=T)
        CQT = ws(1024).rearrange("p (k s) -> p k s", k=2)
        CKVT = ws(512)
        KPR = ws(T * 128).rearrange("p (t n) -> p t n", t=T)
        KPET = ws(512)
        QNT = ws(2048).rearrange("p (h s) -> p h s", h=NH)
        KNT = ws(2048).rearrange("p (h s) -> p h s", h=NH)
        QPQPR = ws(2 * T * 256)
        QP = QPQPR[:, 0:1024].rearrange("p (t n) -> p t n", t=T)
        QPR = QPQPR[:, 1024:2048].rearrange("p (t n) -> p t n", t=T)
        QPET = ws(1024).rearrange("p (k s) -> p k s", k=2)
        VT = ws(2048).rearrange("p (t n) -> p t n", t=T)
        PR = [ws(512) for _ in range(2)]
        PT0 = ws(2048)
        PTs = [PT0.rearrange("p (k s) -> p k s", k=T),
               QPQPR.rearrange("p (k s) -> p k s", k=T)]
        ROT = [PT0[:, 0:128], PT0[:, 128:256]]

        gat = [0]

        def gw(n):
            gat[0] += n
            assert gat[0] <= 8192, gat
            return R1B[:, gat[0] - n:gat[0]]

        h4 = lambda ap: ap.rearrange("p (h n) -> p h n", h=NH)
        A = [gw(1024) for _ in range(2)]
        DIFF = [gw(512) for _ in range(2)]
        LO = [gw(512) for _ in range(2)]
        TM = [gw(512) for _ in range(2)]
        XM = [gw(512) for _ in range(2)]
        EG = [gw(512) for _ in range(2)]
        KBG = [MISC[:, 1856 + 512 * i:2368 + 512 * i] for i in range(2)]
        KDC = [MISC[:, 2880 + 512 * i:3392 + 512 * i] for i in range(2)]
        VB = [gw(512) for _ in range(2)]
        ST = [MISC[:, 512 * i:512 * (i + 1)] for i in range(2)]
        O = TOK[:, :, 0:NH, :]

        block = ctx.enter_context(nc.Block())

        dirs = "fb"
        chunk_of = lambda d, s: s if d == 0 else T - 1 - s
        last_of = (P - 1, 0)
        tok = lambda t: slice(t * P, (t + 1) * P)

        @block.sync
        def _(sp):
            sp.dma_start(CONST[:], consts).then_inc(sem("consts_in"), 16)
            for t in range(T):
                sp.dma_start(H[:, t, :], x[0, tok(t), :]).then_inc(sem(f"x_in{t}"), 16)
            sp.dma_start(COLS, columns).then_inc(sem("cols_in"), 16)
            sp.dma_start(POS_I, positions).then_inc(sem("pos_in"), 16)
            for g in range(4):
                c0, c1 = QKV0 + g * 3 * P, QKV0 + (g + 1) * 3 * P
                src = w_in[0].rearrange("(k p) n -> p k n", p=P)
                sp.dma_start(WA[:, :, c0:c1], src[:, 0:KA, c0:c1]).then_inc(sem(f"w_qkv{g}_in"), 16)
                sp.dma_start(WB[:, :, c0:c1], src[:, KA:KD, c0:c1]).then_inc(sem(f"w_qkv{g}_in"), 16)
            for c0, c1 in ((Z0, IN_W), (0, MLA_IN)):
                sp.dma_start(WA[:, :, c0:c1], src[:, 0:KA, c0:c1]).then_inc(sem("w_rest_in"), 16)
                sp.dma_start(WB[:, :, c0:c1], src[:, KA:KD, c0:c1]).then_inc(sem("w_rest_in"), 16)
            sp.dma_start(WQU, w_q_up[0].rearrange("(k p) n -> p k n", p=P)).then_inc(sem("w_up_in"), 16)
            sp.dma_start(WKU, w_kv_up[0]).then_inc(sem("w_up_in"), 16)

        @block.gpsimd
        def _(pool):
            for n, (src, dst) in enumerate(((dt_bias_f, BIAS[:, 0:4]), (dt_bias_b, BIAS[:, 4:8]),
                                            (a_log_f, ALOG[:, 0:4]), (a_log_b, ALOG[:, 4:8]))):
                pool.dma_start(dst, src[0].partition_broadcast(P)).then_inc(sem("gate_rows_in"), 16)
            nc.gpsimd.memset(ONES, 1.0).then_inc(sem("ones"), 1)

            def rotate(src1, src2, dst1, dst2, c, s, a, b, name, wait, n):
                pool.wait_ge(*wait)
                if n:
                    pool.wait_ge(sem(name), 6 * n)
                steps = [(a, src1, c, ALU.mult), (b, src2, s, ALU.mult), (dst1, a, b, ALU.subtract),
                         (a, src2, c, ALU.mult), (b, src1, s, ALU.mult), (dst2, a, b, ALU.add)]
                for k, (o, i0, i1, op) in enumerate(steps):
                    if k in (2, 3, 5):
                        pool.wait_ge(sem(name), 6 * n + k)
                    nc.gpsimd.tensor_tensor(o, i0, i1, op).then_inc(sem(name), 1)

            pool.wait_ge(sem("rotary_sin"), 2)
            ra, rb = (r[:, 0:128] for r in ROT)
            v3 = lambda ap: ap.rearrange("p (t n) -> p t n", n=HR)
            rotate(MG[:, :, 384:416], MG[:, :, 416:448], KPR[:, :, 0:HR], KPR[:, :, HR:ROPE],
                   v3(cos), v3(sin), v3(ra), v3(rb), "k_rotated", (sem("mg_ready"), T), 0)
            pool.wait_ge(sem("k_rotated"), 6)
            nc.gpsimd.tensor_copy(KPR[:, :, ROPE:2 * ROPE], KPR[:, :, 0:ROPE]).then_inc(sem("k_rotated"), 1)
            pool.wait_ge(sem("k_rotated"), 7)
            for t in range(T):
                q3 = QP[:, t, :].rearrange("p (h n) -> p h n", n=ROPE)
                o3 = QPR[:, t, :].rearrange("p (h n) -> p h n", n=ROPE)
                ct, st = (over_rows(m[:, t * HR:(t + 1) * HR], NH) for m in (cos, sin))
                rotate(q3[:, :, 0:HR], q3[:, :, HR:], o3[:, :, 0:HR], o3[:, :, HR:], ct, st,
                       v3(ra), v3(rb), "q_rotated", (sem("qp_ready"), 2 * t + 1), t)

            for s in range(T):
                for d in range(2):
                    t, D_ = chunk_of(d, s), dirs[d]
                    bs = slice((d * T + t) * NH, (d * T + t + 1) * NH)
                    pool.wait_ge(sem("exponents" + D_), s + 1)
                    if s:
                        pool.wait_ge(sem("o_mm" + D_), s)
                        pool.wait_ge(sem("state" + D_), s)
                    nc.gpsimd.tensor_tensor(h4(A[d][:, 0:512]), h4(DIFF[d]), over_rows(cmat["strict_" + D_], NH),
                                            ALU.add).then_inc(sem("masked" + D_), 1)
                    nc.gpsimd.tensor_tensor(h4(A[d][:, 512:1024]), over_rows(cmat["incl_" + D_], NH), h4(DIFF[d]),
                                            ALU.subtract).then_inc(sem("masked" + D_), 1)
                for d in range(2):
                    t, D_ = chunk_of(d, s), dirs[d]
                    bs = slice((d * T + t) * NH, (d * T + t + 1) * NH)
                    pool.wait_ge(sem("eg_row" + D_), 2 * s + 2)
                    pool.wait_ge(sem("egl" + D_), s + 1)
                    pool.wait_ge(sem("beta_eg"), 1)
                    nc.gpsimd.tensor_tensor(h4(VB[d]), TOK[:, t, 8:12, :], over_cols(beta[:, bs], P),
                                            ALU.mult).then_inc(sem("scaled" + D_), 1)
                    nc.gpsimd.tensor_tensor(h4(KBG[d]), TOK[:, t, 4:8, :], over_cols(beg[:, bs], P),
                                            ALU.mult).then_inc(sem("scaled" + D_), 1)
                    nc.gpsimd.tensor_tensor(h4(KDC[d]), TOK[:, t, 4:8, :], over_cols(skd[d], P),
                                            ALU.mult).then_inc(sem("scaled" + D_), 1)
                    nc.gpsimd.tensor_tensor(h4(EG[d]), KQT[:, :, 1, tok(t)], h4(EG[d]),
                                            ALU.mult).then_inc(sem("scaled" + D_), 1)
                for l in range(LEVELS):
                    for d in range(2):
                        D_ = dirs[d]
                        pool.wait_ge(sem("lower" + D_), s + 1)
                        if l == 1:
                            pool.wait_ge(sem("x_init" + D_), 2 * s + 2)
                        elif l > 1:
                            pool.wait_ge(sem("n_mm" + D_), s * 6 + l - 1)
                        elif s:
                            pool.wait_ge(sem("n_mm" + D_), s * 6)
                        nc.gpsimd.tensor_tensor(h4(LO[d]), h4(A[d][:, 0:512]), over_rows(cmat[f"off_{D_}{l}"], NH),
                                                ALU.mult).then_inc(sem("level" + D_), 1)

        @block.scalar
        def _(act):
            def act_(out, in_, f, name, **kw):
                return nc.scalar.activation(out, in_, f, **kw).then_inc(sem(name), 1)

            for t in range(T):
                act.wait_ge(sem(f"x_in{t}"), 16)
                act_(XS[:, t, :], H[:, t, :], ACT.Square, "x_squares", accum_out=ssq[:, t:t + 1])
            act.wait_ge(sem("mean_squares"), 1)
            act_(rstd, ssq, ACT.Sqrt, "roots")
            act.wait_ge(sem("cols_in"), 16)
            for k in range(1, KD, 2):
                act.wait_ge(sem("n1t_mm"), k + 1)
                act_(n1T[:, k, :], PS[:, k, :], ACT.Copy, "n1t", scale=ln1_col(k))

            def raw(c):
                act.wait_ge(sem("qkv_mm"), c + 1)
                if c >= 2:
                    act.wait_ge(sem("conv"), c - 1)
                act_(RAW[c % 2][:, 2:514], PS[:, c % 2, :], ACT.Copy, "raw")

            def silu(c):
                act.wait_ge(sem("conv"), c + 1)
                act_(CV[c % 2], CV[c % 2], ACT.Silu, "silu")

            def tok_copy(c):
                act.wait_ge(sem("conv_tp"), c + 1)
                act_(TOK[:, :, c, :], PS[:, 2 + c % 2, :].rearrange("p (t n) -> p t n", t=T), ACT.Copy, "tok")

            act.wait_ge(sem("raw_pads"), 4)
            act.wait_ge(sem("xs"), T)
            raw(0)
            for c in range(CT_N):
                if c + 1 < CT_N:
                    raw(c + 1)
                silu(c)
                if c >= 1:
                    tok_copy(c - 1)
            tok_copy(CT_N - 1)
            for t in range(T):
                act.wait_ge(sem("by_token_mm"), 2 * t + 1)
                act_(Z[:, t, :], PS[:, 4 + t % 2, :], ACT.Silu, "z")
            act.wait_ge(sem("mean_squares"), 2)
            act_(r2, ss2, ACT.Sqrt, "roots")
            act.wait_ge(sem("mean_squares"), 3)
            act_(rm, ssm, ACT.Sqrt, "roots")
            act.wait_ge(sem("rotary_args"), 1)
            act_(sin, ANG_S, ACT.Sin, "rotary_sin")
            act_(cos, ANG_C, ACT.Sin, "rotary_sin")

            act.wait_ge(sem("gate_args"), 1)
            act_(G_E, G_NA, ACT.Exp, "gate_exp", scale=-1.0)
            act.wait_ge(sem("gate_exp"), 1)
            act_(G_E, G_E, ACT.Ln, "gate_exp", bias=1.0)
            act_(G_B, G_B, ACT.Exp, "gate_exp", scale=-1.0)
            act.wait_ge(sem("gate_rows_in"), 64)
            act_(ALOG, ALOG, ACT.Exp, "gate_exp")

            for c in range(1, 8, 2):
                act.wait_ge(sem("kqt_mm"), c + 1)
                act_(KQT[:, c // 2, c % 2, :], PS[:, c, :], ACT.Copy, "kqt")
            for h in range(NH):
                act.wait_ge(sem("nope_mm"), 2 * h + 1)
                act_(QNT[:, h, :], PS[:, 4 + h % 2, :], ACT.Copy, "nope")
                act.wait_ge(sem("nope_mm"), 2 * h + 2)
                act_(KNT[:, h, :], PS[:, 6 + h % 2, :], ACT.Copy, "nope")

            def softmax_exp(n):
                act.wait_ge(sem("row_max"), n + 1)
                if n >= 2:
                    act.wait_ge(sem("p_tp"), n - 1)
                act_(PR[n % 2], PS[:, n % 2, :], ACT.Exp, "p_exp", bias=nb[:, n:n + 1], scale=SCALE,
                     accum_out=rs[:, n:n + 1])

            N = NH * T
            softmax_exp(0)
            for n in range(N):
                h, qt = divmod(n, T)
                if n + 1 < N:
                    softmax_exp(n + 1)
                act.wait_ge(sem("p_tp"), n + 1)
                if qt == 0 and h >= 2:
                    act.wait_ge(sem("pv_mm"), h - 1)
                act_(PTs[h % 2][:, :, tok(qt)], PS[:, 2 + n % 2, :].rearrange("p (k q) -> p k q", k=T),
                     ACT.Copy, "pt")

            act.wait_ge(sem("g_cum"), 2)
            act_(eg_, gc_, ACT.Exp, "eg")
            for s in range(T):
                for d in range(2):
                    D_, b = dirs[d], 4 * d
                    act.wait_ge(sem("g_rows" + D_), s + 1)
                    act.wait_ge(sem("exponents" + D_), s + 1)
                    if s:
                        act.wait_ge(sem("o_mm" + D_), s)
                        act.wait_ge(sem("state" + D_), s)
                    act_(EG[d], PS[:, b, :], ACT.Exp, "eg_row" + D_)
                    act_(skd[d], skd[d], ACT.Exp, "eg_row" + D_)
                for d in range(2):
                    D_ = dirs[d]
                    act.wait_ge(sem("masked" + D_), 2 * s + 2)
                    act_(A[d], A[d], ACT.Exp, "decay" + D_, scale=-1.0)
                for l in range(1, LEVELS):
                    for d in range(2):
                        D_, b = dirs[d], 4 * d
                        act.wait_ge(sem("n_mm" + D_), s * 6 + l)
                        act_(DIFF[d], PS[:, b + 1, :], ACT.Copy, "n" + D_)
                for d in range(2):
                    D_, b = dirs[d], 4 * d
                    act.wait_ge(sem("w_mm" + D_), s + 1)
                    act_(TM[d], PS[:, b + 1, :], ACT.Copy, "w" + D_, scale=-1.0)
                for d in range(2):
                    D_, b = dirs[d], 4 * d
                    act.wait_ge(sem("vn_mm" + D_), s + 1)
                    act_(KBG[d], PS[:, b + 2, :], ACT.Copy, "vn" + D_)
            act.wait_ge(sem("mean_squares"), 4)
            act_(orr, osq, ACT.Sqrt, "roots")

        @block.vector
        def _(dve):
            v = nc.vector
            chain = [0]

            def mark(ins):
                chain[0] += 1
                ins.then_inc(sem("dve_chain"), 1)

            def link(ins):
                mark(ins)
                dve.wait_ge(sem("dve_chain"), chain[0])

            for r in RAW:
                v.memset(r[:, 0:2], 0.0).then_inc(sem("raw_pads"), 1)
                v.memset(r[:, 514:516], 0.0).then_inc(sem("raw_pads"), 1)
            dve.wait_ge(sem("cols_in"), 16)
            dve.wait_ge(sem("x_squares"), T)
            v.tensor_scalar(ssq, ssq, 1.0 / D, EPS, ALU.mult, ALU.add).then_inc(sem("mean_squares"), 1)
            dve.wait_ge(sem("roots"), 1)
            link(v.reciprocal(rstd, rstd))
            for t in range(T):
                v.tensor_scalar(XS[:, t, :], H[:, t, :], rstd[:, t:t + 1], None, ALU.mult).then_inc(sem("xs"), 1)
            for k in range(0, KD, 2):
                dve.wait_ge(sem("n1t_mm"), k + 1)
                v.tensor_scalar(n1T[:, k, :], PS[:, k, :], ln1_col(k), None, ALU.mult).then_inc(sem("n1t"), 1)

            dve.wait_ge(sem("pos_in"), 16)
            dve.wait_ge(sem("consts_in"), 16)
            link(v.tensor_copy(POS_F, POS_I))
            a3 = lambda ap: ap.rearrange("p (t n) -> p t n", n=HR)
            link(v.tensor_tensor(a3(ANG), over_rows(inv_freq, T), over_cols(POS_F, HR), ALU.mult))
            for dst, shift in ((ANG_S, 0.0), (ANG_C, 0.25)):
                link(v.tensor_scalar(TURN, ANG, 1.0 / TWO_PI, shift, ALU.mult, ALU.add))
                link(v.tensor_scalar(TURN, TURN, MAGIC, None, ALU.add))
                link(v.tensor_scalar(TURN, TURN, -MAGIC, None, ALU.add))
                link(v.scalar_tensor_tensor(out=dst, in0=TURN, scalar=-PI_HI, in1=ANG, op0=ALU.mult, op1=ALU.add))
                link(v.scalar_tensor_tensor(out=dst, in0=TURN, scalar=-PI_LO, in1=dst, op0=ALU.mult, op1=ALU.add))
                if shift:
                    link(v.tensor_scalar(dst, dst, math.pi / 2, None, ALU.add))
                ins = v.tensor_scalar(dst, dst, PI_F, -PI_F, ALU.min, ALU.max)
                if shift:
                    ins.then_inc(sem("rotary_args"), 1)
                else:
                    link(ins)

            def conv(c):
                dve.wait_ge(sem("raw"), c + 1)
                if c >= 2:
                    dve.wait_ge(sem("conv_tp"), c - 1)
                r = RAW[c % 2]
                link(v.tensor_scalar(CV[c % 2], r[:, 0:512], conv_col(0, c), None, ALU.mult))
                for tap in range(1, TAPS):
                    ins = v.scalar_tensor_tensor(out=CV[c % 2], in0=r[:, tap:tap + 512], scalar=conv_col(tap, c),
                                                 in1=CV[c % 2], op0=ALU.mult, op1=ALU.add)
                    if tap < TAPS - 1:
                        link(ins)
                    else:
                        ins.then_inc(sem("conv"), 1)

            def qk_sum(c):
                dve.wait_ge(sem("tok"), c + 1)
                link(v.tensor_tensor(SQ3, TOK[:, :, c, :], TOK[:, :, c, :], ALU.mult))
                link(v.tensor_reduce(ss2[:, c * T:(c + 1) * T], SQ3, AX, ALU.add))

            for c in range(CT_N):
                conv(c)
                if 2 <= c < 10:
                    qk_sum(c - 2)
            v.tensor_scalar(ss2, ss2, EPS, None, ALU.add).then_inc(sem("mean_squares"), 1)
            for t in range(T):
                dve.wait_ge(sem("by_token_mm"), 2 * t + 2)
                v.tensor_copy(MG[:, t, :], PS[:, 6 + t % 2, 0:464]).then_inc(sem("mg_ready"), 1)
            dve.wait_ge(sem("mg_ready"), T)
            for t in range(T):
                for k, (a, b) in enumerate(((0, QR), (QR, QR + KVR))):
                    ins = v.tensor_tensor_reduce(out=SQA[:, a:b], in0=MG[:, t, a:b], in1=MG[:, t, a:b], scale=1.0 / (b - a),
                                                 scalar=EPS, op0=ALU.mult, op1=ALU.add,
                                                 accum_out=ssm[:, 2 * t + k:2 * t + k + 1])
                    if t == T - 1 and k == 1:
                        ins.then_inc(sem("mean_squares"), 1)
                    elif k:
                        link(ins)
            dve.wait_ge(sem("gate_rows_in"), 64)
            mg4 = MG[:, :, 448:464].rearrange("p t (d w h) -> p d t w h", d=2, w=2)
            for d in range(2):
                o3 = lambda ap: ap[:, 16 * d:16 * d + 16].rearrange("p (t h) -> p t h", t=T)
                mark(v.tensor_tensor(o3(G_A), mg4[:, d, :, 0, :], over_rows(BIAS[:, 4 * d:4 * d + 4], T), ALU.add))
                link(v.tensor_copy(o3(G_B), mg4[:, d, :, 1, :]))
            v.scalar_tensor_tensor(out=G_NA, in0=G_A, scalar=-1.0, in1=G_A, op0=ALU.mult, op1=ALU.max) \
                .then_inc(sem("gate_args"), 1)
            dve.wait_ge(sem("roots"), 2)
            link(v.reciprocal(r2, r2))
            link(v.tensor_scalar(r2[:, 0:NH * T], r2[:, 0:NH * T], float(P) ** -0.5, None, ALU.mult))
            r2v = r2.rearrange("p (c t) -> p t c", t=T)
            for t in range(T):
                v.tensor_tensor(TOK[:, t, 0:8, :], TOK[:, t, 0:8, :], over_cols(r2v[:, t, :], P), ALU.mult) \
                    .then_inc(sem("qk_unit"), 1)
            dve.wait_ge(sem("roots"), 3)
            link(v.reciprocal(rm, rm))
            dve.wait_ge(sem("by_token_mm"), 2 * T)
            for t in range(T):
                v.tensor_scalar(CQ[:, t, 0:QR], MG[:, t, 0:QR], rm[:, 2 * t:2 * t + 1], None, ALU.mult) \
                    .then_inc(sem("latents"), 1)
                v.tensor_scalar(CQ[:, t, QR:384], MG[:, t, QR:384], rm[:, 2 * t + 1:2 * t + 2], None, ALU.mult) \
                    .then_inc(sem("latents"), 1)
            for c in range(0, 8, 2):
                dve.wait_ge(sem("kqt_mm"), c + 1)
                v.tensor_copy(KQT[:, c // 2, c % 2, :], PS[:, c, :]).then_inc(sem("kqt"), 1)
            for k in range(3):
                dve.wait_ge(sem("latents_tp"), k + 1)
                dst, col = (CQT[:, k, :], qa_col(k)) if k < 2 else (CKVT, kva_col)
                v.tensor_scalar(dst, PS[:, k, :], col, None, ALU.mult).then_inc(sem("latents_t"), 1)
            for t in range(T):
                dve.wait_ge(sem("qp_mm"), 2 * t + 1)
                v.tensor_copy(QP[:, t, :], PS[:, t % 2, 0:256]).then_inc(sem("qp_ready"), 1)
                dve.wait_ge(sem("qp_mm"), 2 * t + 2)
                v.tensor_copy(VT[:, t, :], PS[:, 2 + t % 2, :]).then_inc(sem("qp_ready"), 1)
            dve.wait_ge(sem("pe_tp"), 1)
            v.tensor_copy(KPET, PS[:, 0, :]).then_inc(sem("pe_t"), 1)
            for pr in range(2):
                dve.wait_ge(sem("pe_tp"), pr + 2)
                v.tensor_copy(QPET[:, pr, :], PS[:, 1 + pr, :]).then_inc(sem("pe_t"), 1)

            dve.wait_ge(sem("gate_exp"), 4)
            link(v.scalar_tensor_tensor(out=gg, in0=G_A, scalar=0.0, in1=G_E, op0=ALU.max, op1=ALU.add))
            link(v.tensor_scalar(ALOG, ALOG, -1.0, None, ALU.mult))
            for d in range(2):
                o3 = gg[:, 16 * d:16 * d + 16].rearrange("p (t h) -> p t h", t=T)
                link(v.tensor_tensor(o3, o3, over_rows(ALOG[:, 4 * d:4 * d + 4], T), ALU.mult))
            v.tensor_scalar(beta, G_B, 1.0, None, ALU.add).then_inc(sem("g_ready"), 1)
            dve.wait_ge(sem("g_ready"), 1)
            link(v.reciprocal(beta, beta))

            def row_max(n):
                dve.wait_ge(sem("s_mm"), n + 1)
                link(v.reduce_max(mx[:, n:n + 1], PS[:, n % 2, :], AX))
                v.tensor_scalar(nb[:, n:n + 1], mx[:, n:n + 1], -SCALE, None, ALU.mult).then_inc(sem("row_max"), 1)

            N = NH * T
            row_max(0)
            for n in range(N):
                if n + 1 < N:
                    row_max(n + 1)
                dve.wait_ge(sem("p_exp"), n + 1)
                link(v.reciprocal(rr[:, n:n + 1], rs[:, n:n + 1]))
                v.tensor_scalar(PR[n % 2], PR[n % 2], rr[:, n:n + 1], None, ALU.mult).then_inc(sem("p_norm"), 1)
                h, qt = divmod(n, T)
                if qt == 1 and h:
                    dve.wait_ge(sem("pv_mm"), h)
                    v.tensor_copy(MIXT[:, h - 1, :], PS[:, 4 + (h - 1) % 2, :]).then_inc(sem("mla_out"), 1)
            dve.wait_ge(sem("pv_mm"), NH)
            v.tensor_copy(MIXT[:, NH - 1, :], PS[:, 4 + (NH - 1) % 2, :]).then_inc(sem("mla_out"), 1)

            for d in range(2):
                dve.wait_ge(sem("gc_mm"), d + 1)
                v.tensor_copy(gc_[:, 16 * d:16 * d + 16], PS[:, 4 * d, 0:16]).then_inc(sem("g_cum"), 1)
            dve.wait_ge(sem("eg"), 1)
            v.tensor_tensor(beg, beta, eg_, ALU.mult).then_inc(sem("beta_eg"), 1)
            for s in range(T):
                for d in range(2):
                    D_, t = dirs[d], chunk_of(d, s)
                    bs = slice((d * T + t) * NH, (d * T + t + 1) * NH)
                    if s:
                        dve.wait_ge(sem("d_mm" + D_), 6 * s)
                    v.tensor_tensor(h4(DIFF[d]), over_rows(cmat["tri_" + D_], NH), over_cols(gg[:, bs], P),
                                    ALU.mult).then_inc(sem("g_tri" + D_), 1)
                for d in range(2):
                    D_, t, b = dirs[d], chunk_of(d, s), 4 * d
                    bs = slice((d * T + t) * NH, (d * T + t + 1) * NH)
                    dve.wait_ge(sem("g_rows" + D_), s + 1)
                    if s:
                        dve.wait_ge(sem("scaled" + D_), 4 * s)
                    gl = h4(PS[:, b, :])[:, :, last_of[d]]
                    mark(v.tensor_tensor(skd[d], gl, gc_[:, bs], ALU.subtract))
                    v.tensor_tensor(h4(DIFF[d]), h4(PS[:, b, :]), over_cols(gc_[:, bs], P), ALU.subtract) \
                        .then_inc(sem("exponents" + D_), 1)
                for d in range(2):
                    D_ = dirs[d]
                    dve.wait_ge(sem("eg_row" + D_), 2 * s + 2)
                    v.tensor_copy(egl[d], h4(EG[d])[:, :, last_of[d]]).then_inc(sem("egl" + D_), 1)
                for d in range(2):
                    D_, t, b = dirs[d], chunk_of(d, s), 4 * d
                    dve.wait_ge(sem("decay" + D_), s + 1)
                    dve.wait_ge(sem("kq_mm" + D_), s + 1)
                    kq = PS[:, b + 1:b + 3, :].rearrange("p b (h w n) -> p (b h) w n", h=2, w=2)
                    for h in range(NH):
                        n = (d * T + t) * NH + h
                        ah = A[d][:, h * P:(h + 1) * P]
                        ins = v.scalar_tensor_tensor(out=ah, in0=kq[:, h, 0, :], scalar=beta[:, n:n + 1], in1=ah,
                                                     op0=ALU.mult, op1=ALU.mult)
                        if h < NH - 1:
                            mark(ins)
                    ins.then_inc(sem("lower" + D_), 1)
                    v.tensor_tensor(h4(A[d][:, 512:1024]), kq[:, :, 1, :], h4(A[d][:, 512:1024]), ALU.mult) \
                        .then_inc(sem("attn" + D_), 1)
                for d in range(2):
                    D_, b = dirs[d], 4 * d
                    dve.wait_ge(sem("lo_tp" + D_), s + 1)
                    if s:
                        dve.wait_ge(sem("vn_mm" + D_), s)
                    v.tensor_tensor(h4(TM[d]), over_rows(ident, NH), h4(LO[d]), ALU.subtract) \
                        .then_inc(sem("x_init" + D_), 1)
                    v.tensor_tensor(h4(XM[d]), over_rows(ident, NH), h4(PS[:, b + 3, :]), ALU.subtract) \
                        .then_inc(sem("x_init" + D_), 1)
                for l in range(1, LEVELS):
                    for d in range(2):
                        D_, b = dirs[d], 4 * d
                        dve.wait_ge(sem("d_mm" + D_), s * 6 + l)
                        if l < LEVELS - 1:
                            mark(v.tensor_tensor(TM[d], TM[d], PS[:, b + 3, :], ALU.subtract))
                        v.tensor_tensor(XM[d], XM[d], PS[:, b + 2, :], ALU.subtract).then_inc(sem("x_up" + D_), 1)
                for d in range(2):
                    D_, t, b = dirs[d], chunk_of(d, s), 4 * d
                    dve.wait_ge(sem("o_mm" + D_), s + 1)
                    o, ps = O[:, t, :, :], h4(PS[:, b + 3, :])
                    if s < T // 2:
                        v.tensor_copy(o, ps).then_inc(sem("o_out"), 1)
                    else:
                        dve.wait_ge(sem("o_out"), 2 * s)
                        v.tensor_tensor(o, o, ps, ALU.add).then_inc(sem("o_out"), 1)
                    if s == 0:
                        v.tensor_copy(ST[d], PS[:, b, :]).then_inc(sem("state" + D_), 1)
                    else:
                        for h in range(NH):
                            sh = ST[d][:, h * P:(h + 1) * P]
                            ins = v.scalar_tensor_tensor(out=sh, in0=sh, scalar=egl[d][:, h:h + 1],
                                                         in1=PS[:, b, h * P:(h + 1) * P], op0=ALU.mult, op1=ALU.add)
                            if h < NH - 1:
                                mark(ins)
                        ins.then_inc(sem("state" + D_), 1)
            dve.wait_ge(sem("o_out"), 2 * T)
            SQO = h4(DIFF[0])
            for t in range(T):
                link(v.tensor_tensor(SQO, O[:, t, :, :], O[:, t, :, :], ALU.mult))
                link(v.tensor_reduce(osq[:, t * NH:(t + 1) * NH], SQO, AX, ALU.add))
            v.tensor_scalar(osq, osq, 1.0 / P, EPS, ALU.mult, ALU.add).then_inc(sem("mean_squares"), 1)
            dve.wait_ge(sem("roots"), 4)
            link(v.reciprocal(orr, orr))
            for t in range(T):
                link(v.tensor_tensor(O[:, t, :, :], O[:, t, :, :], over_cols(orr[:, t * NH:(t + 1) * NH], P), ALU.mult))
                v.tensor_tensor(O[:, t, :, :], O[:, t, :, :], h4(Z[:, t, :]), ALU.mult).then_inc(sem("o_gated"), 1)
            for t in range(T):
                dve.wait_ge(sem("o_tp"), t + 1)
                v.tensor_scalar(MIXT[:, NH:2 * NH, tok(t)], h4(PS[:, t % 2, :]), gdn_col, None, ALU.mult) \
                    .then_inc(sem("gdn_out"), 1)

        @block.tensor
        def _(pe):
            mm = nc.tensor.matmul
            tp = lambda o, i, n=P: nc.tensor.transpose(o, i, ident[0:n, 0:n])
            pe.wait_ge(sem("consts_in"), 16)
            pe.wait_ge(sem("xs"), T)
            for k in range(KD):
                for t in range(T):
                    ins = tp(PS[:, k, tok(t)], XS[:, t, k * P:(k + 1) * P])
                ins.then_inc(sem("n1t_mm"), 1)
            pe.wait_ge(sem("n1t"), KD)

            def conv_tp(c):
                pe.wait_ge(sem("silu"), c + 1)
                if c >= 2:
                    pe.wait_ge(sem("tok"), c - 1)
                for t in range(T):
                    ins = tp(PS[:, 2 + c % 2, tok(t)], CV[c % 2][:, tok(t)])
                ins.then_inc(sem("conv_tp"), 1)

            for c in range(CT_N):
                pe.wait_ge(sem(f"w_qkv{c // 3}_in"), 32)
                if c >= 2:
                    pe.wait_ge(sem("raw"), c - 1)
                for k in range(KD):
                    c0 = QKV0 + c * P
                    ins = mm(PS[:, c % 2, :], w_in_at(k, c0, c0 + P), n1T[:, k, :], start=k == 0, stop=k == KD - 1)
                ins.then_inc(sem("qkv_mm"), 1)
                if c >= 2:
                    conv_tp(c - 2)
            pe.wait_ge(sem("w_rest_in"), 64)
            for t in range(T):
                if t >= 2:
                    pe.wait_ge(sem("z"), t - 1)
                    pe.wait_ge(sem("mg_ready"), t - 1)
                for k in range(KD):
                    ins = mm(PS[:, 4 + t % 2, :], n1T[:, k, tok(t)], w_in_at(k, Z0, G0), start=k == 0, stop=k == KD - 1)
                ins.then_inc(sem("by_token_mm"), 1)
                if t == 1:
                    pe.wait_ge(sem("mean_squares"), 2)
                for k in range(KD):
                    mm(PS[:, 6 + t % 2, 0:448], n1T[:, k, tok(t)], w_in_at(k, 0, MLA_IN), start=k == 0, stop=k == KD - 1)
                for k in range(KD):
                    ins = mm(PS[:, 6 + t % 2, 448:464], n1T[:, k, tok(t)], w_in_at(k, G0, IN_W), start=k == 0, stop=k == KD - 1)
                ins.then_inc(sem("by_token_mm"), 1)
                if t < 2:
                    conv_tp(CT_N - 2 + t)
            pe.wait_ge(sem("qk_unit"), T)
            pe.wait_ge(sem("tok"), CT_N)
            pe.wait_ge(sem("z"), T)
            pe.wait_ge(sem("mg_ready"), T)
            for c in range(8):
                h, w = divmod(c, 2)
                for t in range(T):
                    ins = tp(PS[:, c, tok(t)], TOK[:, t, h + (NH if w == 0 else 0), :])
                ins.then_inc(sem("kqt_mm"), 1)
            pe.wait_ge(sem("latents"), 2 * T)
            pe.wait_ge(sem("kqt"), 2 * NH)
            for k in range(3):
                for t in range(T):
                    ins = tp(PS[:, k, tok(t)], CQ[:, t, k * P:(k + 1) * P])
                ins.then_inc(sem("latents_tp"), 1)
            pe.wait_ge(sem("latents_t"), 3)
            pe.wait_ge(sem("w_up_in"), 32)
            for h in range(NH):
                if h >= 2:
                    pe.wait_ge(sem("nope"), 2 * (h - 1))
                for k in range(2):
                    ins = mm(PS[:, 4 + h % 2, :], WQU[:, k, h * 192:h * 192 + P], CQT[:, k, :], start=k == 0, stop=k == 1)
                ins.then_inc(sem("nope_mm"), 1)
                mm(PS[:, 6 + h % 2, :], WKU[:, h * 256:h * 256 + P], CKVT, start=True, stop=True) \
                    .then_inc(sem("nope_mm"), 1)
            for t in range(T):
                if t >= 2:
                    pe.wait_ge(sem("qp_ready"), 2 * (t - 1))
                for k in range(2):
                    w = WQU[:, k, :].rearrange("p (h n) -> p h n", h=NH)[:, :, NOPE:]
                    ins = mm(PS[:, t % 2, 0:256], CQT[:, k, tok(t)], w, start=k == 0, stop=k == 1)
                ins.then_inc(sem("qp_mm"), 1)
                w = WKU.rearrange("p (h n) -> p h n", h=NH)[:, :, NOPE:]
                mm(PS[:, 2 + t % 2, :], CKVT[:, tok(t)], w, start=True, stop=True).then_inc(sem("qp_mm"), 1)
            pe.wait_ge(sem("qp_ready"), 2 * T)
            pe.wait_ge(sem("k_rotated"), 7)
            for t in range(T):
                ins = tp(PS[:, 0, tok(t)], KPR[:, t, :])
            ins.then_inc(sem("pe_tp"), 1)
            pe.wait_ge(sem("q_rotated"), 6 * T)
            for pr in range(2):
                for t in range(T):
                    ins = tp(PS[:, 1 + pr, tok(t)], QPR[:, t, pr * P:(pr + 1) * P])
                ins.then_inc(sem("pe_tp"), 1)
            pe.wait_ge(sem("pe_t"), 3)
            pe.wait_ge(sem("nope"), 2 * NH)

            def scores(n):
                h, qt = divmod(n, T)
                if n >= 2:
                    pe.wait_ge(sem("p_exp"), n - 1)
                mm(PS[:, n % 2, :], QNT[:, h, tok(qt)], KNT[:, h, :], start=True, stop=False)
                r = slice(64 * (h % 2), 64 * (h % 2) + 64)
                mm(PS[:, n % 2, :], QPET[r, h // 2, tok(qt)], KPET[r, :], start=False, stop=True) \
                    .then_inc(sem("s_mm"), 1)

            def values(h):
                pe.wait_ge(sem("pt"), T * (h + 1))
                if h >= 2:
                    pe.wait_ge(sem("mla_out"), h - 1)
                for kt in range(T):
                    ins = mm(PS[:, 4 + h % 2, :], VT[:, kt, h * P:(h + 1) * P], PTs[h % 2][:, kt, :],
                             start=kt == 0, stop=kt == T - 1)
                ins.then_inc(sem("pv_mm"), 1)

            scores(0)
            for n in range(NH * T):
                if n + 1 < NH * T:
                    scores(n + 1)
                if n % T == 0 and n:
                    values(n // T - 1)
                pe.wait_ge(sem("p_norm"), n + 1)
                if n >= 2:
                    pe.wait_ge(sem("pt"), n - 1)
                for kt in range(T):
                    ins = tp(PS[:, 2 + n % 2, tok(kt)], PR[n % 2][:, tok(kt)])
                ins.then_inc(sem("p_tp"), 1)
            values(NH - 1)

            pe.wait_ge(sem("mla_out"), NH)
            pe.wait_ge(sem("p_exp"), NH * T)
            pe.wait_ge(sem("pt"), NH * T)
            pe.wait_ge(sem("g_ready"), 1)
            pe.wait_ge(sem("ones"), 1)
            for d in range(2):
                mm(PS[:, 4 * d, 0:16], cmat["tri_" + dirs[d]], gg[:, 16 * d:16 * d + 16], start=True, stop=True) \
                    .then_inc(sem("gc_mm"), 1)
            pe.wait_ge(sem("g_cum"), 2)
            hs = lambda h: slice(h * P, (h + 1) * P)
            for s in range(T):
                for d in range(2):
                    D_, t, b = dirs[d], chunk_of(d, s), 4 * d
                    pe.wait_ge(sem("g_tri" + D_), s + 1)
                    if s:
                        pe.wait_ge(sem("state" + D_), s)
                    mm(PS[:, b, :], ONES, DIFF[d], start=True, stop=True).then_inc(sem("g_rows" + D_), 1)
                    if s:
                        pe.wait_ge(sem("w" + D_), s)
                        pe.wait_ge(sem("vn" + D_), s)
                    for h in range(NH):
                        o = PS[:, b + 1 + h // 2, 256 * (h % 2):256 * (h % 2) + 256]
                        ins = mm(o.rearrange("p (w n) -> p w n", w=2), KQT[:, h, 0, tok(t)], KQT[:, h, :, tok(t)],
                                 start=True, stop=True)
                    ins.then_inc(sem("kq_mm" + D_), 1)
                for d in range(2):
                    D_, b = dirs[d], 4 * d
                    pe.wait_ge(sem("level" + D_), LEVELS * s + 1)
                    for h in range(NH):
                        ins = tp(PS[:, b + 3, hs(h)], LO[d][:, hs(h)])
                    ins.then_inc(sem("lo_tp" + D_), 1)
                for l in range(1, LEVELS):
                    for d in range(2):
                        D_, b = dirs[d], 4 * d
                        pe.wait_ge(sem("level" + D_), LEVELS * s + l + 1)
                        if l == 1:
                            pe.wait_ge(sem("x_init" + D_), 2 * s + 2)
                            pe.wait_ge(sem("attn" + D_), s + 1)
                        else:
                            pe.wait_ge(sem("x_up" + D_), 6 * s + l - 1)
                        for h in range(NH):
                            ins = mm(PS[:, b + 1, hs(h)], LO[d][:, hs(h)], XM[d][:, hs(h)], start=True, stop=True)
                        ins.then_inc(sem("n_mm" + D_), 1)
                    for d in range(2):
                        D_, b = dirs[d], 4 * d
                        pe.wait_ge(sem("n" + D_), 6 * s + l)
                        for h in range(NH):
                            ins = mm(PS[:, b + 2, hs(h)], TM[d][:, hs(h)], DIFF[d][:, hs(h)], start=True, stop=True)
                        if l < LEVELS - 1:
                            for h in range(NH):
                                ins = mm(PS[:, b + 3, hs(h)], DIFF[d][:, hs(h)], TM[d][:, hs(h)], start=True, stop=True)
                        ins.then_inc(sem("d_mm" + D_), 1)
                for d in range(2):
                    D_, b = dirs[d], 4 * d
                    pe.wait_ge(sem("scaled" + D_), 4 * s + 4)
                    pe.wait_ge(sem("x_up" + D_), 6 * s + 6)
                    for h in range(NH):
                        ins = mm(PS[:, b + 1, hs(h)], KBG[d][:, hs(h)], XM[d][:, hs(h)], start=True, stop=True)
                    ins.then_inc(sem("w_mm" + D_), 1)
                for d in range(2):
                    D_, b = dirs[d], 4 * d
                    pe.wait_ge(sem("w" + D_), s + 1)
                    for h in range(NH):
                        ins = mm(PS[:, b + 2, hs(h)], XM[d][:, hs(h)], VB[d][:, hs(h)], start=True, stop=s == 0)
                        if s:
                            ins = mm(PS[:, b + 2, hs(h)], TM[d][:, hs(h)], ST[d][:, hs(h)], start=False, stop=True)
                    ins.then_inc(sem("vn_mm" + D_), 1)
                for d in range(2):
                    D_, b = dirs[d], 4 * d
                    pe.wait_ge(sem("vn" + D_), s + 1)
                    for h in range(NH):
                        mm(PS[:, b, hs(h)], KDC[d][:, hs(h)], KBG[d][:, hs(h)], start=True, stop=True)
                    for h in range(NH):
                        if s:
                            mm(PS[:, b + 3, hs(h)], EG[d][:, hs(h)], ST[d][:, hs(h)], start=True, stop=False)
                        ins = mm(PS[:, b + 3, hs(h)], A[d][:, 512 + h * P:512 + (h + 1) * P], KBG[d][:, hs(h)],
                                 start=s == 0, stop=True)
                    ins.then_inc(sem("o_mm" + D_), 1)
            for t in range(T):
                pe.wait_ge(sem("o_gated"), t + 1)
                if t == 0:
                    pe.wait_ge(sem("o_out"), 2 * T)
                    pe.wait_ge(sem("statef"), T)
                if t >= 2:
                    pe.wait_ge(sem("gdn_out"), t - 1)
                for h in range(NH):
                    ins = tp(PS[:, t % 2, hs(h)], O[:, t, h, :])
                ins.then_inc(sem("o_tp"), 1)

        WO = R1B[:, :].rearrange("p (k n) -> p k n", k=KD)
        WQ = R1A[:, :].rearrange("p (k n) -> p k n", k=KD)
        N2 = MIXT[:, :, :].rearrange("p k s -> p (k s)").rearrange("p (t n) -> p t n", t=T)
        SKT = CONST[:, P:P + 2 * PH * NK].rearrange("p (c n) -> p c n", n=NK)
        iota = CONST[:, NCONST + HR:]
        UR = [R2[:, D * j:D * (j + 1)] for j in range(UN)]
        VR = [R2[:, D * (UN + j):D * (UN + j + 1)] for j in range(VN)]
        LN2B, FINB, YS = (R2[:, 12288 + D * j:12288 + D * (j + 1)] for j in range(3))
        DG = [R2[:, 15360 + P * j:15360 + P * (j + 1)] for j in range(DN)]
        rat = [0]

        def rw(n):
            rat[0] += n
            assert rat[0] <= 8192, rat
            return R1B[:, rat[0] - n:rat[0]]

        QPT = rw(1024).rearrange("p (c n) -> p c n", n=P)
        N2T = LN2B.rearrange("p (k n) -> p k n", n=P)
        SCORES = [rw(2048) for _ in range(2)]
        SC, SC2, CAND, CAND2, OH = rw(256), rw(256), rw(256), rw(256), rw(512)
        TOPS, TOPI, TOPIF = rw(32), rw(32).bitcast(U32), rw(32)
        BEST, BESTI, BESTIJ, BESTF, ROWS = rw(16), rw(16).bitcast(U32), rw(32).bitcast(U32), rw(32), rw(32)
        EXPERT, GATE = [rw(TOPK).bitcast(I32) for _ in range(2)], [rw(TOPK) for _ in range(2)]
        UIDX, VIDX = ([rw(TOPK).bitcast(I32) for _ in range(2)] for _ in range(2))
        HID, GEL, WGT = ([rw(TOPK) for _ in range(2)] for _ in range(3))
        n2sq, n2r, gsum = ssq, rstd, [rw(1) for _ in range(2)]
        ysq = [rw(1) for _ in range(2)]

        def steps(eng, body):
            for t in range(T):
                body(t, 0, 0)
                if t == 0:
                    body(t, 1, 1)
                    body(t, 2, 0)
                with eng.Fori(1 if t == 0 else 0, 3, 1) as i:
                    body(t, 2 * i + 1, 1)
                    body(t, 2 * i + 2, 0)
                body(t, PH - 1, 1)
            body(T, 0, 0)

        @block.sync
        def _(sp):
            sp.wait_ge(sem("mla_out"), NH)
            sp.wait_ge(sem("pt"), NH * T)
            sp.dma_start(WQ, peer_wq[0].rearrange("(k p) n -> p k n", p=P)).then_inc(sem("wq_in"), 16)
            sp.wait_ge(sem("mean_squares"), 4)
            for k in range(0, KD, 4):
                sp.dma_start(WO[:, k:k + 4, :], w_out[0].rearrange("(k p) n -> p k n", p=P)[:, k:k + 4, :]) \
                    .then_inc(sem("wo_in"), 16)
            sp.dma_start(LN2B, ln2_w[0].partition_broadcast(P)).then_inc(sem("ln2_in"), 16)
            sp.dma_start(SKT, sub_keys).then_inc(sem("keys_in"), 16)
            sp.dma_start(FINB, final_norm_w.partition_broadcast(P)).then_inc(sem("fin_in"), 16)
            for t in range(T):
                sp.wait_ge(sem("y_dve"), 3 * (t + 1))
                sp.dma_start(out[0, tok(t), :], YS).then_inc(sem("y_out"), 16)
            sp.wait_ge(sem("y_out"), 16 * T)

        @block.gpsimd
        def _(pool):
            def hold(name, value):
                pool.wait_ge(sem(name), value)
                pool.sem_inc(sem("gather_may_go"), 1)

            def body(t, h, par):
                first, last = (t == 0 and opens(h)), t == T
                gu = PH * t + h
                gv = gu - 1
                if not last:
                    hold("experts", gu + 1)
                    if not first:
                        hold("u_dot", TOPK * gu - 8)
                    nc.gpsimd.tensor_copy(UIDX[par], EXPERT[par]).then_inc(sem("u_idx"), 1)
                if not first:
                    nc.gpsimd.tensor_copy(VIDX[1 - par], UIDX[1 - par]).then_inc(sem("v_idx"), 1)
                    hold("v_idx", gv + 1)
                if not last:
                    hold("u_idx", gu + 1)
                for s in range(TOPK):
                    if not last:
                        if not first or s >= UN:
                            hold("u_dot", TOPK * gu + s + 1 - UN)
                        pool.indirect_dma_start(UR[s % UN], None, peer_u[0],
                                                bass.IndirectOffsetOnAxis(ap=UIDX[par][:, s:s + 1], axis=0)) \
                            .then_inc(sem(f"u_row{s % UN}"), 16)
                    if not first:
                        if not isinstance(gv, int) or TOPK * gv + s + 1 > VN:
                            hold("v_sum", TOPK * gv + s + 1 - VN)
                        pool.indirect_dma_start(VR[s % VN], None, peer_v[0],
                                                bass.IndirectOffsetOnAxis(ap=VIDX[1 - par][:, s:s + 1], axis=0)) \
                            .then_inc(sem(f"v_row{s % VN}"), 16)

            pool.wait_ge(sem("o_tp"), T)
            pool.wait_ge(sem("gdn_out"), T)
            steps(pool, body)

        @block.scalar
        def _(act):
            def act_(out, in_, f, name, **kw):
                return nc.scalar.activation(out, in_, f, **kw).then_inc(sem(name), 1)

            for t in range(T):
                act.wait_ge(sem("h_sum"), t + 1)
                if t:
                    act.wait_ge(sem("n2_squares"), t)
                act_(YS, H[:, t, :], ACT.Square, "n2_squares", accum_out=n2sq[:, t:t + 1])
            act.wait_ge(sem("mean_squares"), 5)
            act_(n2r, n2sq, ACT.Sqrt, "roots")

            def queries(t, b):
                act.wait_ge(sem("q_mm"), 4 * t + b + 1)
                if 4 * t + b >= 2:
                    act.wait_ge(sem("score_mm"), 4 * t + b - 1)
                act_(QPT[:, 4 * (b % 2):4 * (b % 2) + 4, :], h4(PS[:, 6 + b % 2, :]), ACT.Copy, "q")

            def scores(t, b):
                act.wait_ge(sem("score_mm"), 4 * t + b + 1)
                if t >= 2:
                    act.wait_ge(sem("experts"), PH * (t - 1))
                act_(SCORES[t % 2][:, 512 * b:512 * (b + 1)], PS[:, 4 + b % 2, :], ACT.Copy, "scores")

            def normed(t):
                act.wait_ge(sem("n2t_mm"), t + 1)
                act_(N2T.rearrange("p k n -> p (k n)"), PS[:, 4:6, :].rearrange("p b n -> p (b n)"), ACT.Copy, "n2t")

            def front_after(t, half, s):
                if half == 0 and s == 0:
                    normed(t)
                if s in (4, 8):
                    queries(t, 2 * half + (s == 8))
                if s in (12, 14):
                    scores(t, 2 * half + (s == 14))

            def body(t, h, par):
                first, last = (t == 0 and opens(h)), t == T
                gu = PH * t + h
                gv = gu - 1
                half = 0 if opens(h) else 1 if isinstance(h, int) and h == PH - 1 else None
                if t >= T - 1:
                    half = None
                if not first:
                    act.wait_ge(sem("u_dot"), TOPK * (gv + 1))
                    act_(GEL[1 - par], HID[1 - par], ACT.Gelu, "gelu")
                    act.wait_ge(sem("weight"), gv + 1)
                for s in range(TOPK):
                    if not first:
                        if not isinstance(gv, int) or TOPK * gv + s + 1 > DN:
                            act.wait_ge(sem("v_sum"), TOPK * gv + s + 1 - DN)
                        act_(DG[s % DN], ident, ACT.Copy, "diag", scale=WGT[1 - par][:, s:s + 1])
                    if half is not None:
                        front_after(t + 1, half, s)
                if not (t == T or (t == T - 1 and isinstance(h, int) and h == PH - 1)):
                    act.wait_ge(sem("gate_arg"), gu + 2)
                    act_(GATE[1 - par], GATE[1 - par], ACT.Exp, "gate_exps", accum_out=gsum[1 - par])
                if opens(h) and t:
                    b = 2 * ((t - 1) % 2)
                    act.wait_ge(sem("v_sum"), TOPK * PH * t)
                    if t >= 2:
                        act.wait_ge(sem("y_out"), 16 * (t - 1))
                    act_(YS, PS[:, b:b + 2, :].rearrange("p b n -> p (b n)"), ACT.Square, "y_act", accum_out=ysq[0])
                    act.wait_ge(sem("y_dve"), 3 * t - 2)
                    act_(ysq[1], ysq[0], ACT.Sqrt, "y_act")
                    act.wait_ge(sem("y_dve"), 3 * t - 1)
                    act_(YS, PS[:, b:b + 2, :].rearrange("p b n -> p (b n)"), ACT.Copy, "y_act", scale=ysq[1])

            normed(0)
            for b in range(2):
                queries(0, b)
            for b in range(2):
                scores(0, b)
            for b in range(2, 4):
                queries(0, b)
            for b in range(2, 4):
                scores(0, b)
            act.wait_ge(sem("gate_arg"), 1)
            act_(GATE[0], GATE[0], ACT.Exp, "gate_exps", accum_out=gsum[0])
            steps(act, body)

        @block.vector
        def _(dve):
            v = nc.vector
            for t in range(T):
                dve.wait_ge(sem("out_mm"), t + 1)
                b = 2 * (t % 2)
                v.tensor_tensor(H[:, t, :], H[:, t, :], PS[:, b:b + 2, :].rearrange("p b n -> p (b n)"), ALU.add) \
                    .then_inc(sem("h_sum"), 1)
            dve.wait_ge(sem("n2_squares"), T)
            v.tensor_scalar(n2sq, n2sq, 1.0 / D, EPS, ALU.mult, ALU.add).then_inc(sem("mean_squares"), 1)
            dve.wait_ge(sem("roots"), 5)
            v.reciprocal(n2r, n2r)
            v.drain()
            dve.wait_ge(sem("ln2_in"), 16)
            for t in range(T):
                v.scalar_tensor_tensor(out=N2[:, t, :], in0=H[:, t, :], scalar=n2r[:, t:t + 1], in1=LN2B,
                                       op0=ALU.mult, op1=ALU.mult).then_inc(sem("n2"), 1)

            def top_experts(t, h, par):
                v.tensor_copy(SC, SCORES[t % 2][:, bass.ds(256 * h, 256)])
                v.drain()
                half = lambda ap, w: ap[:, NK * w:NK * (w + 1)]
                s8 = lambda ap, w, r: ap[:, TOPK * w + 8 * r:TOPK * w + 8 * r + 8]
                for w in range(2):
                    v.max(s8(TOPS, w, 0), half(SC, w))
                v.drain()
                for w in range(2):
                    v.match_replace(half(SC2, w), s8(TOPS, w, 0), half(SC, w), LOWEST)
                for w in range(2):
                    v.max_index(s8(TOPI, w, 0), s8(TOPS, w, 0), half(SC, w))
                v.drain()
                for w in range(2):
                    v.max(s8(TOPS, w, 1), half(SC2, w))
                v.drain()
                for w in range(2):
                    v.max_index(s8(TOPI, w, 1), s8(TOPS, w, 1), half(SC2, w))
                c3 = lambda ap: ap.rearrange("p (i j) -> p i j", i=TOPK)
                v.tensor_tensor(c3(CAND), over_cols(TOPS[:, 0:TOPK], TOPK), over_rows(TOPS[:, TOPK:2 * TOPK], TOPK), ALU.add)
                v.drain()
                v.tensor_copy(TOPIF, TOPI)
                v.max(BEST[:, 0:8], CAND)
                v.drain()
                v.match_replace(CAND2, BEST[:, 0:8], CAND, LOWEST)
                v.max_index(BESTI[:, 0:8], BEST[:, 0:8], CAND)
                v.drain()
                v.max(BEST[:, 8:16], CAND2)
                v.drain()
                v.max_index(BESTI[:, 8:16], BEST[:, 8:16], CAND2)
                v.tensor_scalar(GATE[par], BEST, BEST[:, 0:1], None, ALU.subtract).then_inc(sem("gate_arg"), 1)
                v.drain()
                v.tensor_scalar(BESTIJ[:, 0:TOPK], BESTI, 4, None, ALU.logical_shift_right)
                v.tensor_scalar(BESTIJ[:, TOPK:], BESTI, TOPK - 1, None, ALU.bitwise_and)
                v.drain()
                v.tensor_copy(BESTF, BESTIJ)
                v.drain()
                o3 = OH.rearrange("p (k j) -> p k j", j=TOPK)
                v.tensor_tensor(o3, over_cols(BESTF, TOPK), over_rows(iota, 2 * TOPK), ALU.is_equal)
                v.drain()
                o4 = OH.rearrange("p (w k j) -> p w k j", w=2, j=TOPK)
                keys = TOPIF.rearrange("p (w j) -> p w j", w=2).unsqueeze(2).broadcast_to([P, 2, TOPK, TOPK])
                v.tensor_tensor(o4, o4, keys, ALU.mult)
                v.drain()
                v.tensor_reduce(ROWS, o3, AX, ALU.add)
                v.drain()
                if not (isinstance(h, int) and PH * t + h < 2):
                    dve.wait_ge(sem("u_idx"), PH * t + h - 1)
                v.scalar_tensor_tensor(out=EXPERT[par], in0=ROWS[:, 0:TOPK],
                                       scalar=float(NK), in1=ROWS[:, TOPK:], op0=ALU.mult, op1=ALU.add) \
                    .then_inc(sem("experts"), 1)

            def body(t, h, par):
                first, last = (t == 0 and opens(h)), t == T
                gu = PH * t + h
                gv = gu - 1

                def weights():
                    dve.wait_ge(sem("gate_exps"), gv + 1)
                    v.reciprocal(gsum[1 - par], gsum[1 - par])
                    v.drain()
                    dve.wait_ge(sem("gelu"), gv + 1)
                    v.scalar_tensor_tensor(out=WGT[1 - par], in0=GEL[1 - par], scalar=gsum[1 - par], in1=GATE[1 - par],
                                           op0=ALU.mult, op1=ALU.mult).then_inc(sem("weight"), 1)

                if last:
                    weights()
                else:
                    for s in range(TOPK):
                        if s == 2 and not first:
                            weights()
                        if s == 4:
                            if isinstance(h, int) and h == PH - 1:
                                if t < T - 1:
                                    dve.wait_ge(sem("scores"), 4 * (t + 1) + 1)
                                    top_experts(t + 1, 0, 1 - par)
                            else:
                                if isinstance(h, int) or t:
                                    dve.wait_ge(sem("scores"), 4 * t + ((h + 1) // 2 + 1 if t == 0 else 4))
                                else:
                                    dve.wait_ge(sem("scores"), 4)
                                top_experts(t, h + 1, 1 - par)
                        dve.wait_ge(sem(f"u_row{s % UN}"), 16 * ((TOPK // UN) * gu + s // UN + 1))
                        v.tensor_tensor_reduce(out=UR[s % UN], in0=UR[s % UN], in1=N2[:, t, :], scale=1.0, scalar=0.0,
                                               op0=ALU.mult, op1=ALU.add, accum_out=HID[par][:, s:s + 1]) \
                            .then_inc(sem("u_dot"), 1)
                if opens(h) and t:
                    dve.wait_ge(sem("y_act"), 3 * t - 2)
                    v.tensor_scalar(ysq[0], ysq[0], 1.0 / D, EPS, ALU.mult, ALU.add).then_inc(sem("y_dve"), 1)
                    dve.wait_ge(sem("y_act"), 3 * t - 1)
                    v.reciprocal(ysq[1], ysq[1]).then_inc(sem("y_dve"), 1)
                    dve.wait_ge(sem("y_act"), 3 * t)
                    dve.wait_ge(sem("fin_in"), 16)
                    v.tensor_tensor(YS, YS, FINB, ALU.mult).then_inc(sem("y_dve"), 1)

            dve.wait_ge(sem("keys_in"), 16)
            dve.wait_ge(sem("scores"), 1)
            top_experts(0, 0, 0)
            steps(dve, body)

        @block.tensor
        def _(pe):
            mm = nc.tensor.matmul
            for t in range(T):
                b = 2 * (t % 2)
                if t == 0:
                    pe.wait_ge(sem("gdn_out"), T)
                    pe.wait_ge(sem("wo_in"), 32)
                if t >= 2:
                    pe.wait_ge(sem("h_sum"), t - 1)
                for half in range(2):
                    for k in range(KD):
                        ins = mm(PS[:, b + half, :], MIXT[:, k, tok(t)], WO[:, k, 512 * half:512 * half + 512],
                                 start=k == 0, stop=k == KD - 1)
                ins.then_inc(sem("out_mm"), 1)
            pe.wait_ge(sem("h_sum"), T)

            cols = lambda c: slice((c % 4) * P, (c % 4 + 1) * P)

            def normed(t):
                pe.wait_ge(sem("n2"), T)
                if t:
                    pe.wait_ge(sem("scores"), 4 * t)
                for k in range(KD):
                    ins = nc.tensor.transpose(PS[:, 4 + k // 4, cols(k)], N2[:, t, k * P:(k + 1) * P], ident)
                ins.then_inc(sem("n2t_mm"), 1)

            def query(t, c):
                b = c // 4
                if c == 0:
                    pe.wait_ge(sem("n2t"), t + 1)
                if c % 4 == 0 and 4 * t + b >= 2:
                    pe.wait_ge(sem("q"), 4 * t + b - 1)
                for k in range(KD):
                    ins = mm(PS[:, 6 + b % 2, cols(c)], WQ[:, k, c * P:(c + 1) * P], N2T[:, k, :],
                             start=k == 0, stop=k == KD - 1)
                if c % 4 == 3:
                    ins.then_inc(sem("q_mm"), 1)

            def score(t, b):
                pe.wait_ge(sem("q"), 4 * t + b + 1)
                if 4 * t + b >= 2:
                    pe.wait_ge(sem("scores"), 4 * t + b - 1)
                for c in range(4 * b, 4 * b + 4):
                    ins = mm(PS[:, 4 + b % 2, cols(c)], QPT[:, c % 8, :], SKT[:, c, :], start=True, stop=True)
                ins.then_inc(sem("score_mm"), 1)

            def front_after(t, half, s):
                if half == 0 and s == 0:
                    normed(t)
                if s < 8:
                    query(t, 8 * half + s)
                if s in (10, 12):
                    score(t, 2 * half + (s == 12))

            def body(t, h, par):
                first, last = (t == 0 and opens(h)), t == T
                gu = PH * t + h
                gv = gu - 1
                tv = t - 1 if opens(h) else t
                half = 0 if opens(h) else 1 if isinstance(h, int) and h == PH - 1 else None
                if t >= T - 1:
                    half = None
                for s in range(TOPK):
                    if not first:
                        pe.wait_ge(sem("diag"), TOPK * gv + s + 1)
                        pe.wait_ge(sem(f"v_row{s % VN}"), 16 * ((TOPK // VN) * gv + s // VN + 1))
                        for c in range(2):
                            ins = mm(PS[:, 2 * (tv % 2) + c, :], DG[s % DN], VR[s % VN][:, 512 * c:512 * c + 512],
                                     start=False, stop=tv != t and s == TOPK - 1)
                        ins.then_inc(sem("v_sum"), 1)
                    if half is not None:
                        front_after(t + 1, half, s)
                if opens(h) and not last:
                    if t >= 2:
                        pe.wait_ge(sem("y_act"), 3 * (t - 1))
                    for c in range(2):
                        mm(PS[:, 2 * (t % 2) + c, :], ident, H[:, t, 512 * c:512 * c + 512], start=True, stop=False)

            pe.wait_ge(sem("wq_in"), 16)
            pe.wait_ge(sem("keys_in"), 16)
            normed(0)
            for half in range(2):
                for c in range(8):
                    query(0, 8 * half + c)
                for b in range(2):
                    score(0, 2 * half + b)
            steps(pe, body)


def kernel(**inputs):
    import concourse.bacc as bacc
    from concourse.bass_utils import run_bass_kernel_spmd as run
    nc = bacc.Bacc("TRN2", target_bir_lowering=False, num_devices=1)
    laid_out = {name: inputs.get(name) for name in NAMES}
    laid_out["positions"] = inputs["positions"].reshape(T, P).T
    laid_out["sub_keys"] = np.transpose(inputs["peer_sub_keys"][0].reshape(2 * PH, NK, P), (2, 0, 1))
    columns = [inputs[n].reshape(-1, P) for n in ("conv_w", "ln1_w", "q_a_norm_w", "kv_a_norm_w", "gdn_norm_w")]
    laid_out["columns"] = np.concatenate(columns).T
    laid_out["consts"] = shape_constants()
    arrays, args = {}, []
    for name, a in laid_out.items():
        arrays["in_" + name] = a = np.ascontiguousarray(a)
        args.append(nc.dram_tensor("in_" + name, a.shape, mybir.dt.from_np(a.dtype), kind="ExternalInput").ap())
    args.append(nc.dram_tensor("out", OUT_SHAPE, F32, kind="ExternalOutput").ap())
    encoder_block(nc, *args)
    return run(nc, [arrays], core_ids=[0]).results[0]["out"]


NAMES = ["x", "positions", "w_in", "w_q_up", "w_kv_up", "a_log_f", "dt_bias_f", "a_log_b", "dt_bias_b", "w_out",
         "ln2_w", "peer_wq", "sub_keys", "peer_u", "peer_v", "final_norm_w"]
OUT_SHAPE = (1, S, D)
```

```python
import math
import numpy as np
import concourse.bass as bass
from concourse import mybir
from contextlib import ExitStack

F32 = mybir.dt.float32
I32 = mybir.dt.int32
U32 = mybir.dt.uint32
ALU = mybir.AluOpType
ACT = mybir.ActivationFunctionType
AX = mybir.AxisListType.X

P = 128
D = 1024
S = 512
T = S // P
KD = D // P
NH = 4
NOPE, ROPE, VD = 128, 64, 128
HR = ROPE // 2
QR, KVR = 256, 128
MLA_IN = QR + KVR + ROPE
QKV0 = MLA_IN
CT_N = 12
Z0 = QKV0 + CT_N * P
G0 = Z0 + NH * P
IN_W = G0 + 4 * NH
TAPS = 5
UNITS = NH * T
SLOTS = 5
LEVELS = 7
PH = 8
NK = 128
TOPK = 16
EPS = 1e-6
SCALE = (NOPE + ROPE) ** -0.5
BIG = 1e30
TWO_PI = 2 * math.pi
PI_HI = 6.28125
PI_LO = TWO_PI - PI_HI
PI_F = 3.1415925
MAGIC = 12582912.0
LOWEST = -3.0e38
UN, VN, DN = 8, 4, 8

CONSTS = ["ident", "tri_f", "tri_b", "strict_f", "strict_b", "incl_f", "incl_b"]
CONSTS += [f"off_{d}{l}" for d in "fb" for l in range(LEVELS)]
NCONST = len(CONSTS) * P
CONST_W = NCONST + HR + TOPK


def shape_constants():
    i, j = np.arange(P)[:, None], np.arange(P)[None, :]
    m = {"ident": i == j, "tri_f": i <= j, "tri_b": i >= j}
    m["strict_f"], m["strict_b"] = np.where(j < i, 0, BIG), np.where(j > i, 0, BIG)
    m["incl_f"], m["incl_b"] = np.where(j >= i, 0, BIG), np.where(j <= i, 0, BIG)
    for l in range(LEVELS):
        b = 1 << l
        off = (i // (2 * b) == j // (2 * b)) & ((i // b) % 2 == 1) & ((j // b) % 2 == 0)
        m[f"off_f{l}"], m[f"off_b{l}"] = off, off.T
    out = np.zeros((P, CONST_W), np.float32)
    for n, name in enumerate(CONSTS):
        out[:, n * P:(n + 1) * P] = m[name]
    inv = np.float32(10000.0) ** (-np.arange(0, ROPE, 2, dtype=np.float32) / np.float32(ROPE))
    out[:, NCONST:NCONST + HR] = inv
    out[:, NCONST + HR:] = np.arange(TOPK)
    return out


def opens(h):
    return isinstance(h, int) and h == 0


def over_rows(ap, n):
    return ap.unsqueeze(1).broadcast_to([ap.shape[0], n, ap.shape[1]])


def over_cols(ap, m):
    return ap.unsqueeze(len(ap.shape)).broadcast_to(list(ap.shape) + [m])


class Names:

    def __init__(self, nc, ctx):
        self._nc, self._ctx, self._made = nc, ctx, {}

    def __call__(self, name):
        if name not in self._made:
            self._made[name] = self._ctx.enter_context(self._nc.semaphore(name))
        return self._made[name]


def encoder_block(nc, x, positions, w_in, w_q_up, w_kv_up, a_log_f, dt_bias_f, a_log_b, dt_bias_b, w_out,
                  ln2_w, peer_wq, sub_keys, peer_u, peer_v, final_norm_w, columns, consts, out):
    ctx = ExitStack()
    with ctx:
        sem = Names(nc, ctx)

        def sb(name, shape, dt=F32):
            return ctx.enter_context(nc.sbuf_tensor(name, shape, dt))

        CONST = sb("CONST", [P, CONST_W])
        H = sb("H", [P, T, D])
        R1A = sb("R1A", [P, 16384])
        R1B = sb("R1B", [P, 8192])
        R2 = sb("R2", [P, 16384])
        MIXT = sb("MIXT", [P, KD, S])
        SMALL = sb("SMALL", [P, 1100])
        PS = ctx.enter_context(nc.psum_tensor("PS", [P, 8, 512], F32))

        cmat = {n: CONST[:, k * P:(k + 1) * P] for k, n in enumerate(CONSTS)}
        ident = cmat["ident"]
        inv_freq = CONST[:, NCONST:NCONST + HR]
        n1T = MIXT

        KA = 6
        WA = R1A[:, 0:KA * IN_W].rearrange("p (k n) -> p k n", n=IN_W)
        WB = R1B[:, 0:(KD - KA) * IN_W].rearrange("p (k n) -> p k n", n=IN_W)

        def w_in_at(k, c0, c1):
            return WA[:, k, c0:c1] if k < KA else WB[:, k - KA, c0:c1]

        off = (KD - KA) * IN_W
        WQU = R1B[:, off:off + 2 * 768].rearrange("p (k n) -> p k n", k=2)
        WKU = R1B[:, off + 1536:off + 1536 + 1024]
        XS = R2[:, 0:T * D].rearrange("p (t n) -> p t n", t=T)
        TOK = R2[:, 0:T * CT_N * P].rearrange("p (t c n) -> p t c n", t=T, c=CT_N)
        KQT = R2[:, 6144:10240].rearrange("p (h w s) -> p h w s", h=NH, w=2)
        Z = R2[:, 10240:12288].rearrange("p (t n) -> p t n", t=T)
        MISC = R2[:, 12288:16384]
        MG = MISC[:, 0:T * 464].rearrange("p (t n) -> p t n", t=T)
        RAW = [MISC[:, 1856 + 516 * i:1856 + 516 * (i + 1)] for i in range(2)]
        CV = [MISC[:, 2888 + 512 * i:2888 + 512 * (i + 1)] for i in range(2)]

        at = [0]

        def small(n):
            at[0] += n
            assert at[0] <= 1100, at
            return SMALL[:, at[0] - n:at[0]]

        ONES = small(P)
        COLS = small(72)
        ssq, rstd = small(T), small(T)
        ss2, r2 = small(8 * T), small(8 * T)
        ssm, rm = small(2 * T), small(2 * T)
        BIAS, ALOG = small(8), small(8)
        cos, sin = small(T * HR), small(T * HR)
        mx, nb, rs, rr = small(16), small(16), small(16), small(16)
        gc_ = small(32)
        eg_ = small(32)
        beta = small(32)
        gg = small(32)
        beg = small(32)
        skd = [small(4), small(4)]
        egl = [small(4), small(4)]
        osq, orr = small(16), small(16)
        POS_I, POS_F = small(T).bitcast(I32), small(T)
        G_A, G_NA, G_E, G_B = small(32), small(32), small(32), small(32)
        ANG, ANG_S, ANG_C, TURN = (R1B[:, 7584 + 128 * i:7712 + 128 * i] for i in range(4))
        SQ3 = PS[:, 7, :].rearrange("p (t n) -> p t n", t=T)
        SQA = CV[0]

        conv_col = lambda tap, c: COLS[:, tap * CT_N + c:tap * CT_N + c + 1]
        ln1_col = lambda k: COLS[:, 60 + k:61 + k]
        qa_col = lambda k: COLS[:, 68 + k:69 + k]
        kva_col, gdn_col = COLS[:, 70:71], COLS[:, 71:72]

        wsat = [0]

        def ws(n):
            wsat[0] += n
            assert wsat[0] <= 16384, wsat
            return R1A[:, wsat[0] - n:wsat[0]]

        CQ = ws(T * 384).rearrange("p (t n) -> p t n", t=T)
        CQT = ws(1024).rearrange("p (k s) -> p k s", k=2)
        CKVT = ws(512)
        KPR = ws(T * 128).rearrange("p (t n) -> p t n", t=T)
        KPET = ws(512)
        QNT = ws(2048).rearrange("p (h s) -> p h s", h=NH)
        KNT = ws(2048).rearrange("p (h s) -> p h s", h=NH)
        QPQPR = ws(2 * T * 256)
        QP = QPQPR[:, 0:1024].rearrange("p (t n) -> p t n", t=T)
        QPR = QPQPR[:, 1024:2048].rearrange("p (t n) -> p t n", t=T)
        QPET = ws(1024).rearrange("p (k s) -> p k s", k=2)
        VT = ws(2048).rearrange("p (t n) -> p t n", t=T)
        PR = [ws(512) for _ in range(2)]
        PT0 = ws(2048)
        PTs = [PT0.rearrange("p (k s) -> p k s", k=T),
               QPQPR.rearrange("p (k s) -> p k s", k=T)]
        ROT = [PT0[:, 0:128], PT0[:, 128:256]]

        gat = [0]

        def gw(n):
            gat[0] += n
            assert gat[0] <= 8192, gat
            return R1B[:, gat[0] - n:gat[0]]

        h4 = lambda ap: ap.rearrange("p (h n) -> p h n", h=NH)
        A = [gw(1024) for _ in range(2)]
        DIFF = [gw(512) for _ in range(2)]
        LO = [gw(512) for _ in range(2)]
        TM = [gw(512) for _ in range(2)]
        XM = [gw(512) for _ in range(2)]
        EG = [gw(512) for _ in range(2)]
        KBG = [MISC[:, 1856 + 512 * i:2368 + 512 * i] for i in range(2)]
        KDC = [MISC[:, 2880 + 512 * i:3392 + 512 * i] for i in range(2)]
        VB = [gw(512) for _ in range(2)]
        ST = [MISC[:, 512 * i:512 * (i + 1)] for i in range(2)]
        O = TOK[:, :, 0:NH, :]

        block = ctx.enter_context(nc.Block())

        dirs = "fb"
        chunk_of = lambda d, s: s if d == 0 else T - 1 - s
        last_of = (P - 1, 0)
        tok = lambda t: slice(t * P, (t + 1) * P)

        @block.sync
        def _(sp):
            sp.dma_start(ident, consts[:, 0:P]).then_inc(sem("cols_in"), 16)
            sp.dma_start(COLS, columns).then_inc(sem("cols_in"), 16)
            for t in range(T):
                sp.dma_start(H[:, t, :], x[0, tok(t), :]).then_inc(sem(f"x_in{t}"), 16)
            sp.dma_start(POS_I, positions).then_inc(sem("pos_in"), 16)
            sp.dma_start(CONST[:, NCONST:], consts[:, NCONST:]).then_inc(sem("pos_in"), 16)
            for g in range(4):
                c0, c1 = QKV0 + g * 3 * P, QKV0 + (g + 1) * 3 * P
                src = w_in[0].rearrange("(k p) n -> p k n", p=P)
                sp.dma_start(WA[:, :, c0:c1], src[:, 0:KA, c0:c1]).then_inc(sem(f"w_qkv{g}_in"), 16)
                sp.dma_start(WB[:, :, c0:c1], src[:, KA:KD, c0:c1]).then_inc(sem(f"w_qkv{g}_in"), 16)
            for c0, c1 in ((0, MLA_IN), (Z0, IN_W)):
                sp.dma_start(WA[:, :, c0:c1], src[:, 0:KA, c0:c1]).then_inc(sem("w_rest_in"), 16)
                sp.dma_start(WB[:, :, c0:c1], src[:, KA:KD, c0:c1]).then_inc(sem("w_rest_in"), 16)
            sp.dma_start(WQU, w_q_up[0].rearrange("(k p) n -> p k n", p=P)).then_inc(sem("w_up_in"), 16)
            sp.dma_start(WKU, w_kv_up[0]).then_inc(sem("w_up_in"), 16)
            sp.dma_start(CONST[:, P:NCONST], consts[:, P:NCONST]).then_inc(sem("masks_in"), 16)

        @block.gpsimd
        def _(pool):
            for n, (src, dst) in enumerate(((dt_bias_f, BIAS[:, 0:4]), (dt_bias_b, BIAS[:, 4:8]),
                                            (a_log_f, ALOG[:, 0:4]), (a_log_b, ALOG[:, 4:8]))):
                pool.dma_start(dst, src[0].partition_broadcast(P)).then_inc(sem("gate_rows_in"), 16)
            nc.gpsimd.memset(ONES, 1.0).then_inc(sem("ones"), 1)

            def rotate(src1, src2, dst1, dst2, c, s, a, b, name, wait, n):
                pool.wait_ge(*wait)
                if n:
                    pool.wait_ge(sem(name), 6 * n)
                steps = [(a, src1, c, ALU.mult), (b, src2, s, ALU.mult), (dst1, a, b, ALU.subtract),
                         (a, src2, c, ALU.mult), (b, src1, s, ALU.mult), (dst2, a, b, ALU.add)]
                for k, (o, i0, i1, op) in enumerate(steps):
                    if k in (2, 3, 5):
                        pool.wait_ge(sem(name), 6 * n + k)
                    nc.gpsimd.tensor_tensor(o, i0, i1, op).then_inc(sem(name), 1)

            pool.wait_ge(sem("rotary_sin"), 2)
            ra, rb = (r[:, 0:128] for r in ROT)
            v3 = lambda ap: ap.rearrange("p (t n) -> p t n", n=HR)
            rotate(MG[:, :, 384:416], MG[:, :, 416:448], KPR[:, :, 0:HR], KPR[:, :, HR:ROPE],
                   v3(cos), v3(sin), v3(ra), v3(rb), "k_rotated", (sem("mg_ready"), T), 0)
            pool.wait_ge(sem("k_rotated"), 6)
            nc.gpsimd.tensor_copy(KPR[:, :, ROPE:2 * ROPE], KPR[:, :, 0:ROPE]).then_inc(sem("k_rotated"), 1)
            pool.wait_ge(sem("k_rotated"), 7)
            for t in range(T):
                q3 = QP[:, t, :].rearrange("p (h n) -> p h n", n=ROPE)
                o3 = QPR[:, t, :].rearrange("p (h n) -> p h n", n=ROPE)
                ct, st = (over_rows(m[:, t * HR:(t + 1) * HR], NH) for m in (cos, sin))
                rotate(q3[:, :, 0:HR], q3[:, :, HR:], o3[:, :, 0:HR], o3[:, :, HR:], ct, st,
                       v3(ra), v3(rb), "q_rotated", (sem("qp_ready"), 2 * t + 1), t)

            def factor(d, s, k):
                t, D_ = chunk_of(d, s), dirs[d]
                bs = slice((d * T + t) * NH, (d * T + t + 1) * NH)
                dst, a, b = ((VB[d], TOK[:, t, 8:12, :], over_cols(beta[:, bs], P)),
                             (KBG[d], TOK[:, t, 4:8, :], over_cols(beg[:, bs], P)),
                             (KDC[d], TOK[:, t, 4:8, :], over_cols(skd[d], P)),
                             (EG[d], KQT[:, :, 1, tok(t)], h4(EG[d])))[k]
                if k == 0:
                    pool.wait_ge(sem("eg_row" + D_), 2 * s + 2)
                    pool.wait_ge(sem("egl" + D_), s + 1)
                    pool.wait_ge(sem("beta_eg"), 1)
                nc.gpsimd.tensor_tensor(h4(dst), a, b, ALU.mult).then_inc(sem("scaled" + D_), 1)

            for s in range(T):
                for d in range(2):
                    D_ = dirs[d]
                    pool.wait_ge(sem("exponents" + D_), s + 1)
                    if s:
                        pool.wait_ge(sem("o_mm" + D_), s)
                        pool.wait_ge(sem("state" + D_), s)
                    nc.gpsimd.tensor_tensor(h4(A[d][:, 0:512]), h4(DIFF[d]), over_rows(cmat["strict_" + D_], NH),
                                            ALU.add).then_inc(sem("masked" + D_), 1)
                    nc.gpsimd.tensor_tensor(h4(A[d][:, 512:1024]), over_rows(cmat["incl_" + D_], NH), h4(DIFF[d]),
                                            ALU.subtract).then_inc(sem("masked" + D_), 1)
                for l in range(LEVELS):
                    for d in range(2):
                        D_ = dirs[d]
                        pool.wait_ge(sem("lower" + D_), s + 1)
                        if l == 1:
                            pool.wait_ge(sem("x_init" + D_), 2 * s + 2)
                        elif l > 1:
                            pool.wait_ge(sem("n_mm" + D_), s * 6 + l - 1)
                        elif s:
                            pool.wait_ge(sem("n_mm" + D_), s * 6)
                        nc.gpsimd.tensor_tensor(h4(LO[d]), h4(A[d][:, 0:512]), over_rows(cmat[f"off_{D_}{l}"], NH),
                                                ALU.mult).then_inc(sem("level" + D_), 1)
                    if 1 <= l <= 4:
                        factor(0, s, l - 1)
                        factor(1, s, l - 1)

        @block.scalar
        def _(act):
            def act_(out, in_, f, name, **kw):
                return nc.scalar.activation(out, in_, f, **kw).then_inc(sem(name), 1)

            for t in range(T):
                act.wait_ge(sem(f"x_in{t}"), 16)
                act_(XS[:, t, :], H[:, t, :], ACT.Square, "x_squares", accum_out=ssq[:, t:t + 1])
            act.wait_ge(sem("mean_squares"), 1)
            act_(rstd, ssq, ACT.Sqrt, "roots")
            act.wait_ge(sem("cols_in"), 32)
            for k in range(1, KD, 2):
                act.wait_ge(sem("n1t_mm"), k + 1)
                act_(n1T[:, k, :], PS[:, k, :], ACT.Copy, "n1t", scale=ln1_col(k))

            def raw(c):
                act.wait_ge(sem("qkv_mm"), c + 1)
                if c >= 2:
                    act.wait_ge(sem("conv"), c - 1)
                act_(RAW[c % 2][:, 2:514], PS[:, c % 2, :], ACT.Copy, "raw")

            def silu(c):
                act.wait_ge(sem("conv"), c + 1)
                act_(CV[c % 2], CV[c % 2], ACT.Silu, "silu")

            def tok_copy(c):
                act.wait_ge(sem("conv_tp"), c + 1)
                act_(TOK[:, :, c, :], PS[:, 2 + c % 2, :].rearrange("p (t n) -> p t n", t=T), ACT.Copy, "tok")

            act.wait_ge(sem("raw_pads"), 4)
            act.wait_ge(sem("xs"), T)
            raw(0)
            for c in range(CT_N):
                if c + 1 < CT_N:
                    raw(c + 1)
                silu(c)
                if c >= 1:
                    tok_copy(c - 1)
            tok_copy(CT_N - 1)
            for t in range(T):
                act.wait_ge(sem("z_mm"), t + 1)
                act_(Z[:, t, :], PS[:, 6 + t % 2, :], ACT.Silu, "z")
            act.wait_ge(sem("mean_squares"), 2)
            act_(r2, ss2, ACT.Sqrt, "roots")
            act.wait_ge(sem("mean_squares"), 3)
            act_(rm, ssm, ACT.Sqrt, "roots")
            act.wait_ge(sem("rotary_args"), 1)
            act_(sin, ANG_S, ACT.Sin, "rotary_sin")
            act_(cos, ANG_C, ACT.Sin, "rotary_sin")

            act.wait_ge(sem("gate_args"), 1)
            act_(G_E, G_NA, ACT.Exp, "gate_exp", scale=-1.0)
            act.wait_ge(sem("gate_exp"), 1)
            act_(G_E, G_E, ACT.Ln, "gate_exp", bias=1.0)
            act_(G_B, G_B, ACT.Exp, "gate_exp", scale=-1.0)
            act.wait_ge(sem("gate_rows_in"), 64)
            act_(ALOG, ALOG, ACT.Exp, "gate_exp")

            for c in range(1, 8, 2):
                act.wait_ge(sem("kqt_mm"), c + 1)
                act_(KQT[:, c // 2, c % 2, :], PS[:, c, :], ACT.Copy, "kqt")
            for h in range(NH):
                act.wait_ge(sem("nope_mm"), 2 * h + 1)
                act_(QNT[:, h, :], PS[:, 4 + h % 2, :], ACT.Copy, "nope")
                act.wait_ge(sem("nope_mm"), 2 * h + 2)
                act_(KNT[:, h, :], PS[:, 6 + h % 2, :], ACT.Copy, "nope")

            def attend(q):
                n = q - 2
                if 0 <= n < UNITS:
                    h, qt = divmod(n, T)
                    act.wait_ge(sem("p_tp"), n + 1)
                    if qt == 0 and h >= 2:
                        act.wait_ge(sem("pv_mm"), h - 1)
                    act_(PTs[h % 2][:, :, tok(qt)], PS[:, 7, :].rearrange("p (k q) -> p k q", k=T), ACT.Copy, "pt")
                if q < UNITS:
                    act.wait_ge(sem("row_max"), q + 1)
                    act_(PR[q % 2], PS[:, 6, :], ACT.Exp, "p_exp", bias=nb[:, q:q + 1], scale=SCALE,
                         accum_out=rs[:, q:q + 1])

            act.wait_ge(sem("g_cum"), 2)
            act_(eg_, gc_, ACT.Exp, "eg")
            for s in range(T):
                for d in range(2):
                    D_, b = dirs[d], 3 * d
                    act.wait_ge(sem("g_rows" + D_), s + 1)
                    act.wait_ge(sem("exponents" + D_), s + 1)
                    if s:
                        act.wait_ge(sem("o_mm" + D_), s)
                        act.wait_ge(sem("state" + D_), s)
                    act_(EG[d], PS[:, b, :], ACT.Exp, "eg_row" + D_)
                    act_(skd[d], skd[d], ACT.Exp, "eg_row" + D_)
                for d in range(2):
                    D_ = dirs[d]
                    act.wait_ge(sem("masked" + D_), 2 * s + 2)
                    act_(A[d], A[d], ACT.Exp, "decay" + D_, scale=-1.0)
                attend(SLOTS * s)
                for l in range(1, LEVELS):
                    for d in range(2):
                        D_, b = dirs[d], 3 * d
                        act.wait_ge(sem("n_mm" + D_), s * 6 + l)
                        act_(DIFF[d], PS[:, b + 1, :], ACT.Copy, "n" + D_)
                    if l < SLOTS:
                        attend(SLOTS * s + l)
                for d in range(2):
                    D_, b = dirs[d], 3 * d
                    act.wait_ge(sem("w_mm" + D_), s + 1)
                    act_(TM[d], PS[:, b + 1, :], ACT.Copy, "w" + D_, scale=-1.0)
                for d in range(2):
                    D_, b = dirs[d], 3 * d
                    act.wait_ge(sem("vn_mm" + D_), s + 1)
                    act_(KBG[d], PS[:, b + 2, :], ACT.Copy, "vn" + D_)
            act.wait_ge(sem("mean_squares"), 4)
            act_(orr, osq, ACT.Sqrt, "roots")

        @block.vector
        def _(dve):
            v = nc.vector
            chain = [0]

            def mark(ins):
                chain[0] += 1
                ins.then_inc(sem("dve_chain"), 1)

            def link(ins):
                mark(ins)
                dve.wait_ge(sem("dve_chain"), chain[0])

            for r in RAW:
                v.memset(r[:, 0:2], 0.0).then_inc(sem("raw_pads"), 1)
                v.memset(r[:, 514:516], 0.0).then_inc(sem("raw_pads"), 1)
            dve.wait_ge(sem("cols_in"), 32)
            dve.wait_ge(sem("x_squares"), T)
            v.tensor_scalar(ssq, ssq, 1.0 / D, EPS, ALU.mult, ALU.add).then_inc(sem("mean_squares"), 1)
            dve.wait_ge(sem("roots"), 1)
            link(v.reciprocal(rstd, rstd))
            for t in range(T):
                v.tensor_scalar(XS[:, t, :], H[:, t, :], rstd[:, t:t + 1], None, ALU.mult).then_inc(sem("xs"), 1)
            for k in range(0, KD, 2):
                dve.wait_ge(sem("n1t_mm"), k + 1)
                v.tensor_scalar(n1T[:, k, :], PS[:, k, :], ln1_col(k), None, ALU.mult).then_inc(sem("n1t"), 1)

            dve.wait_ge(sem("pos_in"), 32)
            link(v.tensor_copy(POS_F, POS_I))
            a3 = lambda ap: ap.rearrange("p (t n) -> p t n", n=HR)
            link(v.tensor_tensor(a3(ANG), over_rows(inv_freq, T), over_cols(POS_F, HR), ALU.mult))
            for dst, shift in ((ANG_S, 0.0), (ANG_C, 0.25)):
                link(v.tensor_scalar(TURN, ANG, 1.0 / TWO_PI, shift, ALU.mult, ALU.add))
                link(v.tensor_scalar(TURN, TURN, MAGIC, None, ALU.add))
                link(v.tensor_scalar(TURN, TURN, -MAGIC, None, ALU.add))
                link(v.scalar_tensor_tensor(out=dst, in0=TURN, scalar=-PI_HI, in1=ANG, op0=ALU.mult, op1=ALU.add))
                link(v.scalar_tensor_tensor(out=dst, in0=TURN, scalar=-PI_LO, in1=dst, op0=ALU.mult, op1=ALU.add))
                if shift:
                    link(v.tensor_scalar(dst, dst, math.pi / 2, None, ALU.add))
                ins = v.tensor_scalar(dst, dst, PI_F, -PI_F, ALU.min, ALU.max)
                if shift:
                    ins.then_inc(sem("rotary_args"), 1)
                else:
                    link(ins)

            def conv(c):
                dve.wait_ge(sem("raw"), c + 1)
                if c >= 2:
                    dve.wait_ge(sem("conv_tp"), c - 1)
                r = RAW[c % 2]
                link(v.tensor_scalar(CV[c % 2], r[:, 0:512], conv_col(0, c), None, ALU.mult))
                for tap in range(1, TAPS):
                    ins = v.scalar_tensor_tensor(out=CV[c % 2], in0=r[:, tap:tap + 512], scalar=conv_col(tap, c),
                                                 in1=CV[c % 2], op0=ALU.mult, op1=ALU.add)
                    if tap < TAPS - 1:
                        link(ins)
                    else:
                        ins.then_inc(sem("conv"), 1)

            def qk_sum(c):
                dve.wait_ge(sem("tok"), c + 1)
                link(v.tensor_tensor(SQ3, TOK[:, :, c, :], TOK[:, :, c, :], ALU.mult))
                link(v.tensor_reduce(ss2[:, c * T:(c + 1) * T], SQ3, AX, ALU.add))

            for c in range(CT_N):
                conv(c)
                if 2 <= c < 10:
                    qk_sum(c - 2)
            v.tensor_scalar(ss2, ss2, EPS, None, ALU.add).then_inc(sem("mean_squares"), 1)
            for t in range(T):
                dve.wait_ge(sem("mg_mm"), t + 1)
                v.tensor_copy(MG[:, t, :], PS[:, 4 + t % 2, 0:464]).then_inc(sem("mg_ready"), 1)
            dve.wait_ge(sem("mg_ready"), T)
            for t in range(T):
                for k, (a, b) in enumerate(((0, QR), (QR, QR + KVR))):
                    ins = v.tensor_tensor_reduce(out=SQA[:, a:b], in0=MG[:, t, a:b], in1=MG[:, t, a:b], scale=1.0 / (b - a),
                                                 scalar=EPS, op0=ALU.mult, op1=ALU.add,
                                                 accum_out=ssm[:, 2 * t + k:2 * t + k + 1])
                    if t == T - 1 and k == 1:
                        ins.then_inc(sem("mean_squares"), 1)
                    elif k:
                        link(ins)
            dve.wait_ge(sem("gate_rows_in"), 64)
            mg4 = MG[:, :, 448:464].rearrange("p t (d w h) -> p d t w h", d=2, w=2)
            for d in range(2):
                o3 = lambda ap: ap[:, 16 * d:16 * d + 16].rearrange("p (t h) -> p t h", t=T)
                mark(v.tensor_tensor(o3(G_A), mg4[:, d, :, 0, :], over_rows(BIAS[:, 4 * d:4 * d + 4], T), ALU.add))
                link(v.tensor_copy(o3(G_B), mg4[:, d, :, 1, :]))
            v.scalar_tensor_tensor(out=G_NA, in0=G_A, scalar=-1.0, in1=G_A, op0=ALU.mult, op1=ALU.max) \
                .then_inc(sem("gate_args"), 1)
            dve.wait_ge(sem("roots"), 2)
            link(v.reciprocal(r2, r2))
            link(v.tensor_scalar(r2[:, 0:NH * T], r2[:, 0:NH * T], float(P) ** -0.5, None, ALU.mult))
            r2v = r2.rearrange("p (c t) -> p t c", t=T)
            for t in range(T):
                v.tensor_tensor(TOK[:, t, 0:8, :], TOK[:, t, 0:8, :], over_cols(r2v[:, t, :], P), ALU.mult) \
                    .then_inc(sem("qk_unit"), 1)
            dve.wait_ge(sem("roots"), 3)
            link(v.reciprocal(rm, rm))
            dve.wait_ge(sem("z_mm"), T)
            for t in range(T):
                v.tensor_scalar(CQ[:, t, 0:QR], MG[:, t, 0:QR], rm[:, 2 * t:2 * t + 1], None, ALU.mult) \
                    .then_inc(sem("latents"), 1)
                v.tensor_scalar(CQ[:, t, QR:384], MG[:, t, QR:384], rm[:, 2 * t + 1:2 * t + 2], None, ALU.mult) \
                    .then_inc(sem("latents"), 1)
            for c in range(0, 8, 2):
                dve.wait_ge(sem("kqt_mm"), c + 1)
                v.tensor_copy(KQT[:, c // 2, c % 2, :], PS[:, c, :]).then_inc(sem("kqt"), 1)
            for k in range(3):
                dve.wait_ge(sem("latents_tp"), k + 1)
                dst, col = (CQT[:, k, :], qa_col(k)) if k < 2 else (CKVT, kva_col)
                v.tensor_scalar(dst, PS[:, k, :], col, None, ALU.mult).then_inc(sem("latents_t"), 1)
            for t in range(T):
                dve.wait_ge(sem("qp_mm"), 2 * t + 1)
                v.tensor_copy(QP[:, t, :], PS[:, t % 2, 0:256]).then_inc(sem("qp_ready"), 1)
                dve.wait_ge(sem("qp_mm"), 2 * t + 2)
                v.tensor_copy(VT[:, t, :], PS[:, 2 + t % 2, :]).then_inc(sem("qp_ready"), 1)
            dve.wait_ge(sem("pe_tp"), 1)
            v.tensor_copy(KPET, PS[:, 0, :]).then_inc(sem("pe_t"), 1)
            for pr in range(2):
                dve.wait_ge(sem("pe_tp"), pr + 2)
                v.tensor_copy(QPET[:, pr, :], PS[:, 1 + pr, :]).then_inc(sem("pe_t"), 1)

            dve.wait_ge(sem("masks_in"), 16)
            dve.wait_ge(sem("gate_exp"), 4)
            link(v.scalar_tensor_tensor(out=gg, in0=G_A, scalar=0.0, in1=G_E, op0=ALU.max, op1=ALU.add))
            link(v.tensor_scalar(ALOG, ALOG, -1.0, None, ALU.mult))
            for d in range(2):
                o3 = gg[:, 16 * d:16 * d + 16].rearrange("p (t h) -> p t h", t=T)
                link(v.tensor_tensor(o3, o3, over_rows(ALOG[:, 4 * d:4 * d + 4], T), ALU.mult))
            v.tensor_scalar(beta, G_B, 1.0, None, ALU.add).then_inc(sem("g_ready"), 1)
            dve.wait_ge(sem("g_ready"), 1)
            link(v.reciprocal(beta, beta))

            def attend(q):
                n = q - 1
                if 0 <= n < UNITS:
                    dve.wait_ge(sem("p_exp"), n + 1)
                    link(v.reciprocal(rr[:, n:n + 1], rs[:, n:n + 1]))
                    v.tensor_scalar(PR[n % 2], PR[n % 2], rr[:, n:n + 1], None, ALU.mult).then_inc(sem("p_norm"), 1)
                if q >= T + 2 and (q - 2) % T == 0:
                    h = (q - 2) // T - 1
                    dve.wait_ge(sem("pv_mm"), h + 1)
                    v.tensor_copy(MIXT[:, h, :], PS[:, 7, :]).then_inc(sem("mla_out"), 1)
                if q < UNITS:
                    dve.wait_ge(sem("s_mm"), q + 1)
                    link(v.reduce_max(mx[:, q:q + 1], PS[:, 6, :], AX))
                    v.tensor_scalar(nb[:, q:q + 1], mx[:, q:q + 1], -SCALE, None, ALU.mult).then_inc(sem("row_max"), 1)

            for d in range(2):
                dve.wait_ge(sem("gc_mm"), d + 1)
                v.tensor_copy(gc_[:, 16 * d:16 * d + 16], PS[:, 3 * d, 0:16]).then_inc(sem("g_cum"), 1)
            dve.wait_ge(sem("eg"), 1)
            v.tensor_tensor(beg, beta, eg_, ALU.mult).then_inc(sem("beta_eg"), 1)
            for s in range(T):
                for d in range(2):
                    D_, t = dirs[d], chunk_of(d, s)
                    bs = slice((d * T + t) * NH, (d * T + t + 1) * NH)
                    if s:
                        dve.wait_ge(sem("d_mm" + D_), 6 * s)
                    v.tensor_tensor(h4(DIFF[d]), over_rows(cmat["tri_" + D_], NH), over_cols(gg[:, bs], P),
                                    ALU.mult).then_inc(sem("g_tri" + D_), 1)
                for d in range(2):
                    D_, t, b = dirs[d], chunk_of(d, s), 3 * d
                    bs = slice((d * T + t) * NH, (d * T + t + 1) * NH)
                    dve.wait_ge(sem("g_rows" + D_), s + 1)
                    if s:
                        dve.wait_ge(sem("scaled" + D_), 4 * s)
                    gl = h4(PS[:, b, :])[:, :, last_of[d]]
                    mark(v.tensor_tensor(skd[d], gl, gc_[:, bs], ALU.subtract))
                    v.tensor_tensor(h4(DIFF[d]), h4(PS[:, b, :]), over_cols(gc_[:, bs], P), ALU.subtract) \
                        .then_inc(sem("exponents" + D_), 1)
                for d in range(2):
                    D_ = dirs[d]
                    dve.wait_ge(sem("eg_row" + D_), 2 * s + 2)
                    v.tensor_copy(egl[d], h4(EG[d])[:, :, last_of[d]]).then_inc(sem("egl" + D_), 1)
                attend(SLOTS * s)
                for d in range(2):
                    D_, t, b = dirs[d], chunk_of(d, s), 3 * d
                    dve.wait_ge(sem("decay" + D_), s + 1)
                    dve.wait_ge(sem("kq_mm" + D_), s + 1)
                    kq = PS[:, b + 1:b + 3, :].rearrange("p b (h w n) -> p (b h) w n", h=2, w=2)
                    for h in range(NH):
                        n = (d * T + t) * NH + h
                        ah = A[d][:, h * P:(h + 1) * P]
                        ins = v.scalar_tensor_tensor(out=ah, in0=kq[:, h, 0, :], scalar=beta[:, n:n + 1], in1=ah,
                                                     op0=ALU.mult, op1=ALU.mult)
                        if h < NH - 1:
                            mark(ins)
                    ins.then_inc(sem("lower" + D_), 1)
                    v.tensor_tensor(h4(A[d][:, 512:1024]), kq[:, :, 1, :], h4(A[d][:, 512:1024]), ALU.mult) \
                        .then_inc(sem("attn" + D_), 1)
                for d in range(2):
                    D_, b = dirs[d], 3 * d
                    dve.wait_ge(sem("lo_tp" + D_), s + 1)
                    if s:
                        dve.wait_ge(sem("vn_mm" + D_), s)
                    v.tensor_tensor(h4(TM[d]), over_rows(ident, NH), h4(LO[d]), ALU.subtract) \
                        .then_inc(sem("x_init" + D_), 1)
                    v.tensor_tensor(h4(XM[d]), over_rows(ident, NH), h4(PS[:, b, :]), ALU.subtract) \
                        .then_inc(sem("x_init" + D_), 1)
                for l in range(1, LEVELS):
                    if l < SLOTS:
                        attend(SLOTS * s + l)
                    for d in range(2):
                        D_, b = dirs[d], 3 * d
                        dve.wait_ge(sem("d_mm" + D_), s * 6 + l)
                        if l < LEVELS - 1:
                            mark(v.tensor_tensor(TM[d], TM[d], PS[:, b, :], ALU.subtract))
                        v.tensor_tensor(XM[d], XM[d], PS[:, b + 2, :], ALU.subtract).then_inc(sem("x_up" + D_), 1)
                for d in range(2):
                    D_, t, b = dirs[d], chunk_of(d, s), 3 * d
                    dve.wait_ge(sem("o_mm" + D_), s + 1)
                    o, ps = O[:, t, :, :], h4(PS[:, b + 1, :])
                    if s < T // 2:
                        v.tensor_copy(o, ps).then_inc(sem("o_out"), 1)
                    else:
                        dve.wait_ge(sem("o_out"), 2 * s)
                        v.tensor_tensor(o, o, ps, ALU.add).then_inc(sem("o_out"), 1)
                    if s == 0:
                        v.tensor_copy(ST[d], PS[:, b, :]).then_inc(sem("state" + D_), 1)
                    else:
                        for h in range(NH):
                            sh = ST[d][:, h * P:(h + 1) * P]
                            ins = v.scalar_tensor_tensor(out=sh, in0=sh, scalar=egl[d][:, h:h + 1],
                                                         in1=PS[:, b, h * P:(h + 1) * P], op0=ALU.mult, op1=ALU.add)
                            if h < NH - 1:
                                mark(ins)
                        ins.then_inc(sem("state" + D_), 1)
            dve.wait_ge(sem("o_out"), 2 * T)
            SQO = h4(DIFF[0])
            for t in range(T):
                link(v.tensor_tensor(SQO, O[:, t, :, :], O[:, t, :, :], ALU.mult))
                link(v.tensor_reduce(osq[:, t * NH:(t + 1) * NH], SQO, AX, ALU.add))
            v.tensor_scalar(osq, osq, 1.0 / P, EPS, ALU.mult, ALU.add).then_inc(sem("mean_squares"), 1)
            dve.wait_ge(sem("roots"), 4)
            link(v.reciprocal(orr, orr))
            for t in range(T):
                link(v.tensor_tensor(O[:, t, :, :], O[:, t, :, :], over_cols(orr[:, t * NH:(t + 1) * NH], P), ALU.mult))
                v.tensor_tensor(O[:, t, :, :], O[:, t, :, :], h4(Z[:, t, :]), ALU.mult).then_inc(sem("o_gated"), 1)
            for t in range(T):
                dve.wait_ge(sem("o_tp"), t + 1)
                v.tensor_scalar(MIXT[:, NH:2 * NH, tok(t)], h4(PS[:, t % 2, :]), gdn_col, None, ALU.mult) \
                    .then_inc(sem("gdn_out"), 1)

        @block.tensor
        def _(pe):
            mm = nc.tensor.matmul
            tp = lambda o, i, n=P: nc.tensor.transpose(o, i, ident[0:n, 0:n])
            pe.wait_ge(sem("cols_in"), 32)
            pe.wait_ge(sem("xs"), T)
            for k in range(KD):
                for t in range(T):
                    ins = tp(PS[:, k, tok(t)], XS[:, t, k * P:(k + 1) * P])
                ins.then_inc(sem("n1t_mm"), 1)
            pe.wait_ge(sem("n1t"), KD)

            def conv_tp(c):
                pe.wait_ge(sem("silu"), c + 1)
                if c >= 2:
                    pe.wait_ge(sem("tok"), c - 1)
                for t in range(T):
                    ins = tp(PS[:, 2 + c % 2, tok(t)], CV[c % 2][:, tok(t)])
                ins.then_inc(sem("conv_tp"), 1)

            for c in range(CT_N):
                pe.wait_ge(sem(f"w_qkv{c // 3}_in"), 32)
                if c >= 2:
                    pe.wait_ge(sem("raw"), c - 1)
                for k in range(KD):
                    c0 = QKV0 + c * P
                    ins = mm(PS[:, c % 2, :], w_in_at(k, c0, c0 + P), n1T[:, k, :], start=k == 0, stop=k == KD - 1)
                ins.then_inc(sem("qkv_mm"), 1)
                if c >= 2:
                    conv_tp(c - 2)
            pe.wait_ge(sem("w_rest_in"), 64)
            for t in range(T):
                if t >= 2:
                    pe.wait_ge(sem("mg_ready"), t - 1)
                for k in range(KD):
                    mm(PS[:, 4 + t % 2, 0:448], n1T[:, k, tok(t)], w_in_at(k, 0, MLA_IN), start=k == 0, stop=k == KD - 1)
                for k in range(KD):
                    ins = mm(PS[:, 4 + t % 2, 448:464], n1T[:, k, tok(t)], w_in_at(k, G0, IN_W), start=k == 0, stop=k == KD - 1)
                ins.then_inc(sem("mg_mm"), 1)
                if t < 2:
                    conv_tp(CT_N - 2 + t)
            pe.wait_ge(sem("mean_squares"), 2)
            for t in range(T):
                if t >= 2:
                    pe.wait_ge(sem("z"), t - 1)
                for k in range(KD):
                    ins = mm(PS[:, 6 + t % 2, :], n1T[:, k, tok(t)], w_in_at(k, Z0, G0), start=k == 0, stop=k == KD - 1)
                ins.then_inc(sem("z_mm"), 1)
            pe.wait_ge(sem("qk_unit"), T)
            pe.wait_ge(sem("tok"), CT_N)
            pe.wait_ge(sem("mg_ready"), T)
            for c in range(8):
                h, w = divmod(c, 2)
                if c == 6:
                    pe.wait_ge(sem("z"), T)
                for t in range(T):
                    ins = tp(PS[:, c, tok(t)], TOK[:, t, h + (NH if w == 0 else 0), :])
                ins.then_inc(sem("kqt_mm"), 1)
            pe.wait_ge(sem("latents"), 2 * T)
            pe.wait_ge(sem("kqt"), 2 * NH)
            for k in range(3):
                for t in range(T):
                    ins = tp(PS[:, k, tok(t)], CQ[:, t, k * P:(k + 1) * P])
                ins.then_inc(sem("latents_tp"), 1)
            pe.wait_ge(sem("latents_t"), 3)
            pe.wait_ge(sem("w_up_in"), 32)
            for h in range(NH):
                if h >= 2:
                    pe.wait_ge(sem("nope"), 2 * (h - 1))
                for k in range(2):
                    ins = mm(PS[:, 4 + h % 2, :], WQU[:, k, h * 192:h * 192 + P], CQT[:, k, :], start=k == 0, stop=k == 1)
                ins.then_inc(sem("nope_mm"), 1)
                mm(PS[:, 6 + h % 2, :], WKU[:, h * 256:h * 256 + P], CKVT, start=True, stop=True) \
                    .then_inc(sem("nope_mm"), 1)
            for t in range(T):
                if t >= 2:
                    pe.wait_ge(sem("qp_ready"), 2 * (t - 1))
                for k in range(2):
                    w = WQU[:, k, :].rearrange("p (h n) -> p h n", h=NH)[:, :, NOPE:]
                    ins = mm(PS[:, t % 2, 0:256], CQT[:, k, tok(t)], w, start=k == 0, stop=k == 1)
                ins.then_inc(sem("qp_mm"), 1)
                w = WKU.rearrange("p (h n) -> p h n", h=NH)[:, :, NOPE:]
                mm(PS[:, 2 + t % 2, :], CKVT[:, tok(t)], w, start=True, stop=True).then_inc(sem("qp_mm"), 1)
            pe.wait_ge(sem("qp_ready"), 2 * T)
            pe.wait_ge(sem("k_rotated"), 7)
            for t in range(T):
                ins = tp(PS[:, 0, tok(t)], KPR[:, t, :])
            ins.then_inc(sem("pe_tp"), 1)
            pe.wait_ge(sem("q_rotated"), 6 * T)
            for pr in range(2):
                for t in range(T):
                    ins = tp(PS[:, 1 + pr, tok(t)], QPR[:, t, pr * P:(pr + 1) * P])
                ins.then_inc(sem("pe_tp"), 1)
            pe.wait_ge(sem("pe_t"), 3)
            pe.wait_ge(sem("nope"), 2 * NH)

            def attend(q):
                if q >= T + 2 and (q - 2) % T == 0:
                    h = (q - 2) // T - 1
                    pe.wait_ge(sem("pt"), T * (h + 1))
                    for kt in range(T):
                        ins = mm(PS[:, 7, :], VT[:, kt, h * P:(h + 1) * P], PTs[h % 2][:, kt, :],
                                 start=kt == 0, stop=kt == T - 1)
                    ins.then_inc(sem("pv_mm"), 1)
                if q < UNITS:
                    h, qt = divmod(q, T)
                    if q:
                        pe.wait_ge(sem("p_exp"), q)
                    mm(PS[:, 6, :], QNT[:, h, tok(qt)], KNT[:, h, :], start=True, stop=False)
                    r = slice(64 * (h % 2), 64 * (h % 2) + 64)
                    mm(PS[:, 6, :], QPET[r, h // 2, tok(qt)], KPET[r, :], start=False, stop=True) \
                        .then_inc(sem("s_mm"), 1)
                n = q - 2
                if 0 <= n < UNITS:
                    pe.wait_ge(sem("p_norm"), n + 1)
                    if n:
                        pe.wait_ge(sem("pt"), n)
                    if n >= T and n % T == 0:
                        pe.wait_ge(sem("mla_out"), n // T)
                    for kt in range(T):
                        ins = tp(PS[:, 7, tok(kt)], PR[n % 2][:, tok(kt)])
                    ins.then_inc(sem("p_tp"), 1)

            pe.wait_ge(sem("g_ready"), 1)
            pe.wait_ge(sem("ones"), 1)
            for d in range(2):
                mm(PS[:, 3 * d, 0:16], cmat["tri_" + dirs[d]], gg[:, 16 * d:16 * d + 16], start=True, stop=True) \
                    .then_inc(sem("gc_mm"), 1)
            pe.wait_ge(sem("g_cum"), 2)
            hs = lambda h: slice(h * P, (h + 1) * P)
            for s in range(T):
                for d in range(2):
                    D_, t, b = dirs[d], chunk_of(d, s), 3 * d
                    pe.wait_ge(sem("g_tri" + D_), s + 1)
                    if s:
                        pe.wait_ge(sem("state" + D_), s)
                    mm(PS[:, b, :], ONES, DIFF[d], start=True, stop=True).then_inc(sem("g_rows" + D_), 1)
                    if s:
                        pe.wait_ge(sem("w" + D_), s)
                        pe.wait_ge(sem("vn" + D_), s)
                    for h in range(NH):
                        o = PS[:, b + 1 + h // 2, 256 * (h % 2):256 * (h % 2) + 256]
                        ins = mm(o.rearrange("p (w n) -> p w n", w=2), KQT[:, h, 0, tok(t)], KQT[:, h, :, tok(t)],
                                 start=True, stop=True)
                    ins.then_inc(sem("kq_mm" + D_), 1)
                attend(SLOTS * s)
                for d in range(2):
                    D_, b = dirs[d], 3 * d
                    pe.wait_ge(sem("level" + D_), LEVELS * s + 1)
                    for h in range(NH):
                        ins = tp(PS[:, b, hs(h)], LO[d][:, hs(h)])
                    ins.then_inc(sem("lo_tp" + D_), 1)
                for l in range(1, LEVELS):
                    for d in range(2):
                        D_, b = dirs[d], 3 * d
                        pe.wait_ge(sem("level" + D_), LEVELS * s + l + 1)
                        if l == 1:
                            pe.wait_ge(sem("x_init" + D_), 2 * s + 2)
                            pe.wait_ge(sem("attn" + D_), s + 1)
                        else:
                            pe.wait_ge(sem("x_up" + D_), 6 * s + l - 1)
                        for h in range(NH):
                            ins = mm(PS[:, b + 1, hs(h)], LO[d][:, hs(h)], XM[d][:, hs(h)], start=True, stop=True)
                        ins.then_inc(sem("n_mm" + D_), 1)
                    if l < SLOTS:
                        attend(SLOTS * s + l)
                    for d in range(2):
                        D_, b = dirs[d], 3 * d
                        pe.wait_ge(sem("n" + D_), 6 * s + l)
                        for h in range(NH):
                            ins = mm(PS[:, b + 2, hs(h)], TM[d][:, hs(h)], DIFF[d][:, hs(h)], start=True, stop=True)
                        if l < LEVELS - 1:
                            for h in range(NH):
                                ins = mm(PS[:, b, hs(h)], DIFF[d][:, hs(h)], TM[d][:, hs(h)], start=True, stop=True)
                        ins.then_inc(sem("d_mm" + D_), 1)
                for d in range(2):
                    D_, b = dirs[d], 3 * d
                    pe.wait_ge(sem("scaled" + D_), 4 * s + 4)
                    pe.wait_ge(sem("x_up" + D_), 6 * s + 6)
                    for h in range(NH):
                        ins = mm(PS[:, b + 1, hs(h)], KBG[d][:, hs(h)], XM[d][:, hs(h)], start=True, stop=True)
                    ins.then_inc(sem("w_mm" + D_), 1)
                for d in range(2):
                    D_, b = dirs[d], 3 * d
                    pe.wait_ge(sem("w" + D_), s + 1)
                    for h in range(NH):
                        ins = mm(PS[:, b + 2, hs(h)], XM[d][:, hs(h)], VB[d][:, hs(h)], start=True, stop=s == 0)
                        if s:
                            ins = mm(PS[:, b + 2, hs(h)], TM[d][:, hs(h)], ST[d][:, hs(h)], start=False, stop=True)
                    ins.then_inc(sem("vn_mm" + D_), 1)
                for d in range(2):
                    D_, b = dirs[d], 3 * d
                    pe.wait_ge(sem("vn" + D_), s + 1)
                    for h in range(NH):
                        mm(PS[:, b, hs(h)], KDC[d][:, hs(h)], KBG[d][:, hs(h)], start=True, stop=True)
                    for h in range(NH):
                        if s:
                            mm(PS[:, b + 1, hs(h)], EG[d][:, hs(h)], ST[d][:, hs(h)], start=True, stop=False)
                        ins = mm(PS[:, b + 1, hs(h)], A[d][:, 512 + h * P:512 + (h + 1) * P], KBG[d][:, hs(h)],
                                 start=s == 0, stop=True)
                    ins.then_inc(sem("o_mm" + D_), 1)
            for t in range(T):
                pe.wait_ge(sem("o_gated"), t + 1)
                if t == 0:
                    pe.wait_ge(sem("o_out"), 2 * T)
                    pe.wait_ge(sem("statef"), T)
                if t >= 2:
                    pe.wait_ge(sem("gdn_out"), t - 1)
                for h in range(NH):
                    ins = tp(PS[:, t % 2, hs(h)], O[:, t, h, :])
                ins.then_inc(sem("o_tp"), 1)

        WO = R1A[:, 0:8192].rearrange("p (k n) -> p k n", k=KD)
        WQH = [w.rearrange("p (k n) -> p k n", k=KD // 2) for w in (R1B[:, :], R1A[:, 8192:])]
        N2 = MIXT[:, :, :].rearrange("p k s -> p (k s)").rearrange("p (t n) -> p t n", t=T)
        SKT = CONST[:, P:P + 2 * PH * NK].rearrange("p (c n) -> p c n", n=NK)
        iota = CONST[:, NCONST + HR:]
        UR = [R2[:, D * j:D * (j + 1)] for j in range(UN)]
        VR = [R2[:, D * (UN + j):D * (UN + j + 1)] for j in range(VN)]
        LN2B, FINB, YS = (R2[:, 12288 + D * j:12288 + D * (j + 1)] for j in range(3))
        DG = [R2[:, 15360 + P * j:15360 + P * (j + 1)] for j in range(DN)]
        rat = [0]

        def rw(n):
            rat[0] += n
            assert rat[0] <= 8192, rat
            return R1A[:, rat[0] - n:rat[0]]

        QPT = rw(1024).rearrange("p (c n) -> p c n", n=P)
        N2T = rw(1024).rearrange("p (k n) -> p k n", n=P)
        SCORES = [rw(2048) for _ in range(2)]
        SC, SC2, CAND, CAND2, OH = rw(256), rw(256), rw(256), rw(256), rw(512)
        TOPS, TOPI, TOPIF = rw(32), rw(32).bitcast(U32), rw(32)
        BEST, BESTI, BESTIJ, BESTF, ROWS = rw(16), rw(16).bitcast(U32), rw(32).bitcast(U32), rw(32), rw(32)
        EXPERT, GATE = [rw(TOPK).bitcast(I32) for _ in range(2)], [rw(TOPK) for _ in range(2)]
        UIDX, VIDX = ([rw(TOPK).bitcast(I32) for _ in range(2)] for _ in range(2))
        HID, GEL, WGT = ([rw(TOPK) for _ in range(2)] for _ in range(3))
        n2sq, n2r, gsum = ssq, rstd, [rw(1) for _ in range(2)]
        ysq = [rw(1) for _ in range(2)]

        def steps(eng, body):
            for t in range(T):
                body(t, 0, 0)
                if t == 0:
                    body(t, 1, 1)
                    body(t, 2, 0)
                with eng.Fori(1 if t == 0 else 0, 3, 1) as i:
                    body(t, 2 * i + 1, 1)
                    body(t, 2 * i + 2, 0)
                body(t, PH - 1, 1)
            body(T, 0, 0)

        @block.sync
        def _(sp):
            wq = peer_wq[0].rearrange("(k p) n -> p k n", p=P)
            sp.wait_ge(sem("mla_out"), NH)
            for k in range(0, KD, 4):
                sp.dma_start(WO[:, k:k + 4, :], w_out[0].rearrange("(k p) n -> p k n", p=P)[:, k:k + 4, :]) \
                    .then_inc(sem("wo_in"), 16)
            sp.dma_start(WQH[1], wq[:, KD // 2:, :]).then_inc(sem("wq_in"), 16)
            sp.wait_ge(sem("mean_squares"), 4)
            sp.dma_start(LN2B, ln2_w[0].partition_broadcast(P)).then_inc(sem("norms_in"), 16)
            sp.dma_start(FINB, final_norm_w.partition_broadcast(P)).then_inc(sem("norms_in"), 16)
            sp.dma_start(WQH[0], wq[:, 0:KD // 2, :]).then_inc(sem("wq_in"), 16)
            sp.dma_start(SKT, sub_keys).then_inc(sem("keys_in"), 16)
            for t in range(T):
                sp.wait_ge(sem("y_dve"), 3 * (t + 1))
                sp.dma_start(out[0, tok(t), :], YS).then_inc(sem("y_out"), 16)
            sp.wait_ge(sem("y_out"), 16 * T)

        @block.gpsimd
        def _(pool):
            def hold(name, value):
                pool.wait_ge(sem(name), value)
                pool.sem_inc(sem("gather_may_go"), 1)

            def body(t, h, par):
                first, last = (t == 0 and opens(h)), t == T
                gu = PH * t + h
                gv = gu - 1
                if not last:
                    hold("experts", gu + 1)
                    if not first:
                        hold("u_dot", TOPK * gu - 8)
                    nc.gpsimd.tensor_copy(UIDX[par], EXPERT[par]).then_inc(sem("u_idx"), 1)
                if not first:
                    nc.gpsimd.tensor_copy(VIDX[1 - par], UIDX[1 - par]).then_inc(sem("v_idx"), 1)
                    hold("v_idx", gv + 1)
                if not last:
                    hold("u_idx", gu + 1)
                for s in range(TOPK):
                    if not last:
                        if not first or s >= UN:
                            hold("u_dot", TOPK * gu + s + 1 - UN)
                        pool.indirect_dma_start(UR[s % UN], None, peer_u[0],
                                                bass.IndirectOffsetOnAxis(ap=UIDX[par][:, s:s + 1], axis=0)) \
                            .then_inc(sem(f"u_row{s % UN}"), 16)
                    if not first:
                        if not isinstance(gv, int) or TOPK * gv + s + 1 > VN:
                            hold("v_sum", TOPK * gv + s + 1 - VN)
                        pool.indirect_dma_start(VR[s % VN], None, peer_v[0],
                                                bass.IndirectOffsetOnAxis(ap=VIDX[1 - par][:, s:s + 1], axis=0)) \
                            .then_inc(sem(f"v_row{s % VN}"), 16)

            pool.wait_ge(sem("o_tp"), T)
            pool.wait_ge(sem("gdn_out"), T)
            steps(pool, body)

        @block.scalar
        def _(act):
            def act_(out, in_, f, name, **kw):
                return nc.scalar.activation(out, in_, f, **kw).then_inc(sem(name), 1)

            for t in range(T):
                act.wait_ge(sem("h_sum"), t + 1)
                if t:
                    act.wait_ge(sem("n2_squares"), t)
                act_(YS, H[:, t, :], ACT.Square, "n2_squares", accum_out=n2sq[:, t:t + 1])
                act.wait_ge(sem("mean_squares"), 5 + t)
                act_(n2r[:, t:t + 1], n2sq[:, t:t + 1], ACT.Sqrt, "roots")

            def queries(t, b):
                act.wait_ge(sem("q_mm"), 4 * t + b + 1)
                if 4 * t + b >= 2:
                    act.wait_ge(sem("score_mm"), 4 * t + b - 1)
                act_(QPT[:, 4 * (b % 2):4 * (b % 2) + 4, :], h4(PS[:, 6 + b % 2, :]), ACT.Copy, "q")

            def scores(t, b):
                act.wait_ge(sem("score_mm"), 4 * t + b + 1)
                if t >= 2:
                    act.wait_ge(sem("experts"), PH * (t - 1))
                act_(SCORES[t % 2][:, 512 * b:512 * (b + 1)], PS[:, 4 + b % 2, :], ACT.Copy, "scores")

            def normed(t):
                act.wait_ge(sem("n2t_mm"), t + 1)
                act_(N2T.rearrange("p k n -> p (k n)"), PS[:, 4:6, :].rearrange("p b n -> p (b n)"), ACT.Copy, "n2t")

            def front_after(t, half, s):
                if half == 0 and s == 0:
                    normed(t)
                if s in (4, 8):
                    queries(t, 2 * half + (s == 8))
                if s in (12, 14):
                    scores(t, 2 * half + (s == 14))

            def body(t, h, par):
                first, last = (t == 0 and opens(h)), t == T
                gu = PH * t + h
                gv = gu - 1
                half = 0 if opens(h) else 1 if isinstance(h, int) and h == PH - 1 else None
                if t >= T - 1:
                    half = None
                if not first:
                    act.wait_ge(sem("u_dot"), TOPK * (gv + 1))
                    act_(GEL[1 - par], HID[1 - par], ACT.Gelu, "gelu")
                    act.wait_ge(sem("weight"), gv + 1)
                for s in range(TOPK):
                    if not first:
                        if not isinstance(gv, int) or TOPK * gv + s + 1 > DN:
                            act.wait_ge(sem("v_sum"), TOPK * gv + s + 1 - DN)
                        act_(DG[s % DN], ident, ACT.Copy, "diag", scale=WGT[1 - par][:, s:s + 1])
                    if half is not None:
                        front_after(t + 1, half, s)
                if not (t == T or (t == T - 1 and isinstance(h, int) and h == PH - 1)):
                    act.wait_ge(sem("gate_arg"), gu + 2)
                    act_(GATE[1 - par], GATE[1 - par], ACT.Exp, "gate_exps", accum_out=gsum[1 - par])
                if opens(h) and t:
                    b = 2 * ((t - 1) % 2)
                    act.wait_ge(sem("v_sum"), TOPK * PH * t)
                    if t >= 2:
                        act.wait_ge(sem("y_out"), 16 * (t - 1))
                    act_(YS, PS[:, b:b + 2, :].rearrange("p b n -> p (b n)"), ACT.Square, "y_act", accum_out=ysq[0])
                    act.wait_ge(sem("y_dve"), 3 * t - 2)
                    act_(ysq[1], ysq[0], ACT.Sqrt, "y_act")
                    act.wait_ge(sem("y_dve"), 3 * t - 1)
                    act_(YS, PS[:, b:b + 2, :].rearrange("p b n -> p (b n)"), ACT.Copy, "y_act", scale=ysq[1])

            normed(0)
            for b in range(2):
                queries(0, b)
            for b in range(2):
                scores(0, b)
            for b in range(2, 4):
                queries(0, b)
            for b in range(2, 4):
                scores(0, b)
            act.wait_ge(sem("gate_arg"), 1)
            act_(GATE[0], GATE[0], ACT.Exp, "gate_exps", accum_out=gsum[0])
            steps(act, body)

        @block.vector
        def _(dve):
            v = nc.vector
            def residual(t):
                dve.wait_ge(sem("out_mm"), t + 1)
                b = 2 * (t % 2)
                v.tensor_tensor(H[:, t, :], H[:, t, :], PS[:, b:b + 2, :].rearrange("p b n -> p (b n)"), ALU.add) \
                    .then_inc(sem("h_sum"), 1)

            def rms(t):
                c = n2sq[:, t:t + 1]
                dve.wait_ge(sem("n2_squares"), t + 1)
                v.tensor_scalar(c, c, 1.0 / D, EPS, ALU.mult, ALU.add).then_inc(sem("mean_squares"), 1)
                dve.wait_ge(sem("roots"), 5 + t)
                v.reciprocal(n2r[:, t:t + 1], n2r[:, t:t + 1])
                v.drain()

            def normed(t):
                v.scalar_tensor_tensor(out=N2[:, t, :], in0=H[:, t, :], scalar=n2r[:, t:t + 1], in1=LN2B,
                                       op0=ALU.mult, op1=ALU.mult).then_inc(sem("n2"), 1)

            for t in range(T - 1):
                residual(t)
                rms(t)
            dve.wait_ge(sem("norms_in"), 32)
            dve.wait_ge(sem("out_mm"), T)
            normed(0)
            residual(T - 1)
            for t in range(1, T - 1):
                normed(t)
            rms(T - 1)
            normed(T - 1)

            def top_experts(t, h, par):
                v.tensor_copy(SC, SCORES[t % 2][:, bass.ds(256 * h, 256)])
                v.drain()
                half = lambda ap, w: ap[:, NK * w:NK * (w + 1)]
                s8 = lambda ap, w, r: ap[:, TOPK * w + 8 * r:TOPK * w + 8 * r + 8]
                for w in range(2):
                    v.max(s8(TOPS, w, 0), half(SC, w))
                v.drain()
                for w in range(2):
                    v.match_replace(half(SC2, w), s8(TOPS, w, 0), half(SC, w), LOWEST)
                for w in range(2):
                    v.max_index(s8(TOPI, w, 0), s8(TOPS, w, 0), half(SC, w))
                v.drain()
                for w in range(2):
                    v.max(s8(TOPS, w, 1), half(SC2, w))
                v.drain()
                for w in range(2):
                    v.max_index(s8(TOPI, w, 1), s8(TOPS, w, 1), half(SC2, w))
                c3 = lambda ap: ap.rearrange("p (i j) -> p i j", i=TOPK)
                v.tensor_tensor(c3(CAND), over_cols(TOPS[:, 0:TOPK], TOPK), over_rows(TOPS[:, TOPK:2 * TOPK], TOPK), ALU.add)
                v.drain()
                v.tensor_copy(TOPIF, TOPI)
                v.max(BEST[:, 0:8], CAND)
                v.drain()
                v.match_replace(CAND2, BEST[:, 0:8], CAND, LOWEST)
                v.max_index(BESTI[:, 0:8], BEST[:, 0:8], CAND)
                v.drain()
                v.max(BEST[:, 8:16], CAND2)
                v.drain()
                v.max_index(BESTI[:, 8:16], BEST[:, 8:16], CAND2)
                v.tensor_scalar(GATE[par], BEST, BEST[:, 0:1], None, ALU.subtract).then_inc(sem("gate_arg"), 1)
                v.drain()
                v.tensor_scalar(BESTIJ[:, 0:TOPK], BESTI, 4, None, ALU.logical_shift_right)
                v.tensor_scalar(BESTIJ[:, TOPK:], BESTI, TOPK - 1, None, ALU.bitwise_and)
                v.drain()
                v.tensor_copy(BESTF, BESTIJ)
                v.drain()
                o3 = OH.rearrange("p (k j) -> p k j", j=TOPK)
                v.tensor_tensor(o3, over_cols(BESTF, TOPK), over_rows(iota, 2 * TOPK), ALU.is_equal)
                v.drain()
                o4 = OH.rearrange("p (w k j) -> p w k j", w=2, j=TOPK)
                keys = TOPIF.rearrange("p (w j) -> p w j", w=2).unsqueeze(2).broadcast_to([P, 2, TOPK, TOPK])
                v.tensor_tensor(o4, o4, keys, ALU.mult)
                v.drain()
                v.tensor_reduce(ROWS, o3, AX, ALU.add)
                v.drain()
                if not (isinstance(h, int) and PH * t + h < 2):
                    dve.wait_ge(sem("u_idx"), PH * t + h - 1)
                v.scalar_tensor_tensor(out=EXPERT[par], in0=ROWS[:, 0:TOPK],
                                       scalar=float(NK), in1=ROWS[:, TOPK:], op0=ALU.mult, op1=ALU.add) \
                    .then_inc(sem("experts"), 1)

            def body(t, h, par):
                first, last = (t == 0 and opens(h)), t == T
                gu = PH * t + h
                gv = gu - 1

                def weights():
                    dve.wait_ge(sem("gate_exps"), gv + 1)
                    v.reciprocal(gsum[1 - par], gsum[1 - par])
                    v.drain()
                    dve.wait_ge(sem("gelu"), gv + 1)
                    v.scalar_tensor_tensor(out=WGT[1 - par], in0=GEL[1 - par], scalar=gsum[1 - par], in1=GATE[1 - par],
                                           op0=ALU.mult, op1=ALU.mult).then_inc(sem("weight"), 1)

                if last:
                    weights()
                else:
                    for s in range(TOPK):
                        if s == 2 and not first:
                            weights()
                        if s == 4:
                            if isinstance(h, int) and h == PH - 1:
                                if t < T - 1:
                                    dve.wait_ge(sem("scores"), 4 * (t + 1) + 1)
                                    top_experts(t + 1, 0, 1 - par)
                            else:
                                if isinstance(h, int) or t:
                                    dve.wait_ge(sem("scores"), 4 * t + ((h + 1) // 2 + 1 if t == 0 else 4))
                                else:
                                    dve.wait_ge(sem("scores"), 4)
                                top_experts(t, h + 1, 1 - par)
                        dve.wait_ge(sem(f"u_row{s % UN}"), 16 * ((TOPK // UN) * gu + s // UN + 1))
                        v.tensor_tensor_reduce(out=UR[s % UN], in0=UR[s % UN], in1=N2[:, t, :], scale=1.0, scalar=0.0,
                                               op0=ALU.mult, op1=ALU.add, accum_out=HID[par][:, s:s + 1]) \
                            .then_inc(sem("u_dot"), 1)
                if opens(h) and t:
                    dve.wait_ge(sem("y_act"), 3 * t - 2)
                    v.tensor_scalar(ysq[0], ysq[0], 1.0 / D, EPS, ALU.mult, ALU.add).then_inc(sem("y_dve"), 1)
                    dve.wait_ge(sem("y_act"), 3 * t - 1)
                    v.reciprocal(ysq[1], ysq[1]).then_inc(sem("y_dve"), 1)
                    dve.wait_ge(sem("y_act"), 3 * t)
                    v.tensor_tensor(YS, YS, FINB, ALU.mult).then_inc(sem("y_dve"), 1)

            dve.wait_ge(sem("keys_in"), 16)
            dve.wait_ge(sem("scores"), 1)
            top_experts(0, 0, 0)
            steps(dve, body)

        @block.tensor
        def _(pe):
            mm = nc.tensor.matmul
            for t in range(T):
                b = 2 * (t % 2)
                if t == 0:
                    pe.wait_ge(sem("gdn_out"), T)
                    pe.wait_ge(sem("wo_in"), 32)
                if t >= 2:
                    pe.wait_ge(sem("h_sum"), t - 1)
                for half in range(2):
                    for k in range(KD):
                        ins = mm(PS[:, b + half, :], MIXT[:, k, tok(t)], WO[:, k, 512 * half:512 * half + 512],
                                 start=k == 0, stop=k == KD - 1)
                ins.then_inc(sem("out_mm"), 1)

            cols = lambda c: slice((c % 4) * P, (c % 4 + 1) * P)

            def normed(t):
                pe.wait_ge(sem("n2"), t + 1)
                if t:
                    pe.wait_ge(sem("scores"), 4 * t)
                for k in range(KD):
                    ins = nc.tensor.transpose(PS[:, 4 + k // 4, cols(k)], N2[:, t, k * P:(k + 1) * P], ident)
                ins.then_inc(sem("n2t_mm"), 1)

            def query(t, c):
                b = c // 4
                if c == 0:
                    pe.wait_ge(sem("n2t"), t + 1)
                if c % 4 == 0 and 4 * t + b >= 2:
                    pe.wait_ge(sem("q"), 4 * t + b - 1)
                for k in range(KD):
                    ins = mm(PS[:, 6 + b % 2, cols(c)], WQH[k // 4][:, k % 4, c * P:(c + 1) * P], N2T[:, k, :],
                             start=k == 0, stop=k == KD - 1)
                if c % 4 == 3:
                    ins.then_inc(sem("q_mm"), 1)

            def score(t, b):
                pe.wait_ge(sem("q"), 4 * t + b + 1)
                if 4 * t + b >= 2:
                    pe.wait_ge(sem("scores"), 4 * t + b - 1)
                for c in range(4 * b, 4 * b + 4):
                    ins = mm(PS[:, 4 + b % 2, cols(c)], QPT[:, c % 8, :], SKT[:, c, :], start=True, stop=True)
                ins.then_inc(sem("score_mm"), 1)

            def front_after(t, half, s):
                if half == 0 and s == 0:
                    normed(t)
                if s < 8:
                    query(t, 8 * half + s)
                if s in (10, 12):
                    score(t, 2 * half + (s == 12))

            def body(t, h, par):
                first, last = (t == 0 and opens(h)), t == T
                gu = PH * t + h
                gv = gu - 1
                tv = t - 1 if opens(h) else t
                half = 0 if opens(h) else 1 if isinstance(h, int) and h == PH - 1 else None
                if t >= T - 1:
                    half = None
                for s in range(TOPK):
                    if not first:
                        pe.wait_ge(sem("diag"), TOPK * gv + s + 1)
                        pe.wait_ge(sem(f"v_row{s % VN}"), 16 * ((TOPK // VN) * gv + s // VN + 1))
                        for c in range(2):
                            ins = mm(PS[:, 2 * (tv % 2) + c, :], DG[s % DN], VR[s % VN][:, 512 * c:512 * c + 512],
                                     start=False, stop=tv != t and s == TOPK - 1)
                        ins.then_inc(sem("v_sum"), 1)
                    if half is not None:
                        front_after(t + 1, half, s)
                if opens(h) and not last:
                    if t >= 2:
                        pe.wait_ge(sem("y_act"), 3 * (t - 1))
                    for c in range(2):
                        mm(PS[:, 2 * (t % 2) + c, :], ident, H[:, t, 512 * c:512 * c + 512], start=True, stop=False)

            pe.wait_ge(sem("wq_in"), 32)
            pe.wait_ge(sem("keys_in"), 16)
            normed(0)
            for half in range(2):
                for c in range(8):
                    query(0, 8 * half + c)
                for b in range(2):
                    score(0, 2 * half + b)
            steps(pe, body)


def kernel(**inputs):
    import concourse.bacc as bacc
    from concourse.bass_utils import run_bass_kernel_spmd as run
    nc = bacc.Bacc("TRN2", target_bir_lowering=False, num_devices=1)
    laid_out = {name: inputs.get(name) for name in NAMES}
    laid_out["positions"] = inputs["positions"].reshape(T, P).T
    laid_out["sub_keys"] = np.transpose(inputs["peer_sub_keys"][0].reshape(2 * PH, NK, P), (2, 0, 1))
    columns = [inputs[n].reshape(-1, P) for n in ("conv_w", "ln1_w", "q_a_norm_w", "kv_a_norm_w", "gdn_norm_w")]
    laid_out["columns"] = np.concatenate(columns).T
    laid_out["consts"] = shape_constants()
    arrays, args = {}, []
    for name, a in laid_out.items():
        arrays["in_" + name] = a = np.ascontiguousarray(a)
        args.append(nc.dram_tensor("in_" + name, a.shape, mybir.dt.from_np(a.dtype), kind="ExternalInput").ap())
    args.append(nc.dram_tensor("out", OUT_SHAPE, F32, kind="ExternalOutput").ap())
    encoder_block(nc, *args)
    return run(nc, [arrays], core_ids=[0]).results[0]["out"]


NAMES = ["x", "positions", "w_in", "w_q_up", "w_kv_up", "a_log_f", "dt_bias_f", "a_log_b", "dt_bias_b", "w_out",
         "ln2_w", "peer_wq", "sub_keys", "peer_u", "peer_v", "final_norm_w"]
OUT_SHAPE = (1, S, D)
```

```python
import math
import numpy as np
import concourse.bass as bass
from concourse import mybir
from contextlib import ExitStack

F32 = mybir.dt.float32
I32 = mybir.dt.int32
U32 = mybir.dt.uint32
ALU = mybir.AluOpType
ACT = mybir.ActivationFunctionType
AX = mybir.AxisListType.X

P = 128
D = 1024
S = 512
T = S // P
KD = D // P
NH = 4
NOPE, ROPE = 128, 64
HR = ROPE // 2
QR, KVR = 256, 128
MLA_IN = QR + KVR + ROPE
QKV0 = MLA_IN
CT_N = 12
Z0 = QKV0 + CT_N * P
G0 = Z0 + NH * P
IN_W = G0 + 4 * NH
TAPS = 5
UNITS = NH * T
SLOTS = 5
LEVELS = 7
PH = 8
NK = 128
TOPK = 16
EPS = 1e-6
SCALE = (NOPE + ROPE) ** -0.5
BIG = 1e30
TWO_PI = 2 * math.pi
PI_HI = 6.28125
PI_LO = TWO_PI - PI_HI
PI_F = 3.1415925
MAGIC = 12582912.0
LOWEST = -3.0e38
UN, VN, DN = 8, 4, 8

CONSTS = ["ident", "tri_f", "tri_b", "strict_f", "strict_b", "incl_f", "incl_b"]
CONSTS += [f"off_{d}{l}" for d in "fb" for l in range(LEVELS)]
NCONST = len(CONSTS) * P
CONST_W = NCONST + HR + TOPK


def shape_constants():
    i, j = np.arange(P)[:, None], np.arange(P)[None, :]
    m = {"ident": i == j, "tri_f": i <= j, "tri_b": i >= j}
    m["strict_f"], m["strict_b"] = np.where(j < i, 0, BIG), np.where(j > i, 0, BIG)
    m["incl_f"], m["incl_b"] = np.where(j >= i, 0, BIG), np.where(j <= i, 0, BIG)
    for l in range(LEVELS):
        b = 1 << l
        off = (i // (2 * b) == j // (2 * b)) & ((i // b) % 2 == 1) & ((j // b) % 2 == 0)
        m[f"off_f{l}"], m[f"off_b{l}"] = off, off.T
    out = np.zeros((P, CONST_W), np.float32)
    for n, name in enumerate(CONSTS):
        out[:, n * P:(n + 1) * P] = m[name]
    inv = np.float32(10000.0) ** (-np.arange(0, ROPE, 2, dtype=np.float32) / np.float32(ROPE))
    out[:, NCONST:NCONST + HR] = inv
    out[:, NCONST + HR:] = np.arange(TOPK)
    return out


def opens(h):
    return isinstance(h, int) and h == 0


def over_rows(ap, n):
    return ap.unsqueeze(1).broadcast_to([ap.shape[0], n, ap.shape[1]])


def over_cols(ap, m):
    return ap.unsqueeze(len(ap.shape)).broadcast_to(list(ap.shape) + [m])


class Names:

    def __init__(self, nc, ctx):
        self._nc, self._ctx, self._made = nc, ctx, {}

    def __call__(self, name):
        if name not in self._made:
            self._made[name] = self._ctx.enter_context(self._nc.semaphore(name))
        return self._made[name]


def encoder_block(nc, x, positions, w_in, w_q_up, w_kv_up, a_log_f, dt_bias_f, a_log_b, dt_bias_b, w_out,
                  ln2_w, peer_wq, sub_keys, peer_u, peer_v, final_norm_w, columns, consts, out):
    ctx = ExitStack()
    with ctx:
        sem = Names(nc, ctx)

        def sb(name, shape, dt=F32):
            return ctx.enter_context(nc.sbuf_tensor(name, shape, dt))

        CONST = sb("CONST", [P, CONST_W])
        H = sb("H", [P, T, D])
        R1A = sb("R1A", [P, 16384])
        R1B = sb("R1B", [P, 8192])
        R2 = sb("R2", [P, 16384])
        MIXT = sb("MIXT", [P, KD, S])
        SMALL = sb("SMALL", [P, 1100])
        PS = ctx.enter_context(nc.psum_tensor("PS", [P, 8, 512], F32))

        cmat = {n: CONST[:, k * P:(k + 1) * P] for k, n in enumerate(CONSTS)}
        ident = cmat["ident"]
        inv_freq = CONST[:, NCONST:NCONST + HR]
        n1T = MIXT

        KA = 6
        WA = R1A[:, 0:KA * IN_W].rearrange("p (k n) -> p k n", n=IN_W)
        WB = R1B[:, 0:(KD - KA) * IN_W].rearrange("p (k n) -> p k n", n=IN_W)

        def w_in_at(k, c0, c1):
            return WA[:, k, c0:c1] if k < KA else WB[:, k - KA, c0:c1]

        off = (KD - KA) * IN_W
        WQU = R1B[:, off:off + 2 * 768].rearrange("p (k n) -> p k n", k=2)
        WKU = R1B[:, off + 1536:off + 1536 + 1024]
        XS = R2[:, 0:T * D].rearrange("p (t n) -> p t n", t=T)
        TOK = R2[:, 0:T * CT_N * P].rearrange("p (t c n) -> p t c n", t=T, c=CT_N)
        KQT = R2[:, 6144:10240].rearrange("p (h w s) -> p h w s", h=NH, w=2)
        Z = R2[:, 10240:12288].rearrange("p (t n) -> p t n", t=T)
        MISC = R2[:, 12288:16384]
        MG = MISC[:, 0:T * 464].rearrange("p (t n) -> p t n", t=T)
        RAW = [MISC[:, 1856 + 516 * i:1856 + 516 * (i + 1)] for i in range(2)]
        CV = [MISC[:, 2888 + 512 * i:2888 + 512 * (i + 1)] for i in range(2)]

        at = [0]

        def small(n):
            at[0] += n
            assert at[0] <= 1100, at
            return SMALL[:, at[0] - n:at[0]]

        ONES = small(P)
        COLS = small(72)
        ssq, rstd = small(T), small(T)
        ss2, r2 = small(8 * T), small(8 * T)
        ssm, rm = small(2 * T), small(2 * T)
        BIAS, ALOG = small(8), small(8)
        cos, sin = small(T * HR), small(T * HR)
        mx, nb, rs, rr = small(16), small(16), small(16), small(16)
        gc_ = small(32)
        eg_ = small(32)
        beta = small(32)
        gg = small(32)
        beg = small(32)
        skd = [small(4), small(4)]
        egl = [small(4), small(4)]
        osq, orr = small(16), small(16)
        POS_I, POS_F = small(T).bitcast(I32), small(T)
        G_A, G_NA, G_E, G_B = small(32), small(32), small(32), small(32)
        ANG, ANG_S, ANG_C, TURN = (R1B[:, 7584 + 128 * i:7712 + 128 * i] for i in range(4))
        SQ3 = PS[:, 7, :].rearrange("p (t n) -> p t n", t=T)
        SQA = CV[0]

        conv_col = lambda tap, c: COLS[:, tap * CT_N + c:tap * CT_N + c + 1]
        ln1_col = lambda k: COLS[:, 60 + k:61 + k]
        qa_col = lambda k: COLS[:, 68 + k:69 + k]
        kva_col, gdn_col = COLS[:, 70:71], COLS[:, 71:72]

        wsat = [0]

        def ws(n):
            wsat[0] += n
            assert wsat[0] <= 16384, wsat
            return R1A[:, wsat[0] - n:wsat[0]]

        CQ = ws(T * 384).rearrange("p (t n) -> p t n", t=T)
        CQT = ws(1024).rearrange("p (k s) -> p k s", k=2)
        CKVT = ws(512)
        KPR = ws(T * 128).rearrange("p (t n) -> p t n", t=T)
        KPET = ws(512)
        QNT = ws(2048).rearrange("p (h s) -> p h s", h=NH)
        KNT = ws(2048).rearrange("p (h s) -> p h s", h=NH)
        QPQPR = ws(2 * T * 256)
        QP = QPQPR[:, 0:1024].rearrange("p (t n) -> p t n", t=T)
        QPR = QPQPR[:, 1024:2048].rearrange("p (t n) -> p t n", t=T)
        QPET = ws(1024).rearrange("p (k s) -> p k s", k=2)
        VT = ws(2048).rearrange("p (t n) -> p t n", t=T)
        PR = [ws(512) for _ in range(2)]
        PT0 = ws(2048)
        PTs = [PT0.rearrange("p (k s) -> p k s", k=T),
               QPQPR.rearrange("p (k s) -> p k s", k=T)]
        ROT = [PT0[:, 0:128], PT0[:, 128:256]]

        gat = [0]

        def gw(n):
            gat[0] += n
            assert gat[0] <= 8192, gat
            return R1B[:, gat[0] - n:gat[0]]

        h4 = lambda ap: ap.rearrange("p (h n) -> p h n", h=NH)
        A = [gw(1024) for _ in range(2)]
        DIFF = [gw(512) for _ in range(2)]
        LO = [gw(512) for _ in range(2)]
        TM = [gw(512) for _ in range(2)]
        XM = [gw(512) for _ in range(2)]
        EG = [gw(512) for _ in range(2)]
        KBG = [MISC[:, 1856 + 512 * i:2368 + 512 * i] for i in range(2)]
        KDC = [MISC[:, 2880 + 512 * i:3392 + 512 * i] for i in range(2)]
        VB = [gw(512) for _ in range(2)]
        ST = [MISC[:, 512 * i:512 * (i + 1)] for i in range(2)]
        O = TOK[:, :, 0:NH, :]

        block = ctx.enter_context(nc.Block())

        dirs = "fb"
        chunk_of = lambda d, s: s if d == 0 else T - 1 - s
        last_of = (P - 1, 0)
        tok = lambda t: slice(t * P, (t + 1) * P)

        def blocks(ap, level, odd):
            return ap.rearrange("p (m w n) -> p m w n", w=2, n=1 << level)[:, :, odd, :]

        @block.sync
        def _(sp):
            sp.dma_start(ident, consts[:, 0:P]).then_inc(sem("cols_in"), 16)
            sp.dma_start(COLS, columns).then_inc(sem("cols_in"), 16)
            for t in range(T):
                sp.dma_start(H[:, t, :], x[0, tok(t), :]).then_inc(sem(f"x_in{t}"), 16)
            sp.dma_start(POS_I, positions).then_inc(sem("pos_in"), 16)
            sp.dma_start(CONST[:, NCONST:], consts[:, NCONST:]).then_inc(sem("pos_in"), 16)
            for g in range(4):
                c0, c1 = QKV0 + g * 3 * P, QKV0 + (g + 1) * 3 * P
                src = w_in[0].rearrange("(k p) n -> p k n", p=P)
                sp.dma_start(WA[:, :, c0:c1], src[:, 0:KA, c0:c1]).then_inc(sem(f"w_qkv{g}_in"), 16)
                sp.dma_start(WB[:, :, c0:c1], src[:, KA:KD, c0:c1]).then_inc(sem(f"w_qkv{g}_in"), 16)
            for c0, c1 in ((0, MLA_IN), (Z0, IN_W)):
                sp.dma_start(WA[:, :, c0:c1], src[:, 0:KA, c0:c1]).then_inc(sem("w_rest_in"), 16)
                sp.dma_start(WB[:, :, c0:c1], src[:, KA:KD, c0:c1]).then_inc(sem("w_rest_in"), 16)
            sp.dma_start(WQU, w_q_up[0].rearrange("(k p) n -> p k n", p=P)).then_inc(sem("w_up_in"), 16)
            sp.dma_start(WKU, w_kv_up[0]).then_inc(sem("w_up_in"), 16)
            sp.dma_start(CONST[:, P:NCONST], consts[:, P:NCONST]).then_inc(sem("masks_in"), 16)

        @block.gpsimd
        def _(pool):
            for n, (src, dst) in enumerate(((dt_bias_f, BIAS[:, 0:4]), (dt_bias_b, BIAS[:, 4:8]),
                                            (a_log_f, ALOG[:, 0:4]), (a_log_b, ALOG[:, 4:8]))):
                pool.dma_start(dst, src[0].partition_broadcast(P)).then_inc(sem("gate_rows_in"), 16)
            nc.gpsimd.memset(ONES, 1.0).then_inc(sem("ones"), 1)

            def rotate(src1, src2, dst1, dst2, c, s, a, b, name, wait, n):
                pool.wait_ge(*wait)
                if n:
                    pool.wait_ge(sem(name), 6 * n)
                steps = [(a, src1, c, ALU.mult), (b, src2, s, ALU.mult), (dst1, a, b, ALU.subtract),
                         (a, src2, c, ALU.mult), (b, src1, s, ALU.mult), (dst2, a, b, ALU.add)]
                for k, (o, i0, i1, op) in enumerate(steps):
                    if k in (2, 3, 5):
                        pool.wait_ge(sem(name), 6 * n + k)
                    nc.gpsimd.tensor_tensor(o, i0, i1, op).then_inc(sem(name), 1)

            pool.wait_ge(sem("rotary_sin"), 2)
            pool.wait_ge(sem("z_mm"), T)
            ra, rb = (r[:, 0:128] for r in ROT)
            v3 = lambda ap: ap.rearrange("p (t n) -> p t n", n=HR)
            rotate(MG[:, :, 384:416], MG[:, :, 416:448], KPR[:, :, 0:HR], KPR[:, :, HR:ROPE],
                   v3(cos), v3(sin), v3(ra), v3(rb), "k_rotated", (sem("mg_ready"), T), 0)
            pool.wait_ge(sem("k_rotated"), 6)
            nc.gpsimd.tensor_copy(KPR[:, :, ROPE:2 * ROPE], KPR[:, :, 0:ROPE]).then_inc(sem("k_rotated"), 1)
            pool.wait_ge(sem("k_rotated"), 7)
            for t in range(T):
                q3 = QP[:, t, :].rearrange("p (h n) -> p h n", n=ROPE)
                o3 = QPR[:, t, :].rearrange("p (h n) -> p h n", n=ROPE)
                ct, st = (over_rows(m[:, t * HR:(t + 1) * HR], NH) for m in (cos, sin))
                rotate(q3[:, :, 0:HR], q3[:, :, HR:], o3[:, :, 0:HR], o3[:, :, HR:], ct, st,
                       v3(ra), v3(rb), "q_rotated", (sem("qp_ready"), 2 * t + 1), t)

            def factor(d, s, k):
                t, D_ = chunk_of(d, s), dirs[d]
                bs = slice((d * T + t) * NH, (d * T + t + 1) * NH)
                dst, a, b = ((VB[d], TOK[:, t, 8:12, :], over_cols(beta[:, bs], P)),
                             (KBG[d], TOK[:, t, 4:8, :], over_cols(beg[:, bs], P)),
                             (KDC[d], TOK[:, t, 4:8, :], over_cols(skd[d], P)),
                             (EG[d], KQT[:, :, 1, tok(t)], h4(EG[d])))[k]
                if k == 0:
                    pool.wait_ge(sem("eg_row" + D_), 2 * s + 2)
                    pool.wait_ge(sem("egl" + D_), s + 1)
                    pool.wait_ge(sem("beta_eg"), 1)
                nc.gpsimd.tensor_tensor(h4(dst), a, b, ALU.mult).then_inc(sem("scaled" + D_), 1)

            for s in range(T):
                for d in range(2):
                    D_ = dirs[d]
                    pool.wait_ge(sem("exponents" + D_), s + 1)
                    if s:
                        pool.wait_ge(sem("o_mm" + D_), s)
                        pool.wait_ge(sem("state" + D_), s)
                    nc.gpsimd.tensor_tensor(h4(A[d][:, 0:512]), h4(DIFF[d]), over_rows(cmat["strict_" + D_], NH),
                                            ALU.add).then_inc(sem("masked" + D_), 1)
                    nc.gpsimd.tensor_tensor(h4(A[d][:, 512:1024]), over_rows(cmat["incl_" + D_], NH), h4(DIFF[d]),
                                            ALU.subtract).then_inc(sem("masked" + D_), 1)
                for l in range(LEVELS):
                    for d in range(2):
                        D_ = dirs[d]
                        pool.wait_ge(sem("lower" + D_), s + 1)
                        if l == 1:
                            pool.wait_ge(sem("x_init" + D_), 2 * s + 2)
                        elif l > 1:
                            pool.wait_ge(sem("n_mm" + D_), s * 6 + l - 1)
                        elif s:
                            pool.wait_ge(sem("n_mm" + D_), s * 6)
                        nc.gpsimd.tensor_tensor(h4(LO[d]), h4(A[d][:, 0:512]), over_rows(cmat[f"off_{D_}{l}"], NH),
                                                ALU.mult).then_inc(sem("level" + D_), 1)
                    if 1 <= l <= 4:
                        factor(0, s, l - 1)
                        factor(1, s, l - 1)

        @block.scalar
        def _(act):
            def act_(out, in_, f, name, **kw):
                return nc.scalar.activation(out, in_, f, **kw).then_inc(sem(name), 1)

            for t in range(T):
                act.wait_ge(sem(f"x_in{t}"), 16)
                act_(XS[:, t, :], H[:, t, :], ACT.Square, "x_squares", accum_out=ssq[:, t:t + 1])
                act.wait_ge(sem("mean_squares"), t + 1)
                act_(rstd[:, t:t + 1], ssq[:, t:t + 1], ACT.Sqrt, "roots")
            act.wait_ge(sem("cols_in"), 32)
            for k in range(1, KD, 2):
                act.wait_ge(sem("n1t_mm"), k + 1)
                act_(n1T[:, k, :], PS[:, k, :], ACT.Copy, "n1t", scale=ln1_col(k))

            def raw(c):
                act.wait_ge(sem("qkv_mm"), c + 1)
                if c >= 2:
                    act.wait_ge(sem("conv"), c - 1)
                act_(RAW[c % 2][:, 2:514], PS[:, c % 2, :], ACT.Copy, "raw")

            def silu(c):
                act.wait_ge(sem("conv"), c + 1)
                act_(CV[c % 2], CV[c % 2], ACT.Silu, "silu")

            def tok_copy(c):
                act.wait_ge(sem("conv_tp"), c + 1)
                act_(TOK[:, :, c, :], PS[:, 2 + c % 2, :].rearrange("p (t n) -> p t n", t=T), ACT.Copy, "tok")

            act.wait_ge(sem("raw_pads"), 4)
            act.wait_ge(sem("xs"), T)
            raw(0)
            for c in range(CT_N):
                if c + 1 < CT_N:
                    raw(c + 1)
                silu(c)
                if c >= 1:
                    tok_copy(c - 1)
            tok_copy(CT_N - 1)
            act.wait_ge(sem("mean_squares"), T + 1)
            act_(r2, ss2, ACT.Sqrt, "roots")
            act.wait_ge(sem("mean_squares"), T + 2)
            act_(rm, ssm, ACT.Sqrt, "roots")
            act.wait_ge(sem("rotary_args"), 1)
            act_(sin, ANG_S, ACT.Sin, "rotary_sin")
            act_(cos, ANG_C, ACT.Sin, "rotary_sin")

            act.wait_ge(sem("gate_args"), 1)
            act_(G_E, G_NA, ACT.Exp, "gate_exp", scale=-1.0)
            act.wait_ge(sem("gate_exp"), 1)
            act_(G_E, G_E, ACT.Ln, "gate_exp", bias=1.0)
            act_(G_B, G_B, ACT.Exp, "gate_exp", scale=-1.0)
            act.wait_ge(sem("gate_rows_in"), 64)
            act_(ALOG, ALOG, ACT.Exp, "gate_exp")
            for t in range(T):
                act.wait_ge(sem("z_mm"), t + 1)
                act_(Z[:, t, :], PS[:, 6 + t % 2, :], ACT.Silu, "z")
            act.wait_ge(sem("g_cum"), 2)
            act_(eg_, gc_, ACT.Exp, "eg")

            for c in range(1, 8, 2):
                act.wait_ge(sem("kqt_mm"), c + 1)
                act_(KQT[:, c // 2, c % 2, :], PS[:, c, :], ACT.Copy, "kqt")
            for h in range(NH):
                act.wait_ge(sem("nope_mm"), 2 * h + 1)
                act_(QNT[:, h, :], PS[:, 4 + h % 2, :], ACT.Copy, "nope")
                act.wait_ge(sem("nope_mm"), 2 * h + 2)
                act_(KNT[:, h, :], PS[:, 6 + h % 2, :], ACT.Copy, "nope")

            def attend(q):
                n = q - 2
                if 0 <= n < UNITS:
                    h, qt = divmod(n, T)
                    act.wait_ge(sem("p_tp"), n + 1)
                    if qt == 0 and h >= 2:
                        act.wait_ge(sem("pv_mm"), h - 1)
                    act_(PTs[h % 2][:, :, tok(qt)], PS[:, 7, :].rearrange("p (k q) -> p k q", k=T), ACT.Copy, "pt")
                if q < UNITS:
                    act.wait_ge(sem("row_max"), q + 1)
                    act_(PR[q % 2], PS[:, 6, :], ACT.Exp, "p_exp", bias=nb[:, q:q + 1], scale=SCALE,
                         accum_out=rs[:, q:q + 1])

            for s in range(T):
                for d in range(2):
                    D_, b = dirs[d], 3 * d
                    act.wait_ge(sem("g_rows" + D_), s + 1)
                    act.wait_ge(sem("exponents" + D_), s + 1)
                    if s:
                        act.wait_ge(sem("o_mm" + D_), s)
                        act.wait_ge(sem("state" + D_), s)
                    act_(EG[d], PS[:, b, :], ACT.Exp, "eg_row" + D_)
                    act_(skd[d], skd[d], ACT.Exp, "eg_row" + D_)
                for d in range(2):
                    D_ = dirs[d]
                    act.wait_ge(sem("masked" + D_), 2 * s + 2)
                    act_(A[d], A[d], ACT.Exp, "decay" + D_, scale=-1.0)
                attend(SLOTS * s)
                for l in range(1, LEVELS):
                    for d in range(2):
                        D_, b = dirs[d], 3 * d
                        act.wait_ge(sem("n_mm" + D_), s * 6 + l)
                        act_(DIFF[d], PS[:, b + 1, :], ACT.Copy, "n" + D_)
                    if l < SLOTS:
                        attend(SLOTS * s + l)
                for d in range(2 if s else 0):
                    D_, b = dirs[d], 3 * d
                    act.wait_ge(sem("w_mm" + D_), s)
                    act_(TM[d], PS[:, b + 1, :], ACT.Copy, "w" + D_, scale=-1.0)
                for d in range(2):
                    D_, b = dirs[d], 3 * d
                    act.wait_ge(sem("vn_mm" + D_), s + 1)
                    act_(KBG[d], PS[:, b + 2, :], ACT.Copy, "vn" + D_)

        @block.vector
        def _(dve):
            v = nc.vector
            chain = [0]

            def mark(ins):
                chain[0] += 1
                ins.then_inc(sem("dve_chain"), 1)

            def link(ins):
                mark(ins)
                dve.wait_ge(sem("dve_chain"), chain[0])

            for r in RAW:
                v.memset(r[:, 0:2], 0.0).then_inc(sem("raw_pads"), 1)
                v.memset(r[:, 514:516], 0.0).then_inc(sem("raw_pads"), 1)
            for t in range(T):
                c, r = ssq[:, t:t + 1], rstd[:, t:t + 1]
                dve.wait_ge(sem("x_squares"), t + 1)
                v.tensor_scalar(c, c, 1.0 / D, EPS, ALU.mult, ALU.add).then_inc(sem("mean_squares"), 1)
                dve.wait_ge(sem("roots"), t + 1)
                link(v.reciprocal(r, r))
                v.tensor_scalar(XS[:, t, :], H[:, t, :], rstd[:, t:t + 1], None, ALU.mult).then_inc(sem("xs"), 1)
            dve.wait_ge(sem("cols_in"), 32)
            for k in range(0, KD, 2):
                dve.wait_ge(sem("n1t_mm"), k + 1)
                v.tensor_scalar(n1T[:, k, :], PS[:, k, :], ln1_col(k), None, ALU.mult).then_inc(sem("n1t"), 1)

            dve.wait_ge(sem("pos_in"), 32)
            link(v.tensor_copy(POS_F, POS_I))
            a3 = lambda ap: ap.rearrange("p (t n) -> p t n", n=HR)
            link(v.tensor_tensor(a3(ANG), over_rows(inv_freq, T), over_cols(POS_F, HR), ALU.mult))
            for dst, shift in ((ANG_S, 0.0), (ANG_C, 0.25)):
                link(v.tensor_scalar(TURN, ANG, 1.0 / TWO_PI, shift, ALU.mult, ALU.add))
                link(v.tensor_scalar(TURN, TURN, MAGIC, None, ALU.add))
                link(v.tensor_scalar(TURN, TURN, -MAGIC, None, ALU.add))
                link(v.scalar_tensor_tensor(out=dst, in0=TURN, scalar=-PI_HI, in1=ANG, op0=ALU.mult, op1=ALU.add))
                link(v.scalar_tensor_tensor(out=dst, in0=TURN, scalar=-PI_LO, in1=dst, op0=ALU.mult, op1=ALU.add))
                if shift:
                    link(v.tensor_scalar(dst, dst, math.pi / 2, None, ALU.add))
                ins = v.tensor_scalar(dst, dst, PI_F, -PI_F, ALU.min, ALU.max)
                if shift:
                    ins.then_inc(sem("rotary_args"), 1)
                else:
                    link(ins)

            def conv(c):
                dve.wait_ge(sem("raw"), c + 1)
                if c >= 2:
                    dve.wait_ge(sem("conv_tp"), c - 1)
                r = RAW[c % 2]
                link(v.tensor_scalar(CV[c % 2], r[:, 0:512], conv_col(0, c), None, ALU.mult))
                for tap in range(1, TAPS):
                    ins = v.scalar_tensor_tensor(out=CV[c % 2], in0=r[:, tap:tap + 512], scalar=conv_col(tap, c),
                                                 in1=CV[c % 2], op0=ALU.mult, op1=ALU.add)
                    if tap < TAPS - 1:
                        link(ins)
                    else:
                        ins.then_inc(sem("conv"), 1)

            def qk_sum(c):
                dve.wait_ge(sem("tok"), c + 1)
                link(v.tensor_tensor(SQ3, TOK[:, :, c, :], TOK[:, :, c, :], ALU.mult))
                link(v.tensor_reduce(ss2[:, c * T:(c + 1) * T], SQ3, AX, ALU.add))

            for c in range(CT_N):
                conv(c)
                if 2 <= c < 10:
                    qk_sum(c - 2)
            v.tensor_scalar(ss2, ss2, EPS, None, ALU.add).then_inc(sem("mean_squares"), 1)
            for t in range(T):
                dve.wait_ge(sem("mg_mm"), t + 1)
                v.tensor_copy(MG[:, t, :], PS[:, 4 + t % 2, 0:464]).then_inc(sem("mg_ready"), 1)
            dve.wait_ge(sem("mg_ready"), T)
            for t in range(T):
                for k, (a, b) in enumerate(((0, QR), (QR, QR + KVR))):
                    ins = v.tensor_tensor_reduce(out=SQA[:, a:b], in0=MG[:, t, a:b], in1=MG[:, t, a:b], scale=1.0 / (b - a),
                                                 scalar=EPS, op0=ALU.mult, op1=ALU.add,
                                                 accum_out=ssm[:, 2 * t + k:2 * t + k + 1])
                    if t == T - 1 and k == 1:
                        ins.then_inc(sem("mean_squares"), 1)
                    elif k:
                        link(ins)
            dve.wait_ge(sem("gate_rows_in"), 64)
            mg4 = MG[:, :, 448:464].rearrange("p t (d w h) -> p d t w h", d=2, w=2)
            for d in range(2):
                o3 = lambda ap: ap[:, 16 * d:16 * d + 16].rearrange("p (t h) -> p t h", t=T)
                mark(v.tensor_tensor(o3(G_A), mg4[:, d, :, 0, :], over_rows(BIAS[:, 4 * d:4 * d + 4], T), ALU.add))
                link(v.tensor_copy(o3(G_B), mg4[:, d, :, 1, :]))
            v.scalar_tensor_tensor(out=G_NA, in0=G_A, scalar=-1.0, in1=G_A, op0=ALU.mult, op1=ALU.max) \
                .then_inc(sem("gate_args"), 1)
            dve.wait_ge(sem("roots"), T + 1)
            link(v.reciprocal(r2, r2))
            link(v.tensor_scalar(r2[:, 0:NH * T], r2[:, 0:NH * T], float(P) ** -0.5, None, ALU.mult))
            r2v = r2.rearrange("p (c t) -> p t c", t=T)
            for t in range(T):
                v.tensor_tensor(TOK[:, t, 0:8, :], TOK[:, t, 0:8, :], over_cols(r2v[:, t, :], P), ALU.mult) \
                    .then_inc(sem("qk_unit"), 1)
            dve.wait_ge(sem("roots"), T + 2)
            link(v.reciprocal(rm, rm))
            dve.wait_ge(sem("masks_in"), 16)
            dve.wait_ge(sem("gate_exp"), 4)
            link(v.scalar_tensor_tensor(out=gg, in0=G_A, scalar=0.0, in1=G_E, op0=ALU.max, op1=ALU.add))
            link(v.tensor_scalar(ALOG, ALOG, -1.0, None, ALU.mult))
            for d in range(2):
                o3 = gg[:, 16 * d:16 * d + 16].rearrange("p (t h) -> p t h", t=T)
                link(v.tensor_tensor(o3, o3, over_rows(ALOG[:, 4 * d:4 * d + 4], T), ALU.mult))
            v.tensor_scalar(beta, G_B, 1.0, None, ALU.add).then_inc(sem("g_ready"), 1)
            dve.wait_ge(sem("g_ready"), 1)
            link(v.reciprocal(beta, beta))
            for d in range(2):
                dve.wait_ge(sem("gc_mm"), d + 1)
                v.tensor_copy(gc_[:, 16 * d:16 * d + 16], PS[:, 3 * d, 0:16]).then_inc(sem("g_cum"), 1)
            dve.wait_ge(sem("z_mm"), T)
            for t in range(T):
                v.tensor_scalar(CQ[:, t, 0:QR], MG[:, t, 0:QR], rm[:, 2 * t:2 * t + 1], None, ALU.mult) \
                    .then_inc(sem("latents"), 1)
                v.tensor_scalar(CQ[:, t, QR:384], MG[:, t, QR:384], rm[:, 2 * t + 1:2 * t + 2], None, ALU.mult) \
                    .then_inc(sem("latents"), 1)
            for c in range(0, 8, 2):
                dve.wait_ge(sem("kqt_mm"), c + 1)
                v.tensor_copy(KQT[:, c // 2, c % 2, :], PS[:, c, :]).then_inc(sem("kqt"), 1)
            for k in range(3):
                dve.wait_ge(sem("latents_tp"), k + 1)
                dst, col = (CQT[:, k, :], qa_col(k)) if k < 2 else (CKVT, kva_col)
                v.tensor_scalar(dst, PS[:, k, :], col, None, ALU.mult).then_inc(sem("latents_t"), 1)
            for t in range(T):
                dve.wait_ge(sem("qp_mm"), 2 * t + 1)
                v.tensor_copy(QP[:, t, :], PS[:, t % 2, 0:256]).then_inc(sem("qp_ready"), 1)
                dve.wait_ge(sem("qp_mm"), 2 * t + 2)
                v.tensor_copy(VT[:, t, :], PS[:, 2 + t % 2, :]).then_inc(sem("qp_ready"), 1)
            dve.wait_ge(sem("pe_tp"), 1)
            v.tensor_copy(KPET, PS[:, 0, :]).then_inc(sem("pe_t"), 1)
            for pr in range(2):
                dve.wait_ge(sem("pe_tp"), pr + 2)
                v.tensor_copy(QPET[:, pr, :], PS[:, 1 + pr, :]).then_inc(sem("pe_t"), 1)

            def attend(q):
                n = q - 1
                if 0 <= n < UNITS:
                    dve.wait_ge(sem("p_exp"), n + 1)
                    link(v.reciprocal(rr[:, n:n + 1], rs[:, n:n + 1]))
                    v.tensor_scalar(PR[n % 2], PR[n % 2], rr[:, n:n + 1], None, ALU.mult).then_inc(sem("p_norm"), 1)
                if q >= T + 2 and (q - 2) % T == 0:
                    h = (q - 2) // T - 1
                    dve.wait_ge(sem("pv_mm"), h + 1)
                    v.tensor_copy(MIXT[:, h, :], PS[:, 7, :]).then_inc(sem("mla_out"), 1)
                if q < UNITS:
                    dve.wait_ge(sem("s_mm"), q + 1)
                    link(v.reduce_max(mx[:, q:q + 1], PS[:, 6, :], AX))
                    v.tensor_scalar(nb[:, q:q + 1], mx[:, q:q + 1], -SCALE, None, ALU.mult).then_inc(sem("row_max"), 1)

            dve.wait_ge(sem("eg"), 1)
            v.tensor_tensor(beg, beta, eg_, ALU.mult).then_inc(sem("beta_eg"), 1)

            def spread_gates(s):
                for d in range(2):
                    D_, t = dirs[d], chunk_of(d, s)
                    bs = slice((d * T + t) * NH, (d * T + t + 1) * NH)
                    if s:
                        dve.wait_ge(sem("d_mm" + D_), 6 * s)
                    v.tensor_tensor(h4(DIFF[d]), over_rows(cmat["tri_" + D_], NH), over_cols(gg[:, bs], P),
                                    ALU.mult).then_inc(sem("g_tri" + D_), 1)

            spread_gates(0)
            for s in range(T):
                for d in range(2):
                    D_, t, b = dirs[d], chunk_of(d, s), 3 * d
                    bs = slice((d * T + t) * NH, (d * T + t + 1) * NH)
                    dve.wait_ge(sem("g_rows" + D_), s + 1)
                    if s:
                        dve.wait_ge(sem("scaled" + D_), 4 * s)
                    gl = h4(PS[:, b, :])[:, :, last_of[d]]
                    mark(v.tensor_tensor(skd[d], gl, gc_[:, bs], ALU.subtract))
                    v.tensor_tensor(h4(DIFF[d]), h4(PS[:, b, :]), over_cols(gc_[:, bs], P), ALU.subtract) \
                        .then_inc(sem("exponents" + D_), 1)
                for d in range(2):
                    D_ = dirs[d]
                    dve.wait_ge(sem("eg_row" + D_), 2 * s + 2)
                    v.tensor_copy(egl[d], h4(EG[d])[:, :, last_of[d]]).then_inc(sem("egl" + D_), 1)
                for d in range(2):
                    D_, t, b = dirs[d], chunk_of(d, s), 3 * d
                    dve.wait_ge(sem("decay" + D_), s + 1)
                    dve.wait_ge(sem("kq_mm" + D_), s + 1)
                    kq = PS[:, b + 1:b + 3, :].rearrange("p b (h w n) -> p (b h) w n", h=2, w=2)
                    for h in range(NH):
                        n = (d * T + t) * NH + h
                        ah = A[d][:, h * P:(h + 1) * P]
                        ins = v.scalar_tensor_tensor(out=ah, in0=kq[:, h, 0, :], scalar=beta[:, n:n + 1], in1=ah,
                                                     op0=ALU.mult, op1=ALU.mult)
                        if h < NH - 1:
                            mark(ins)
                    ins.then_inc(sem("lower" + D_), 1)
                    v.tensor_tensor(h4(A[d][:, 512:1024]), kq[:, :, 1, :], h4(A[d][:, 512:1024]), ALU.mult) \
                        .then_inc(sem("attn" + D_), 1)
                attend(SLOTS * s)
                for d in range(2):
                    D_, b = dirs[d], 3 * d
                    dve.wait_ge(sem("lo_tp" + D_), s + 1)
                    if s:
                        dve.wait_ge(sem("vn_mm" + D_), s)
                    v.tensor_tensor(h4(TM[d]), over_rows(ident, NH), h4(LO[d]), ALU.subtract) \
                        .then_inc(sem("x_init" + D_), 1)
                    v.tensor_tensor(h4(XM[d]), over_rows(ident, NH), h4(PS[:, b, :]), ALU.subtract) \
                        .then_inc(sem("x_init" + D_), 1)
                for l in range(1, LEVELS):
                    if l < SLOTS:
                        attend(SLOTS * s + l)
                    for d in range(2):
                        D_, b = dirs[d], 3 * d
                        dve.wait_ge(sem("d_mm" + D_), s * 6 + l)
                        tm, xm = blocks(TM[d], l, d), blocks(XM[d], l, 1 - d)
                        if l < LEVELS - 1:
                            mark(v.tensor_tensor(tm, tm, blocks(PS[:, b, :], l, d), ALU.subtract))
                        v.tensor_tensor(xm, xm, blocks(PS[:, b + 2, :], l, 1 - d), ALU.subtract) \
                            .then_inc(sem("x_up" + D_), 1)
                if s < T - 1:
                    spread_gates(s + 1)
                for d in range(2):
                    D_, t, b = dirs[d], chunk_of(d, s), 3 * d
                    dve.wait_ge(sem("o_mm" + D_), s + 1)
                    o, ps = O[:, t, :, :], h4(PS[:, b + 1, :])
                    if s < T // 2:
                        v.tensor_copy(o, ps).then_inc(sem("o_out"), 1)
                    else:
                        dve.wait_ge(sem("o_out"), 2 * s)
                        v.tensor_tensor(o, o, ps, ALU.add).then_inc(sem("o_out"), 1)
                    if s == 0:
                        v.tensor_copy(ST[d], PS[:, b, :]).then_inc(sem("state" + D_), 1)
                    elif s < T - 1:
                        for h in range(NH):
                            sh = ST[d][:, h * P:(h + 1) * P]
                            ins = v.scalar_tensor_tensor(out=sh, in0=sh, scalar=egl[d][:, h:h + 1],
                                                         in1=PS[:, b, h * P:(h + 1) * P], op0=ALU.mult, op1=ALU.add)
                            if h < NH - 1:
                                mark(ins)
                        ins.then_inc(sem("state" + D_), 1)

        @block.tensor
        def _(pe):
            mm = nc.tensor.matmul
            tp = lambda o, i, n=P: nc.tensor.transpose(o, i, ident[0:n, 0:n])
            pe.wait_ge(sem("cols_in"), 32)
            for t in range(T):
                pe.wait_ge(sem("xs"), t + 1)
                for k in range(KD):
                    ins = tp(PS[:, k, tok(t)], XS[:, t, k * P:(k + 1) * P])
                    if t == T - 1:
                        ins.then_inc(sem("n1t_mm"), 1)
            pe.wait_ge(sem("n1t"), KD)

            def conv_tp(c):
                pe.wait_ge(sem("silu"), c + 1)
                if c >= 2:
                    pe.wait_ge(sem("tok"), c - 1)
                for t in range(T):
                    ins = tp(PS[:, 2 + c % 2, tok(t)], CV[c % 2][:, tok(t)])
                ins.then_inc(sem("conv_tp"), 1)

            for c in range(CT_N):
                pe.wait_ge(sem(f"w_qkv{c // 3}_in"), 32)
                if c >= 2:
                    pe.wait_ge(sem("raw"), c - 1)
                for k in range(KD):
                    c0 = QKV0 + c * P
                    ins = mm(PS[:, c % 2, :], w_in_at(k, c0, c0 + P), n1T[:, k, :], start=k == 0, stop=k == KD - 1)
                ins.then_inc(sem("qkv_mm"), 1)
                if c >= 2:
                    conv_tp(c - 2)
            pe.wait_ge(sem("w_rest_in"), 64)
            for t in range(T):
                if t >= 2:
                    pe.wait_ge(sem("mg_ready"), t - 1)
                for k in range(KD):
                    mm(PS[:, 4 + t % 2, 0:448], n1T[:, k, tok(t)], w_in_at(k, 0, MLA_IN), start=k == 0, stop=k == KD - 1)
                for k in range(KD):
                    ins = mm(PS[:, 4 + t % 2, 448:464], n1T[:, k, tok(t)], w_in_at(k, G0, IN_W), start=k == 0, stop=k == KD - 1)
                ins.then_inc(sem("mg_mm"), 1)
                if t < 2:
                    conv_tp(CT_N - 2 + t)
            pe.wait_ge(sem("mean_squares"), T + 1)
            for t in range(T):
                if t == T - 1:
                    pe.wait_ge(sem("g_ready"), 1)
                    pe.wait_ge(sem("tok"), CT_N)
                    for d in range(2):
                        mm(PS[:, 3 * d, 0:16], cmat["tri_" + dirs[d]], gg[:, 16 * d:16 * d + 16], start=True, stop=True) \
                            .then_inc(sem("gc_mm"), 1)
                if t >= 2:
                    pe.wait_ge(sem("z"), t - 1)
                for k in range(KD):
                    ins = mm(PS[:, 6 + t % 2, :], n1T[:, k, tok(t)], w_in_at(k, Z0, G0), start=k == 0, stop=k == KD - 1)
                ins.then_inc(sem("z_mm"), 1)
            pe.wait_ge(sem("qk_unit"), T)
            pe.wait_ge(sem("tok"), CT_N)
            pe.wait_ge(sem("mg_ready"), T)
            pe.wait_ge(sem("g_cum"), 2)
            for c in range(8):
                h, w = divmod(c, 2)
                if c == 6:
                    pe.wait_ge(sem("z"), T)
                for t in range(T):
                    ins = tp(PS[:, c, tok(t)], TOK[:, t, h + (NH if w == 0 else 0), :])
                ins.then_inc(sem("kqt_mm"), 1)
            pe.wait_ge(sem("latents"), 2 * T)
            pe.wait_ge(sem("kqt"), 2 * NH)
            for k in range(3):
                for t in range(T):
                    ins = tp(PS[:, k, tok(t)], CQ[:, t, k * P:(k + 1) * P])
                ins.then_inc(sem("latents_tp"), 1)
            pe.wait_ge(sem("latents_t"), 3)
            pe.wait_ge(sem("w_up_in"), 32)
            for h in range(NH):
                if h >= 2:
                    pe.wait_ge(sem("nope"), 2 * (h - 1))
                for k in range(2):
                    ins = mm(PS[:, 4 + h % 2, :], WQU[:, k, h * 192:h * 192 + P], CQT[:, k, :], start=k == 0, stop=k == 1)
                ins.then_inc(sem("nope_mm"), 1)
                mm(PS[:, 6 + h % 2, :], WKU[:, h * 256:h * 256 + P], CKVT, start=True, stop=True) \
                    .then_inc(sem("nope_mm"), 1)
            for t in range(T):
                if t >= 2:
                    pe.wait_ge(sem("qp_ready"), 2 * (t - 1))
                for k in range(2):
                    w = WQU[:, k, :].rearrange("p (h n) -> p h n", h=NH)[:, :, NOPE:]
                    ins = mm(PS[:, t % 2, 0:256], CQT[:, k, tok(t)], w, start=k == 0, stop=k == 1)
                ins.then_inc(sem("qp_mm"), 1)
                w = WKU.rearrange("p (h n) -> p h n", h=NH)[:, :, NOPE:]
                mm(PS[:, 2 + t % 2, :], CKVT[:, tok(t)], w, start=True, stop=True).then_inc(sem("qp_mm"), 1)
            pe.wait_ge(sem("qp_ready"), 2 * T)
            pe.wait_ge(sem("k_rotated"), 7)
            for t in range(T):
                ins = tp(PS[:, 0, tok(t)], KPR[:, t, :])
            ins.then_inc(sem("pe_tp"), 1)
            pe.wait_ge(sem("q_rotated"), 6 * T)
            for pr in range(2):
                for t in range(T):
                    ins = tp(PS[:, 1 + pr, tok(t)], QPR[:, t, pr * P:(pr + 1) * P])
                ins.then_inc(sem("pe_tp"), 1)
            pe.wait_ge(sem("pe_t"), 3)
            pe.wait_ge(sem("nope"), 2 * NH)

            def attend(q):
                if q >= T + 2 and (q - 2) % T == 0:
                    h = (q - 2) // T - 1
                    pe.wait_ge(sem("pt"), T * (h + 1))
                    for kt in range(T):
                        ins = mm(PS[:, 7, :], VT[:, kt, h * P:(h + 1) * P], PTs[h % 2][:, kt, :],
                                 start=kt == 0, stop=kt == T - 1)
                    ins.then_inc(sem("pv_mm"), 1)
                if q < UNITS:
                    h, qt = divmod(q, T)
                    if q:
                        pe.wait_ge(sem("p_exp"), q)
                    mm(PS[:, 6, :], QNT[:, h, tok(qt)], KNT[:, h, :], start=True, stop=False)
                    r = slice(64 * (h % 2), 64 * (h % 2) + 64)
                    mm(PS[:, 6, :], QPET[r, h // 2, tok(qt)], KPET[r, :], start=False, stop=True) \
                        .then_inc(sem("s_mm"), 1)
                n = q - 2
                if 0 <= n < UNITS:
                    pe.wait_ge(sem("p_norm"), n + 1)
                    if n:
                        pe.wait_ge(sem("pt"), n)
                    if n >= T and n % T == 0:
                        pe.wait_ge(sem("mla_out"), n // T)
                    for kt in range(T):
                        ins = tp(PS[:, 7, tok(kt)], PR[n % 2][:, tok(kt)])
                    ins.then_inc(sem("p_tp"), 1)

            pe.wait_ge(sem("ones"), 1)
            pe.wait_ge(sem("pe_t"), 3)
            hs = lambda h: slice(h * P, (h + 1) * P)
            for s in range(T):
                for d in range(2):
                    D_, t, b = dirs[d], chunk_of(d, s), 3 * d
                    pe.wait_ge(sem("g_tri" + D_), s + 1)
                    if s:
                        pe.wait_ge(sem("state" + D_), s)
                    mm(PS[:, b, :], ONES, DIFF[d], start=True, stop=True).then_inc(sem("g_rows" + D_), 1)
                    if s:
                        pe.wait_ge(sem("vn" + D_), s)
                    for h in range(NH):
                        o = PS[:, b + 1 + h // 2, 256 * (h % 2):256 * (h % 2) + 256]
                        ins = mm(o.rearrange("p (w n) -> p w n", w=2), KQT[:, h, 0, tok(t)], KQT[:, h, :, tok(t)],
                                 start=True, stop=True)
                    ins.then_inc(sem("kq_mm" + D_), 1)
                attend(SLOTS * s)
                for d in range(2):
                    D_, b = dirs[d], 3 * d
                    pe.wait_ge(sem("level" + D_), LEVELS * s + 1)
                    for h in range(NH):
                        ins = tp(PS[:, b, hs(h)], LO[d][:, hs(h)])
                    ins.then_inc(sem("lo_tp" + D_), 1)
                for l in range(1, LEVELS):
                    if l == 1:
                        attend(SLOTS * s + 1)
                    for d in range(2):
                        D_, b = dirs[d], 3 * d
                        pe.wait_ge(sem("level" + D_), LEVELS * s + l + 1)
                        if l == 1:
                            pe.wait_ge(sem("x_init" + D_), 2 * s + 2)
                            pe.wait_ge(sem("attn" + D_), s + 1)
                        else:
                            pe.wait_ge(sem("x_up" + D_), 6 * s + l - 1)
                        for h in range(NH):
                            ins = mm(PS[:, b + 1, hs(h)], LO[d][:, hs(h)], XM[d][:, hs(h)], start=True, stop=True)
                        ins.then_inc(sem("n_mm" + D_), 1)
                    if 1 < l < SLOTS:
                        attend(SLOTS * s + l)
                    for d in range(2):
                        D_, b = dirs[d], 3 * d
                        pe.wait_ge(sem("n" + D_), 6 * s + l)
                        for h in range(NH):
                            ins = mm(blocks(PS[:, b + 2, hs(h)], l, 1 - d), TM[d][:, hs(h)],
                                     blocks(DIFF[d][:, hs(h)], l, 1 - d), start=True, stop=True)
                        if l < LEVELS - 1:
                            for h in range(NH):
                                ins = mm(blocks(PS[:, b, hs(h)], l, d), DIFF[d][:, hs(h)],
                                         blocks(TM[d][:, hs(h)], l, d), start=True, stop=True)
                        ins.then_inc(sem("d_mm" + D_), 1)
                for d in range(2):
                    D_, b = dirs[d], 3 * d
                    pe.wait_ge(sem("scaled" + D_), 4 * s + 4)
                    pe.wait_ge(sem("x_up" + D_), 6 * s + 6)
                    if s:
                        for h in range(NH):
                            ins = mm(PS[:, b + 1, hs(h)], KBG[d][:, hs(h)], XM[d][:, hs(h)], start=True, stop=True)
                        ins.then_inc(sem("w_mm" + D_), 1)
                for d in range(2):
                    D_, b = dirs[d], 3 * d
                    if s:
                        pe.wait_ge(sem("w" + D_), s)
                    for h in range(NH):
                        ins = mm(PS[:, b + 2, hs(h)], XM[d][:, hs(h)], VB[d][:, hs(h)], start=True, stop=s == 0)
                        if s:
                            ins = mm(PS[:, b + 2, hs(h)], TM[d][:, hs(h)], ST[d][:, hs(h)], start=False, stop=True)
                    ins.then_inc(sem("vn_mm" + D_), 1)
                for d in range(2):
                    D_, b = dirs[d], 3 * d
                    pe.wait_ge(sem("vn" + D_), s + 1)
                    if s < T - 1:
                        for h in range(NH):
                            mm(PS[:, b, hs(h)], KDC[d][:, hs(h)], KBG[d][:, hs(h)], start=True, stop=True)
                    for h in range(NH):
                        if s:
                            mm(PS[:, b + 1, hs(h)], EG[d][:, hs(h)], ST[d][:, hs(h)], start=True, stop=False)
                        ins = mm(PS[:, b + 1, hs(h)], A[d][:, 512 + h * P:512 + (h + 1) * P], KBG[d][:, hs(h)],
                                 start=s == 0, stop=True)
                    ins.then_inc(sem("o_mm" + D_), 1)

        WO = R1A[:, 0:8192].rearrange("p (k n) -> p k n", k=KD)
        WQ = [R1A[:, a:a + 8192].rearrange("p (k n) -> p k n", k=KD) for a in (8192, 0)]
        SKT = CONST[:, P:P + 2 * PH * NK].rearrange("p (c n) -> p c n", n=NK)
        iota = CONST[:, NCONST + HR:]
        UR = [R2[:, D * j:D * (j + 1)] for j in range(UN)]
        VR = [R2[:, D * (UN + j):D * (UN + j + 1)] for j in range(VN)]
        LN2B, FINB, YS = (R2[:, 12288 + D * j:12288 + D * (j + 1)] for j in range(3))
        DG = [R2[:, 15360 + P * j:15360 + P * (j + 1)] for j in range(DN)]
        rat = [0]

        def rw(n):
            rat[0] += n
            assert rat[0] <= 8192, rat
            return R1B[:, rat[0] - n:rat[0]]

        QPT = rw(512).rearrange("p (c n) -> p c n", n=P)
        N2 = [rw(D)] + [MIXT[:, 2 * t:2 * t + 2, :].rearrange("p k s -> p (k s)") for t in range(1, T)]
        N2T = rw(1024).rearrange("p (k n) -> p k n", n=P)
        SCORES = [rw(2048) for _ in range(2)]
        SC, SC2, CAND, CAND2 = (rw(256) for _ in range(4))
        OH = CONST[:, P + 2 * PH * NK:P + 2 * PH * NK + 2 * TOPK * TOPK]
        TOPS, TOPI, TOPIF = rw(32), rw(32).bitcast(U32), rw(32)
        BEST, BESTI, BESTIJ, BESTF, ROWS = rw(16), rw(16).bitcast(U32), rw(32).bitcast(U32), rw(32), rw(32)
        EXPERT, GATE = [rw(TOPK).bitcast(I32) for _ in range(2)], [rw(TOPK) for _ in range(2)]
        UIDX, VIDX = ([rw(TOPK).bitcast(I32) for _ in range(2)] for _ in range(2))
        HID, GEL, WGT = ([rw(TOPK) for _ in range(2)] for _ in range(3))
        n2sq, n2r, gsum = ssq, rstd, [rw(1) for _ in range(2)]
        ysq = [rw(1) for _ in range(2)]

        def steps(eng, body):
            for h in range(PH):
                body(0, h, h % 2)
            for t in range(1, T):
                body(t, 0, 0)
                with eng.Fori(0, 3, 1) as i:
                    body(t, 2 * i + 1, 1)
                    body(t, 2 * i + 2, 0)
                body(t, PH - 1, 1)
            body(T, 0, 0)

        def front(t, h):
            if not isinstance(h, int) or t == T:
                return {}
            if t == 0 and 1 <= h <= 3:
                return {1: {3: (0, 3)}, 2: {3: (0, 4)}, 3: {0: (0, 5), 1: (0, 6), 2: (0, 7)}}[h]
            if t < T - 1 and h in (4 if t == 0 else 0, PH - 1):
                return {i: (t + 1, i + (NH if h == PH - 1 else 0)) for i in range(NH)}
            return {}

        @block.sync
        def _(sp):
            wq = peer_wq[0].rearrange("(k p) n -> p k n", p=P)
            sp.wait_ge(sem("mla_out"), NH)
            for k in range(0, KD, 4):
                sp.dma_start(WO[:, k:k + 4, :], w_out[0].rearrange("(k p) n -> p k n", p=P)[:, k:k + 4, :]) \
                    .then_inc(sem("wo_in"), 16)
            sp.dma_start(WQ[0], wq[:, :, 0:D]).then_inc(sem("wq_in"), 16)
            sp.wait_ge(sem("mean_squares"), T + 3)
            sp.dma_start(LN2B, ln2_w[0].partition_broadcast(P)).then_inc(sem("norms_in"), 16)
            sp.dma_start(FINB, final_norm_w.partition_broadcast(P)).then_inc(sem("norms_in"), 16)
            sp.dma_start(SKT, sub_keys).then_inc(sem("keys_in"), 16)
            sp.wait_ge(sem("out_mm"), T)
            sp.dma_start(WQ[1], wq[:, :, D:]).then_inc(sem("wq_in"), 16)
            for t in range(T):
                sp.wait_ge(sem("y_dve"), 3 * (t + 1))
                sp.dma_start(out[0, tok(t), :], YS).then_inc(sem("y_out"), 16)
            sp.wait_ge(sem("y_out"), 16 * T)

        @block.gpsimd
        def _(pool):
            def hold(name, value):
                pool.wait_ge(sem(name), value)
                pool.sem_inc(sem("gather_may_go"), 1)

            def body(t, h, par):
                first, last = (t == 0 and opens(h)), t == T
                gu = PH * t + h
                gv = gu - 1
                if not last:
                    hold("experts", gu + 1)
                    if not first:
                        hold("u_dot", TOPK * gu - 8)
                    nc.gpsimd.tensor_copy(UIDX[par], EXPERT[par]).then_inc(sem("u_idx"), 1)
                if not first:
                    nc.gpsimd.tensor_copy(VIDX[1 - par], UIDX[1 - par]).then_inc(sem("v_idx"), 1)
                    hold("v_idx", gv + 1)
                if not last:
                    hold("u_idx", gu + 1)
                for s in range(TOPK):
                    if not last:
                        if not first or s >= UN:
                            hold("u_dot", TOPK * gu + s + 1 - UN)
                        pool.indirect_dma_start(UR[s % UN], None, peer_u[0],
                                                bass.IndirectOffsetOnAxis(ap=UIDX[par][:, s:s + 1], axis=0)) \
                            .then_inc(sem(f"u_row{s % UN}"), 16)
                    if not first:
                        if not isinstance(gv, int) or TOPK * gv + s + 1 > VN:
                            hold("v_sum", TOPK * gv + s + 1 - VN)
                        pool.indirect_dma_start(VR[s % VN], None, peer_v[0],
                                                bass.IndirectOffsetOnAxis(ap=VIDX[1 - par][:, s:s + 1], axis=0)) \
                            .then_inc(sem(f"v_row{s % VN}"), 16)

            pool.wait_ge(sem("o_tp"), T)
            pool.wait_ge(sem("gdn_out"), T)
            steps(pool, body)

        @block.scalar
        def _(act):
            def act_(out, in_, f, name, **kw):
                return nc.scalar.activation(out, in_, f, **kw).then_inc(sem(name), 1)

            for t in range(T):
                act.wait_ge(sem("mean_squares"), T + 3 + t)
                act_(orr[:, NH * t:NH * (t + 1)], osq[:, NH * t:NH * (t + 1)], ACT.Sqrt, "roots")

            def rms(t):
                act.wait_ge(sem("h_sum"), t + 1)
                if t:
                    act.wait_ge(sem("n2_squares"), t)
                act_(YS, H[:, t, :], ACT.Square, "n2_squares", accum_out=n2sq[:, t:t + 1])

            def root(t):
                act.wait_ge(sem("mean_squares"), 2 * T + 3 + t)
                act_(n2r[:, t:t + 1], n2sq[:, t:t + 1], ACT.Sqrt, "roots")

            def queries(t, j):
                n = PH * t + j
                act.wait_ge(sem("q_mm"), n + 1)
                if n >= 2:
                    act.wait_ge(sem("score_mm"), n - 1)
                act_(QPT[:, 2 * (j % 2):2 * (j % 2) + 2, :].rearrange("p c n -> p (c n)"), PS[:, 6 + j % 2, 0:2 * P],
                     ACT.Copy, "q")

            def scores(t, j):
                act.wait_ge(sem("score_mm"), PH * t + j + 1)
                if t >= 2:
                    act.wait_ge(sem("experts"), PH * (t - 1))
                act_(SCORES[t % 2][:, 2 * P * j:2 * P * (j + 1)], PS[:, 4 + j % 2, 0:2 * P], ACT.Copy, "scores")

            def normed(t):
                act.wait_ge(sem("n2t_mm"), t + 1)
                act_(N2T.rearrange("p k n -> p (k n)"), PS[:, 4:6, :].rearrange("p b n -> p (b n)"), ACT.Copy, "n2t")

            def front_after(heads, s):
                for i, (t, j) in heads.items():
                    if s == 0 and j == 0:
                        normed(t)
                    if s == 3 * i + 4:
                        queries(t, j)
                    if s == min(3 * i + 8, TOPK - 1):
                        scores(t, j)

            def body(t, h, par):
                first, last = (t == 0 and opens(h)), t == T
                gu = PH * t + h
                gv = gu - 1
                heads = front(t, h)
                if first:
                    rms(1)
                    queries(0, 2)
                    scores(0, 2)
                if not first:
                    act.wait_ge(sem("u_dot"), TOPK * (gv + 1))
                    act_(GEL[1 - par], HID[1 - par], ACT.Gelu, "gelu")
                    act.wait_ge(sem("weight"), gv + 1)
                for s in range(TOPK):
                    if not first:
                        if not isinstance(gv, int) or TOPK * gv + s + 1 > DN:
                            act.wait_ge(sem("v_sum"), TOPK * gv + s + 1 - DN)
                        act_(DG[s % DN], ident, ACT.Copy, "diag", scale=WGT[1 - par][:, s:s + 1])
                    if t == 0 and s == 10 and h in (1, 2):
                        rms(h + 1)
                    if t == 0 and s == 12 and h == 2:
                        for t2 in range(1, T):
                            root(t2)
                    front_after(heads, s)
                if not (t == T or (t == T - 1 and isinstance(h, int) and h == PH - 1)):
                    act.wait_ge(sem("gate_arg"), gu + 2)
                    act_(GATE[1 - par], GATE[1 - par], ACT.Exp, "gate_exps", accum_out=gsum[1 - par])
                if opens(h) and t:
                    b = 2 * ((t - 1) % 2)
                    act.wait_ge(sem("v_sum"), TOPK * PH * t)
                    if t >= 2:
                        act.wait_ge(sem("y_out"), 16 * (t - 1))
                    act_(YS, PS[:, b:b + 2, :].rearrange("p b n -> p (b n)"), ACT.Square, "y_act", accum_out=ysq[0])
                    act.wait_ge(sem("y_dve"), 3 * t - 2)
                    act_(ysq[1], ysq[0], ACT.Sqrt, "y_act")

            rms(0)
            root(0)
            normed(0)
            for j in range(2):
                queries(0, j)
                scores(0, j)
            act.wait_ge(sem("gate_arg"), 1)
            act_(GATE[0], GATE[0], ACT.Exp, "gate_exps", accum_out=gsum[0])
            steps(act, body)

        @block.vector
        def _(dve):
            v = nc.vector
            links = [0]

            def link(ins):
                links[0] += 1
                ins.then_inc(sem("norm_chain"), 1)
                dve.wait_ge(sem("norm_chain"), links[0])

            SQO = h4(DIFF[0])
            dve.wait_ge(sem("o_out"), 2 * T)
            for t in range(T):
                hq = slice(NH * t, NH * (t + 1))
                link(v.tensor_tensor(SQO, O[:, t, :, :], O[:, t, :, :], ALU.mult))
                link(v.tensor_reduce(osq[:, hq], SQO, AX, ALU.add))
                v.tensor_scalar(osq[:, hq], osq[:, hq], 1.0 / P, EPS, ALU.mult, ALU.add) \
                    .then_inc(sem("mean_squares"), 1)
                dve.wait_ge(sem("roots"), T + 3 + t)
                link(v.reciprocal(orr[:, hq], orr[:, hq]))
                link(v.tensor_tensor(O[:, t, :, :], O[:, t, :, :], over_cols(orr[:, hq], P), ALU.mult))
                v.tensor_tensor(O[:, t, :, :], O[:, t, :, :], h4(Z[:, t, :]), ALU.mult).then_inc(sem("o_gated"), 1)
                dve.wait_ge(sem("o_tp"), t + 1)
                v.tensor_scalar(MIXT[:, NH:2 * NH, tok(t)], h4(PS[:, 6 + t % 2, :]), gdn_col, None, ALU.mult) \
                    .then_inc(sem("gdn_out"), 1)

            def residual(t):
                dve.wait_ge(sem("out_mm"), t + 1)
                b = 2 * (t % 2)
                v.tensor_tensor(H[:, t, :], H[:, t, :], PS[:, b:b + 2, :].rearrange("p b n -> p (b n)"), ALU.add) \
                    .then_inc(sem("h_sum"), 1)

            def rms(t):
                c = n2sq[:, t:t + 1]
                dve.wait_ge(sem("n2_squares"), t + 1)
                v.tensor_scalar(c, c, 1.0 / D, EPS, ALU.mult, ALU.add).then_inc(sem("mean_squares"), 1)
                dve.wait_ge(sem("roots"), 2 * T + 3 + t)
                v.reciprocal(n2r[:, t:t + 1], n2r[:, t:t + 1])
                v.drain()

            def normed(t):
                v.scalar_tensor_tensor(out=N2[t], in0=H[:, t, :], scalar=n2r[:, t:t + 1], in1=LN2B,
                                       op0=ALU.mult, op1=ALU.mult).then_inc(sem("n2"), 1)

            residual(0)
            rms(0)
            dve.wait_ge(sem("norms_in"), 32)
            normed(0)

            def top_experts(t, h, par):
                v.tensor_copy(SC, SCORES[t % 2][:, bass.ds(256 * h, 256)])
                v.drain()
                half = lambda ap, w: ap[:, NK * w:NK * (w + 1)]
                s8 = lambda ap, w, r: ap[:, TOPK * w + 8 * r:TOPK * w + 8 * r + 8]
                for w in range(2):
                    v.max(s8(TOPS, w, 0), half(SC, w))
                v.drain()
                for w in range(2):
                    v.match_replace(half(SC2, w), s8(TOPS, w, 0), half(SC, w), LOWEST)
                for w in range(2):
                    v.max_index(s8(TOPI, w, 0), s8(TOPS, w, 0), half(SC, w))
                v.drain()
                for w in range(2):
                    v.max(s8(TOPS, w, 1), half(SC2, w))
                v.drain()
                for w in range(2):
                    v.max_index(s8(TOPI, w, 1), s8(TOPS, w, 1), half(SC2, w))
                c3 = lambda ap: ap.rearrange("p (i j) -> p i j", i=TOPK)
                v.tensor_tensor(c3(CAND), over_cols(TOPS[:, 0:TOPK], TOPK), over_rows(TOPS[:, TOPK:2 * TOPK], TOPK), ALU.add)
                v.drain()
                v.tensor_copy(TOPIF, TOPI)
                v.max(BEST[:, 0:8], CAND)
                v.drain()
                v.match_replace(CAND2, BEST[:, 0:8], CAND, LOWEST)
                v.max_index(BESTI[:, 0:8], BEST[:, 0:8], CAND)
                v.drain()
                v.max(BEST[:, 8:16], CAND2)
                v.drain()
                v.max_index(BESTI[:, 8:16], BEST[:, 8:16], CAND2)
                v.tensor_scalar(GATE[par], BEST, BEST[:, 0:1], None, ALU.subtract).then_inc(sem("gate_arg"), 1)
                v.drain()
                v.tensor_scalar(BESTIJ[:, 0:TOPK], BESTI, 4, None, ALU.logical_shift_right)
                v.tensor_scalar(BESTIJ[:, TOPK:], BESTI, TOPK - 1, None, ALU.bitwise_and)
                v.drain()
                v.tensor_copy(BESTF, BESTIJ)
                v.drain()
                o3 = OH.rearrange("p (k j) -> p k j", j=TOPK)
                v.tensor_tensor(o3, over_cols(BESTF, TOPK), over_rows(iota, 2 * TOPK), ALU.is_equal)
                v.drain()
                o4 = OH.rearrange("p (w k j) -> p w k j", w=2, j=TOPK)
                keys = TOPIF.rearrange("p (w j) -> p w j", w=2).unsqueeze(2).broadcast_to([P, 2, TOPK, TOPK])
                v.tensor_tensor(o4, o4, keys, ALU.mult)
                v.drain()
                v.tensor_reduce(ROWS, o3, AX, ALU.add)
                v.drain()
                if not (isinstance(h, int) and PH * t + h < 2):
                    dve.wait_ge(sem("u_idx"), PH * t + h - 1)
                v.scalar_tensor_tensor(out=EXPERT[par], in0=ROWS[:, 0:TOPK],
                                       scalar=float(NK), in1=ROWS[:, TOPK:], op0=ALU.mult, op1=ALU.add) \
                    .then_inc(sem("experts"), 1)

            def body(t, h, par):
                first, last = (t == 0 and opens(h)), t == T
                gu = PH * t + h
                gv = gu - 1

                def weights():
                    dve.wait_ge(sem("gate_exps"), gv + 1)
                    v.reciprocal(gsum[1 - par], gsum[1 - par])
                    v.drain()
                    dve.wait_ge(sem("gelu"), gv + 1)
                    v.scalar_tensor_tensor(out=WGT[1 - par], in0=GEL[1 - par], scalar=gsum[1 - par], in1=GATE[1 - par],
                                           op0=ALU.mult, op1=ALU.mult).then_inc(sem("weight"), 1)

                if last:
                    weights()
                else:
                    for s in range(TOPK):
                        if s == 2 and not first:
                            weights()
                        if t == 0:
                            if (h, s) in ((0, 8), (0, 12), (2, 3)):
                                residual({(0, 8): 1, (0, 12): 2, (2, 3): 3}[h, s])
                            if (h, s) == (2, 12):
                                for t2 in range(1, T):
                                    rms(t2)
                                    normed(t2)
                        if s == 4:
                            if isinstance(h, int) and h == PH - 1:
                                if t < T - 1:
                                    dve.wait_ge(sem("scores"), PH * (t + 1) + 1)
                                    top_experts(t + 1, 0, 1 - par)
                            else:
                                dve.wait_ge(sem("scores"), h + 2 if t == 0 else PH * (t + 1))
                                top_experts(t, h + 1, 1 - par)
                        dve.wait_ge(sem(f"u_row{s % UN}"), 16 * ((TOPK // UN) * gu + s // UN + 1))
                        v.tensor_tensor_reduce(out=UR[s % UN], in0=UR[s % UN], in1=N2[t], scale=1.0, scalar=0.0,
                                               op0=ALU.mult, op1=ALU.add, accum_out=HID[par][:, s:s + 1]) \
                            .then_inc(sem("u_dot"), 1)
                if opens(h) and t:
                    b = 2 * ((t - 1) % 2)
                    dve.wait_ge(sem("y_act"), 2 * t - 1)
                    v.tensor_scalar(ysq[0], ysq[0], 1.0 / D, EPS, ALU.mult, ALU.add).then_inc(sem("y_dve"), 1)
                    dve.wait_ge(sem("y_act"), 2 * t)
                    v.reciprocal(ysq[1], ysq[1]).then_inc(sem("y_dve"), 1)
                    dve.wait_ge(sem("y_dve"), 3 * t - 1)
                    v.scalar_tensor_tensor(out=YS, in0=PS[:, b:b + 2, :].rearrange("p b n -> p (b n)"), scalar=ysq[1],
                                           in1=FINB, op0=ALU.mult, op1=ALU.mult).then_inc(sem("y_dve"), 1)

            dve.wait_ge(sem("keys_in"), 16)
            dve.wait_ge(sem("scores"), 1)
            top_experts(0, 0, 0)
            steps(dve, body)

        @block.tensor
        def _(pe):
            mm = nc.tensor.matmul
            cols = lambda c: slice(c * P, (c + 1) * P)

            def gdn_tp(t):
                pe.wait_ge(sem("o_gated"), t + 1)
                if t >= 2:
                    pe.wait_ge(sem("gdn_out"), t - 1)
                for h in range(NH):
                    ins = nc.tensor.transpose(PS[:, 6 + t % 2, cols(h)], O[:, t, h, :], ident)
                ins.then_inc(sem("o_tp"), 1)

            def project(t, first, last):
                if first == 0:
                    pe.wait_ge(sem("gdn_out"), t + 1)
                    if t >= 2:
                        pe.wait_ge(sem("h_sum"), t - 1)
                for n in range(first, last):
                    half, k = divmod(n, KD)
                    ins = mm(PS[:, 2 * (t % 2) + half, :], MIXT[:, k, tok(t)], WO[:, k, 512 * half:512 * half + 512],
                             start=k == 0, stop=k == KD - 1)
                if last == 2 * KD:
                    ins.then_inc(sem("out_mm"), 1)

            def normed(t):
                pe.wait_ge(sem("n2"), t + 1)
                if t:
                    pe.wait_ge(sem("scores"), PH * t)
                for k in range(KD):
                    ins = nc.tensor.transpose(PS[:, 4 + k // 4, cols(k % 4)], N2[t][:, k * P:(k + 1) * P], ident)
                ins.then_inc(sem("n2t_mm"), 1)

            def query(t, j, w):
                n = PH * t + j
                if w == 0:
                    if j == 0:
                        pe.wait_ge(sem("n2t"), t + 1)
                    if n == NH:
                        pe.wait_ge(sem("wq_in"), 32)
                    if n >= 2:
                        pe.wait_ge(sem("q"), n - 1)
                for k in range(KD):
                    ins = mm(PS[:, 6 + j % 2, cols(w)], WQ[j // NH][:, k, cols(2 * (j % NH) + w)], N2T[:, k, :],
                             start=k == 0, stop=k == KD - 1)
                if w:
                    ins.then_inc(sem("q_mm"), 1)

            def score(t, j):
                n = PH * t + j
                pe.wait_ge(sem("q"), n + 1)
                if n >= 2:
                    pe.wait_ge(sem("scores"), n - 1)
                for w in range(2):
                    ins = mm(PS[:, 4 + j % 2, cols(w)], QPT[:, 2 * (j % 2) + w, :], SKT[:, 2 * j + w, :],
                             start=True, stop=True)
                ins.then_inc(sem("score_mm"), 1)

            def front_after(heads, s):
                for i, (t, j) in heads.items():
                    if s == 0 and j == 0:
                        normed(t)
                    if s in (3 * i, 3 * i + 1):
                        query(t, j, s - 3 * i)
                    if s == 3 * i + 6:
                        score(t, j)

            def body(t, h, par):
                first, last = (t == 0 and opens(h)), t == T
                gu = PH * t + h
                gv = gu - 1
                tv = t - 1 if opens(h) else t
                heads = front(t, h)
                for s in range(TOPK):
                    if not first:
                        pe.wait_ge(sem("diag"), TOPK * gv + s + 1)
                        pe.wait_ge(sem(f"v_row{s % VN}"), 16 * ((TOPK // VN) * gv + s // VN + 1))
                        for c in range(2):
                            ins = mm(PS[:, 2 * (tv % 2) + c, :], DG[s % DN], VR[s % VN][:, 512 * c:512 * c + 512],
                                     start=False, stop=tv != t and s == TOPK - 1)
                        ins.then_inc(sem("v_sum"), 1)
                    if t == 0 and h == 1:
                        project(3, s, s + 1)
                    front_after(heads, s)
                if first:
                    project(1, KD, 2 * KD)
                    project(2, 0, 2 * KD)
                    for w in range(2):
                        query(0, 2, w)
                    score(0, 2)
                    pe.wait_ge(sem("h_sum"), 3)
                if opens(h) and not last:
                    if t >= 2:
                        pe.wait_ge(sem("y_dve"), 3 * (t - 1))
                    for c in range(2):
                        mm(PS[:, 2 * (t % 2) + c, :], ident, H[:, t, 512 * c:512 * c + 512], start=True, stop=False)

            pe.wait_ge(sem("o_out"), 2 * T)
            gdn_tp(0)
            pe.wait_ge(sem("wo_in"), 32)
            project(0, 0, 8)
            gdn_tp(1)
            project(0, 8, 12)
            gdn_tp(2)
            project(0, 12, 16)
            gdn_tp(3)
            project(1, 0, 6)
            pe.wait_ge(sem("keys_in"), 16)
            normed(0)
            project(1, 6, 8)
            pe.wait_ge(sem("wq_in"), 16)
            pe.wait_ge(sem("gdn_out"), T)
            for j in range(2):
                for w in range(2):
                    query(0, j, w)
                score(0, j)
            steps(pe, body)


def kernel(**inputs):
    import concourse.bacc as bacc
    from concourse.bass_utils import run_bass_kernel_spmd as run
    nc = bacc.Bacc("TRN2", target_bir_lowering=False, num_devices=1)
    laid_out = {name: inputs.get(name) for name in NAMES}
    laid_out["positions"] = inputs["positions"].reshape(T, P).T
    laid_out["sub_keys"] = np.transpose(inputs["peer_sub_keys"][0].reshape(2 * PH, NK, P), (2, 0, 1))
    columns = [inputs[n].reshape(-1, P) for n in ("conv_w", "ln1_w", "q_a_norm_w", "kv_a_norm_w", "gdn_norm_w")]
    laid_out["columns"] = np.concatenate(columns).T
    laid_out["consts"] = shape_constants()
    arrays, args = {}, []
    for name, a in laid_out.items():
        arrays["in_" + name] = a = np.ascontiguousarray(a)
        args.append(nc.dram_tensor("in_" + name, a.shape, mybir.dt.from_np(a.dtype), kind="ExternalInput").ap())
    args.append(nc.dram_tensor("out", OUT_SHAPE, F32, kind="ExternalOutput").ap())
    encoder_block(nc, *args)
    return run(nc, [arrays], core_ids=[0]).results[0]["out"]


NAMES = ["x", "positions", "w_in", "w_q_up", "w_kv_up", "a_log_f", "dt_bias_f", "a_log_b", "dt_bias_b", "w_out",
         "ln2_w", "peer_wq", "sub_keys", "peer_u", "peer_v", "final_norm_w"]
OUT_SHAPE = (1, S, D)
```
